# Optimizing a Trainium2 kernel written in Bass

```python
import math
import jax
import jax.numpy as jnp
from jax import lax
import numpy as np
import jax, jax.numpy as jnp

D_MODEL = 1024
BATCH = 1
SEQ = 256
DEPTH = 1

D_MIX = D_MODEL
GDN_HEADS = 4
GDN_HEAD_DIM = 128
GDN_WIDTH = GDN_HEADS * GDN_HEAD_DIM
CONV_WIDTH = 5
CHUNK = 64
SWA_HEADS = 8
SWA_HEAD_DIM = 64
SWA_WIDTH = SWA_HEADS * SWA_HEAD_DIM
DILATION_PATTERNS = ((128, 1), (512, 4), (2048, 16))
BAND_BLOCK = 64
REL_BUCKETS = 32
REL_MAX_DISTANCE = 1024
D_FF = 2816
EPS = 1e-6
NEG_BIG = -1e30
SPLITS = (3 * GDN_WIDTH, GDN_WIDTH, 2 * GDN_HEADS, 2 * GDN_HEADS, 3 * SWA_WIDTH)
N_IN = sum(SPLITS)


def rms_norm(x, w):
    xf = x.astype(jnp.float32)
    y = xf * lax.rsqrt(jnp.mean(xf * xf, axis=-1, keepdims=True) + EPS)
    return (y * w.astype(jnp.float32)).astype(x.dtype)

def l2_normalize(x):
    return x * lax.rsqrt(jnp.sum(x * x, axis=-1, keepdims=True) + EPS)

def swiglu(x, w_gate, w_up, w_down):
    return (jax.nn.silu(x @ w_gate) * (x @ w_up)) @ w_down

def t5_bucket(rel):
    nb = REL_BUCKETS // 2
    bucket = (rel > 0).astype(np.int32) * nb
    n = np.abs(rel)
    max_exact = nb // 2
    large = max_exact + (np.log(np.maximum(n, 1) / max_exact)
                         / math.log(REL_MAX_DISTANCE / max_exact) * (nb - max_exact)).astype(np.int32)
    large = np.minimum(large, nb - 1)
    return (bucket + np.where(n < max_exact, n, large)).astype(np.int32)

def short_conv(x, w):
    c, kw = w.shape
    rhs = jnp.transpose(w).astype(x.dtype)[:, None, :]
    return lax.conv_general_dilated(x, rhs, window_strides=(1,),
                                    padding=((kw // 2, kw // 2),),
                                    dimension_numbers=('NWC', 'WIO', 'NWC'),
                                    feature_group_count=c)

def gated_delta_chunked(q, k, v, g, beta):
    b, h, t, dk = q.shape
    dv = v.shape[-1]
    nc = t // CHUNK
    q = q * (dk ** -0.5)

    def chunks(a):
        return a.reshape(b, h, nc, CHUNK, *a.shape[3:])

    q, k, v, g, beta = chunks(q), chunks(k), chunks(v), chunks(g), chunks(beta)
    g = jnp.cumsum(g, axis=-1)
    incl = jnp.tril(jnp.ones((CHUNK, CHUNK), dtype=bool))
    strict = jnp.tril(jnp.ones((CHUNK, CHUNK), dtype=bool), -1)
    diff = g[..., :, None] - g[..., None, :]
    decay = jnp.where(incl, jnp.exp(jnp.where(incl, diff, 0.0)), 0.0)
    kb = k * beta[..., None]
    lmat = jnp.where(strict, jnp.einsum('bhncd,bhnjd->bhncj', kb, k) * decay, 0.0)
    eye = jnp.eye(CHUNK, dtype=jnp.float32)
    tmat = lax.linalg.triangular_solve(eye + lmat, jnp.broadcast_to(eye, lmat.shape),
                                       left_side=True, lower=True, unit_diagonal=True)
    u = tmat @ (v * beta[..., None])
    w = tmat @ (kb * jnp.exp(g)[..., None])
    intra = jnp.einsum('bhncd,bhnjd->bhncj', q, k) * decay
    qg = q * jnp.exp(g)[..., None]
    g_last = g[..., -1]
    kdec = k * jnp.exp(g_last[..., None] - g)[..., None]

    def step(state, inp):
        u_c, w_c, qg_c, intra_c, kdec_c, gl_c = inp
        v_new = u_c - w_c @ state
        o_c = qg_c @ state + intra_c @ v_new
        state = state * jnp.exp(gl_c)[..., None, None] + jnp.swapaxes(kdec_c, -1, -2) @ v_new
        return state, o_c

    xs = tuple(jnp.moveaxis(a, 2, 0) for a in (u, w, qg, intra, kdec, g_last))
    state0 = jnp.zeros((b, h, dk, dv), jnp.float32)
    _, o = lax.scan(step, state0, xs)
    return jnp.moveaxis(o, 0, 2).reshape(b, h, t, dv)

def _reverse(a):
    return jnp.flip(a, axis=2)

def gdn_mixer(qkv, z, a, beta_logit, conv_w, a_log, dt_bias, norm_w):
    b, s, _ = qkv.shape
    f32 = jnp.float32
    qkv = jax.nn.silu(short_conv(qkv, conv_w)).astype(f32)
    qkv = qkv.reshape(b, s, 3, GDN_HEADS, GDN_HEAD_DIM).transpose(2, 0, 3, 1, 4)
    q, k, v = l2_normalize(qkv[0]), l2_normalize(qkv[1]), qkv[2]
    a = a.astype(f32).reshape(b, s, 2, GDN_HEADS)
    g = -jnp.exp(a_log.astype(f32)) * jax.nn.softplus(a + dt_bias.astype(f32))
    beta = jax.nn.sigmoid(beta_logit.astype(f32).reshape(b, s, 2, GDN_HEADS))
    g = g.transpose(2, 0, 3, 1)
    beta = beta.transpose(2, 0, 3, 1)
    o_fwd = gated_delta_chunked(q, k, v, g[0], beta[0])
    o_bwd = _reverse(gated_delta_chunked(_reverse(q), _reverse(k), _reverse(v),
                                         _reverse(g[1]), _reverse(beta[1])))
    o = (o_fwd + o_bwd).transpose(0, 2, 1, 3)
    zg = jax.nn.silu(z.astype(f32).reshape(b, s, GDN_HEADS, GDN_HEAD_DIM))
    o = rms_norm(o, norm_w) * zg
    return o.reshape(b, s, GDN_WIDTH).astype(z.dtype)

def dilated_band_attention(q, k, v, rel_bias, window, dilation):
    b, s, h, dh = q.shape
    radius = window // (2 * dilation)
    blk = BAND_BLOCK
    length = s // dilation
    nb = -(-length // blk)
    lp = nb * blk

    def to_blocks(a):
        a = a.reshape(b, length, dilation, h, dh).transpose(0, 2, 3, 1, 4)
        a = jnp.pad(a, ((0, 0), (0, 0), (0, 0), (0, lp - length), (0, 0)))
        return a.reshape(b, dilation, h, nb, blk, dh)

    def band(a):
        ap = jnp.pad(a, ((0, 0), (0, 0), (0, 0), (1, 1), (0, 0), (0, 0)))
        return jnp.concatenate([ap[:, :, :, :-2], ap[:, :, :, 1:-1], ap[:, :, :, 2:]], axis=-2)

    qb = to_blocks(q)
    kw = band(to_blocks(k))
    vw = band(to_blocks(v))
    qi = np.arange(blk)[:, None]
    ki = np.arange(3 * blk)[None, :]
    rel = ki - blk - qi
    key_t = (np.arange(nb)[:, None, None] - 1) * blk + ki[None]
    valid = (np.abs(rel)[None] <= radius) & (key_t >= 0) & (key_t < length)
    bias = jnp.transpose(rel_bias[t5_bucket(rel * dilation)], (2, 0, 1))[:, None]
    logits = jnp.einsum('bdhnqe,bdhnke->bdhnqk', qb, kw, preferred_element_type=jnp.float32)
    logits = jnp.where(valid, logits + bias.astype(jnp.float32), NEG_BIG)
    m = jnp.max(logits, axis=-1, keepdims=True)
    p = jnp.exp(logits - m)
    den = jnp.sum(p, axis=-1, keepdims=True)
    o = jnp.einsum('bdhnqk,bdhnke->bdhnqe', p, vw.astype(jnp.float32)) / den
    lse = (m + jnp.log(den))[..., 0]
    o = o.reshape(b, dilation, h, lp, dh)[:, :, :, :length].transpose(0, 3, 1, 2, 4).reshape(b, s, h, dh)
    lse = lse.reshape(b, dilation, h, lp)[..., :length].transpose(0, 3, 1, 2).reshape(b, s, h)
    return o, lse

def dilated_mixer(qkv, q_norm_w, k_norm_w, rel_bias):
    b, s, _ = qkv.shape
    qkv = qkv.reshape(b, s, 3, SWA_HEADS, SWA_HEAD_DIM)
    q = rms_norm(qkv[:, :, 0], q_norm_w) * (SWA_HEAD_DIM ** -0.5)
    k = rms_norm(qkv[:, :, 1], k_norm_w)
    v = qkv[:, :, 2]
    outs, lses = [], []
    for window, dilation in DILATION_PATTERNS:
        o_p, lse_p = dilated_band_attention(q, k, v, rel_bias, window, dilation)
        outs.append(o_p)
        lses.append(lse_p)
    wts = jax.nn.softmax(jnp.stack(lses, axis=0), axis=0)
    o = jnp.sum(wts[..., None] * jnp.stack(outs, axis=0), axis=0)
    return o.reshape(b, s, SWA_WIDTH).astype(qkv.dtype)

def first_inputs(seed: int = 0) -> dict:
    key = jax.random.key(seed)
    ks = jax.random.split(key, 24)
    f32 = jnp.float32

    def dense(k, shape, fan_in):
        return jax.random.normal(k, shape, f32) * (fan_in ** -0.5)

    def gain(k, shape):
        return 1.0 + 0.02 * jax.random.normal(k, shape, f32)

    x = jax.random.normal(ks[0], (BATCH, SEQ, D_MODEL), f32)
    ffn1_norm = gain(ks[1], (DEPTH, D_MODEL))
    ffn1_w_gate = dense(ks[2], (DEPTH, D_MODEL, D_FF), D_MODEL)
    ffn1_w_up = dense(ks[3], (DEPTH, D_MODEL, D_FF), D_MODEL)
    ffn1_w_down = dense(ks[4], (DEPTH, D_FF, D_MODEL), D_FF)
    mix_norm = gain(ks[5], (DEPTH, D_MODEL))
    w_in = dense(ks[6], (DEPTH, D_MODEL, N_IN), D_MODEL)
    conv_w = dense(ks[7], (DEPTH, 3 * GDN_WIDTH, CONV_WIDTH), CONV_WIDTH)
    a_log = jnp.log(jax.random.uniform(ks[8], (DEPTH, 2, GDN_HEADS), f32, 1.0, 16.0))
    dt = jnp.exp(jax.random.uniform(ks[9], (DEPTH, 2, GDN_HEADS), f32, math.log(1e-3), math.log(1e-1)))
    dt_bias = dt + jnp.log(-jnp.expm1(-dt))
    gdn_norm_w = gain(ks[10], (DEPTH, GDN_HEAD_DIM))
    q_norm_w = gain(ks[11], (DEPTH, SWA_HEAD_DIM))
    k_norm_w = gain(ks[12], (DEPTH, SWA_HEAD_DIM))
    rel_bias = 0.2 * jax.random.normal(ks[13], (REL_BUCKETS, SWA_HEADS), f32)
    w_out = dense(ks[14], (DEPTH, D_MIX, D_MODEL), D_MIX)
    ffn2_norm = gain(ks[15], (DEPTH, D_MODEL))
    ffn2_w_gate = dense(ks[16], (DEPTH, D_MODEL, D_FF), D_MODEL)
    ffn2_w_up = dense(ks[17], (DEPTH, D_MODEL, D_FF), D_MODEL)
    ffn2_w_down = dense(ks[18], (DEPTH, D_FF, D_MODEL), D_FF)
    final_norm = gain(ks[19], (DEPTH, D_MODEL))
    return {"x": x, "ffn1_norm": ffn1_norm, "ffn1_w_gate": ffn1_w_gate, "ffn1_w_up": ffn1_w_up,
            "ffn1_w_down": ffn1_w_down, "mix_norm": mix_norm, "w_in": w_in, "conv_w": conv_w,
            "a_log": a_log, "dt_bias": dt_bias, "gdn_norm_w": gdn_norm_w, "q_norm_w": q_norm_w,
            "k_norm_w": k_norm_w, "rel_bias": rel_bias, "w_out": w_out, "ffn2_norm": ffn2_norm,
            "ffn2_w_gate": ffn2_w_gate, "ffn2_w_up": ffn2_w_up, "ffn2_w_down": ffn2_w_down,
            "final_norm": final_norm}

def first_block(x, ffn1_norm, ffn1_w_gate, ffn1_w_up, ffn1_w_down, mix_norm, w_in, conv_w,
              a_log, dt_bias, gdn_norm_w, q_norm_w, k_norm_w, rel_bias, w_out, ffn2_norm,
              ffn2_w_gate, ffn2_w_up, ffn2_w_down, final_norm):
    split_at = np.cumsum(SPLITS)[:-1].tolist()
    for l in range(DEPTH):
        x = x + 0.5 * swiglu(rms_norm(x, ffn1_norm[l]), ffn1_w_gate[l], ffn1_w_up[l], ffn1_w_down[l])
        h = rms_norm(x, mix_norm[l])
        proj = h @ w_in[l]
        qkv_a, z_a, a_a, b_a, qkv_b = jnp.split(proj, split_at, axis=-1)
        o_a = gdn_mixer(qkv_a, z_a, a_a, b_a, conv_w[l], a_log[l], dt_bias[l], gdn_norm_w[l])
        o_b = dilated_mixer(qkv_b, q_norm_w[l], k_norm_w[l], rel_bias)
        x = x + jnp.concatenate([o_a, o_b], axis=-1) @ w_out[l]
        x = x + 0.5 * swiglu(rms_norm(x, ffn2_norm[l]), ffn2_w_gate[l], ffn2_w_up[l], ffn2_w_down[l])
        x = rms_norm(x, final_norm[l])
    return x


DEPTH_2 = 2

CTX_LEN = 256
GRID_W = 64
HALF = 0.5
N_ADA = 9
CONV_CH = 384
CONV_K = 31
N_HEADS = 8
Q_LORA = 384
KV_LORA = 256
QK_NOPE = 64
QK_ROPE = 32
V_DIM = 64
ROPE_AXIS = QK_ROPE // 2
ROPE_BASE = 10000.0
ATTN_SCALE = (QK_NOPE + QK_ROPE) ** -0.5
Q_BLOCK = 128
FOURIER_GROUPS = 4
FOURIER_GROUP_CH = 128
FOURIER_WIDTH = FOURIER_GROUPS * FOURIER_GROUP_CH
MIX_WIDTH = 2 * CONV_CH + Q_LORA + KV_LORA + QK_ROPE + FOURIER_WIDTH
N_BRANCH = 3


def rms_norm_2(x, g):
    xf = x.astype(jnp.float32)
    y = xf * lax.rsqrt(jnp.mean(xf * xf, axis=-1, keepdims=True) + EPS)
    return (y * g.astype(jnp.float32)).astype(x.dtype)

def layer_norm(x, g, b):
    xf = x.astype(jnp.float32)
    mu = jnp.mean(xf, axis=-1, keepdims=True)
    var = jnp.mean(jnp.square(xf - mu), axis=-1, keepdims=True)
    y = (xf - mu) * lax.rsqrt(var + EPS)
    return (y * g.astype(jnp.float32) + b.astype(jnp.float32)).astype(x.dtype)

def ada_norm(h, g, shift, scale):
    return rms_norm_2(h, g) * (1 + scale) + shift

def swiglu_2(x, w1, w3, w2):
    return (jax.nn.silu(x @ w1) * (x @ w3)) @ w2

def axial_rope_tables(n_tok, dtype):
    rows = n_tok // GRID_W
    row = jnp.broadcast_to(jnp.arange(rows, dtype=jnp.float32)[:, None], (rows, GRID_W)).reshape(-1)
    col = jnp.broadcast_to(jnp.arange(GRID_W, dtype=jnp.float32)[None, :], (rows, GRID_W)).reshape(-1)
    inv = 1.0 / (ROPE_BASE ** (jnp.arange(ROPE_AXIS // 2, dtype=jnp.float32) * 2.0 / ROPE_AXIS))
    ar = row[:, None] * inv
    ac = col[:, None] * inv
    ang = jnp.concatenate([ar, ar, ac, ac], axis=-1)
    return jnp.cos(ang).astype(dtype), jnp.sin(ang).astype(dtype)

def rotate_half_axial(x):
    xr = x.reshape(x.shape[:-1] + (2, 2, ROPE_AXIS // 2))
    xr = jnp.concatenate([-xr[..., 1:2, :], xr[..., 0:1, :]], axis=-2)
    return xr.reshape(x.shape)

def apply_rope(x, cos, sin):
    return x * cos + rotate_half_axial(x) * sin

def split_mixing(z):
    o1 = 2 * CONV_CH
    o2 = o1 + Q_LORA
    o3 = o2 + KV_LORA
    o4 = o3 + QK_ROPE
    return z[..., :o1], z[..., o1:o2], z[..., o2:o3], z[..., o3:o4], z[..., o4:]

def conv_module(zc, w_dw, b_dw, ln_g, ln_b, w_pw, b_pw):
    a, gt = jnp.split(zc, 2, axis=-1)
    v = a * jax.nn.sigmoid(gt)
    v = lax.conv_general_dilated(v, w_dw[:, None, :].astype(v.dtype), window_strides=(1,),
                                 padding=[(CONV_K // 2, CONV_K // 2)],
                                 dimension_numbers=('NWC', 'WIO', 'NWC'),
                                 feature_group_count=CONV_CH) + b_dw
    v = layer_norm(v, ln_g, ln_b)
    return jax.nn.silu(v) @ w_pw + b_pw

def fourier_mix(zf, w, b):
    bsz, t, _ = zf.shape
    g = zf.reshape(bsz, t, FOURIER_GROUPS, FOURIER_GROUP_CH).astype(jnp.float32)
    f = jnp.fft.fftn(g, axes=(1, 3), norm='ortho').real.astype(zf.dtype)
    return f.reshape(bsz, t, FOURIER_WIDTH) @ w + b

def mla_q(cq, g_qn, w_uq, cos, sin):
    bsz, t, _ = cq.shape
    q = (rms_norm_2(cq, g_qn) @ w_uq).reshape(bsz, t, N_HEADS, QK_NOPE + QK_ROPE)
    if cos is None:
        return q
    q_nope, q_rope = q[..., :QK_NOPE], q[..., QK_NOPE:]
    return jnp.concatenate([q_nope, apply_rope(q_rope, cos[:, None, :], sin[:, None, :])], axis=-1)

def mla_kv(ckv, kr, g_kvn, w_ukv, cos, sin):
    bsz, t, _ = ckv.shape
    kv = (rms_norm_2(ckv, g_kvn) @ w_ukv).reshape(bsz, t, N_HEADS, QK_NOPE + V_DIM)
    k_nope, v = kv[..., :QK_NOPE], kv[..., QK_NOPE:]
    if cos is not None:
        kr = apply_rope(kr, cos, sin)
    k = jnp.concatenate([k_nope, jnp.broadcast_to(kr[:, :, None, :], (bsz, t, N_HEADS, QK_ROPE))], axis=-1)
    return k, v

def attend_dense(q, k, v):
    s = jnp.einsum('bqhd,bkhd->bhqk', q, k, preferred_element_type=jnp.float32) * ATTN_SCALE
    p = jax.nn.softmax(s, axis=-1).astype(v.dtype)
    o = jnp.einsum('bhqk,bkhd->bqhd', p, v)
    return o.reshape(o.shape[0], o.shape[1], N_HEADS * V_DIM)

def attend_blocked(q, k, v):
    bsz, s, _, dk = q.shape
    nb = s // Q_BLOCK
    qb = q.reshape(bsz, nb, Q_BLOCK, N_HEADS, dk).transpose(1, 0, 2, 3, 4)
    o = lax.map(lambda blk: attend_dense(blk, k, v), qb)
    return o.transpose(1, 0, 2, 3).reshape(bsz, s, N_HEADS * V_DIM)

def merge_branches(u, y_conv, y_mla, y_four, w_bg, b_bg, w_out):
    g = jax.nn.sigmoid(u @ w_bg + b_bg)
    g0, g1, g2 = jnp.split(g, N_BRANCH, axis=-1)
    return (g0 * y_conv + g1 * y_mla + g2 * y_four) @ w_out

def second_inputs(seed: int = 0) -> dict:
    key = jax.random.key(seed)
    ks = jax.random.split(key, 40)
    L, D = DEPTH_2, D_MODEL

    def nrm(k, shape, std):
        return jax.random.normal(k, shape, jnp.float32) * std

    def gain(k, shape):
        return 1.0 + nrm(k, shape, 0.02)

    return {
        'x': nrm(ks[0], (BATCH, SEQ, D), 1.0),
        'c': nrm(ks[1], (BATCH, D), 1.0),
        'ctx': nrm(ks[2], (BATCH, CTX_LEN, D), 1.0),
        'c_ctx': nrm(ks[3], (D,), 1.0),
        'w_ada': nrm(ks[4], (L, D, N_ADA * D), 0.5 * D ** -0.5),
        'b_ada': nrm(ks[5], (L, N_ADA * D), 0.02),
        'g_ffn1': gain(ks[6], (L, D)),
        'w1_ffn1': nrm(ks[7], (L, D, D_FF), D ** -0.5),
        'w3_ffn1': nrm(ks[8], (L, D, D_FF), D ** -0.5),
        'w2_ffn1': nrm(ks[9], (L, D_FF, D), D_FF ** -0.5),
        'g_mix': gain(ks[10], (L, D)),
        'w_in': nrm(ks[11], (L, D, MIX_WIDTH), D ** -0.5),
        'w_dw': nrm(ks[12], (L, CONV_K, CONV_CH), CONV_K ** -0.5),
        'b_dw': nrm(ks[13], (L, CONV_CH), 0.02),
        'ln_g_conv': gain(ks[14], (L, CONV_CH)),
        'ln_b_conv': nrm(ks[15], (L, CONV_CH), 0.02),
        'w_pw_conv': nrm(ks[16], (L, CONV_CH, D), CONV_CH ** -0.5),
        'b_pw_conv': nrm(ks[17], (L, D), 0.02),
        'g_qnorm': gain(ks[18], (L, Q_LORA)),
        'w_uq': nrm(ks[19], (L, Q_LORA, N_HEADS * (QK_NOPE + QK_ROPE)), Q_LORA ** -0.5),
        'g_kvnorm': gain(ks[20], (L, KV_LORA)),
        'w_ukv': nrm(ks[21], (L, KV_LORA, N_HEADS * (QK_NOPE + V_DIM)), KV_LORA ** -0.5),
        'w_o_mla': nrm(ks[22], (L, N_HEADS * V_DIM, D), (N_HEADS * V_DIM) ** -0.5),
        'w_fourier': nrm(ks[23], (L, FOURIER_WIDTH, D), FOURIER_WIDTH ** -0.5),
        'b_fourier': nrm(ks[24], (L, D), 0.02),
        'w_bgate': nrm(ks[25], (L, D, N_BRANCH * D), D ** -0.5),
        'b_bgate': nrm(ks[26], (L, N_BRANCH * D), 0.02),
        'w_out': nrm(ks[27], (L, D, D), D ** -0.5),
        'g_ffn2': gain(ks[28], (L, D)),
        'w1_ffn2': nrm(ks[29], (L, D, D_FF), D ** -0.5),
        'w3_ffn2': nrm(ks[30], (L, D, D_FF), D ** -0.5),
        'w2_ffn2': nrm(ks[31], (L, D_FF, D), D_FF ** -0.5),
        'g_final': gain(ks[32], (D,)),
    }

def second_block(x, c, ctx, c_ctx, w_ada, b_ada, g_ffn1, w1_ffn1, w3_ffn1, w2_ffn1, g_mix, w_in,
              w_dw, b_dw, ln_g_conv, ln_b_conv, w_pw_conv, b_pw_conv, g_qnorm, w_uq, g_kvnorm,
              w_ukv, w_o_mla, w_fourier, b_fourier, w_bgate, b_bgate, w_out, g_ffn2, w1_ffn2,
              w3_ffn2, w2_ffn2, g_final):
    cos, sin = axial_rope_tables(x.shape[1], x.dtype)
    h, hc = x, ctx
    for l in range(DEPTH_2):
        last = l == DEPTH_2 - 1
        mod = jax.nn.silu(c) @ w_ada[l] + b_ada[l]
        sh1, sc1, gt1, sh2, sc2, gt2, sh3, sc3, gt3 = [m[:, None, :] for m in jnp.split(mod, N_ADA, axis=-1)]
        modc = jax.nn.silu(c_ctx) @ w_ada[l] + b_ada[l]
        csh1, csc1, cgt1, csh2, csc2, cgt2, csh3, csc3, cgt3 = jnp.split(modc, N_ADA, axis=-1)

        h = h + HALF * gt1 * swiglu_2(ada_norm(h, g_ffn1[l], sh1, sc1), w1_ffn1[l], w3_ffn1[l], w2_ffn1[l])
        hc = hc + HALF * cgt1 * swiglu_2(ada_norm(hc, g_ffn1[l], csh1, csc1), w1_ffn1[l], w3_ffn1[l], w2_ffn1[l])

        u = ada_norm(h, g_mix[l], sh2, sc2)
        uc = ada_norm(hc, g_mix[l], csh2, csc2)
        z_conv, z_cq, z_ckv, z_kr, z_four = split_mixing(u @ w_in[l])
        zc_conv, zc_cq, zc_ckv, zc_kr, zc_four = split_mixing(uc @ w_in[l])

        k_lat, v_lat = mla_kv(z_ckv, z_kr, g_kvnorm[l], w_ukv[l], cos, sin)
        k_ctx, v_ctx = mla_kv(zc_ckv, zc_kr, g_kvnorm[l], w_ukv[l], None, None)
        q_lat = mla_q(z_cq, g_qnorm[l], w_uq[l], cos, sin)
        attn = attend_blocked(q_lat, jnp.concatenate([k_ctx, k_lat], axis=1),
                              jnp.concatenate([v_ctx, v_lat], axis=1))
        y = merge_branches(u,
                           conv_module(z_conv, w_dw[l], b_dw[l], ln_g_conv[l], ln_b_conv[l], w_pw_conv[l], b_pw_conv[l]),
                           attn @ w_o_mla[l],
                           fourier_mix(z_four, w_fourier[l], b_fourier[l]),
                           w_bgate[l], b_bgate[l], w_out[l])
        h = h + gt2 * y
        if not last:
            q_ctx = mla_q(zc_cq, g_qnorm[l], w_uq[l], None, None)
            attn_c = attend_dense(q_ctx, k_ctx, v_ctx)
            yc = merge_branches(uc,
                                conv_module(zc_conv, w_dw[l], b_dw[l], ln_g_conv[l], ln_b_conv[l], w_pw_conv[l], b_pw_conv[l]),
                                attn_c @ w_o_mla[l],
                                fourier_mix(zc_four, w_fourier[l], b_fourier[l]),
                                w_bgate[l], b_bgate[l], w_out[l])
            hc = hc + cgt2 * yc

        h = h + HALF * gt3 * swiglu_2(ada_norm(h, g_ffn2[l], sh3, sc3), w1_ffn2[l], w3_ffn2[l], w2_ffn2[l])
        if not last:
            hc = hc + HALF * cgt3 * swiglu_2(ada_norm(hc, g_ffn2[l], csh3, csc3), w1_ffn2[l], w3_ffn2[l], w2_ffn2[l])
    return rms_norm_2(h, g_final)


def setup_inputs(seed=0):
    out = dict(first_inputs(seed))
    for name, value in second_inputs(seed + 1).items():
        if name != "x":
            out[name + "_2"] = value
    return out


def reference(
    x, ffn1_norm, ffn1_w_gate, ffn1_w_up, ffn1_w_down, mix_norm, w_in, conv_w, a_log, dt_bias,
    gdn_norm_w, q_norm_w, k_norm_w, rel_bias, w_out, ffn2_norm, ffn2_w_gate, ffn2_w_up,
    ffn2_w_down, final_norm, c_2, ctx_2, c_ctx_2, w_ada_2, b_ada_2, g_ffn1_2, w1_ffn1_2,
    w3_ffn1_2, w2_ffn1_2, g_mix_2, w_in_2, w_dw_2, b_dw_2, ln_g_conv_2, ln_b_conv_2,
    w_pw_conv_2, b_pw_conv_2, g_qnorm_2, w_uq_2, g_kvnorm_2, w_ukv_2, w_o_mla_2, w_fourier_2,
    b_fourier_2, w_bgate_2, b_bgate_2, w_out_2, g_ffn2_2, w1_ffn2_2, w3_ffn2_2, w2_ffn2_2,
    g_final_2,
):
    x = first_block(
        x, ffn1_norm, ffn1_w_gate, ffn1_w_up, ffn1_w_down, mix_norm, w_in, conv_w, a_log,
        dt_bias, gdn_norm_w, q_norm_w, k_norm_w, rel_bias, w_out, ffn2_norm, ffn2_w_gate,
        ffn2_w_up, ffn2_w_down, final_norm,
    )
    return second_block(
        x, c_2, ctx_2, c_ctx_2, w_ada_2, b_ada_2, g_ffn1_2, w1_ffn1_2, w3_ffn1_2, w2_ffn1_2,
        g_mix_2, w_in_2, w_dw_2, b_dw_2, ln_g_conv_2, ln_b_conv_2, w_pw_conv_2, b_pw_conv_2,
        g_qnorm_2, w_uq_2, g_kvnorm_2, w_ukv_2, w_o_mla_2, w_fourier_2, b_fourier_2, w_bgate_2,
        b_bgate_2, w_out_2, g_ffn2_2, w1_ffn2_2, w3_ffn2_2, w2_ffn2_2, g_final_2,
    )


_drawn_inputs = setup_inputs


def setup_inputs(seed=0):
    import zlib

    import numpy as np

    out = dict(_drawn_inputs(seed))
    spreads = {}
    factors = {'ffn1_norm': 5.448,
     'mix_norm': 4.137,
     'gdn_norm_w': 6.761,
     'q_norm_w': 8.0,
     'k_norm_w': 8.0,
     'rel_bias': 3.091,
     'ffn2_norm': 7.583,
     'final_norm': 2.769,
     'ctx_2': 4.593,
     'g_ffn1_2': 8.0,
     'g_mix_2': 8.0,
     'b_dw_2': 33.544,
     'ln_g_conv_2': 44.355,
     'ln_b_conv_2': 47.88,
     'b_pw_conv_2': 31.231,
     'g_qnorm_2': 8.0,
     'w_uq_2': 2.726,
     'g_kvnorm_2': 8.0,
     'b_fourier_2': 34.124,
     'b_bgate_2': 23.101,
     'g_ffn2_2': 8.0,
     'g_final_2': 7.767}
    for name, (base, spread) in spreads.items():
        noise = np.random.default_rng([zlib.crc32(name.encode()), seed]).standard_normal(out[name].shape)
        drawn = base * np.exp(spread * noise) if base else spread * noise
        out[name] = jnp.asarray(drawn.astype(out[name].dtype))
    for name, factor in factors.items():
        out[name] = (out[name] * factor).astype(out[name].dtype)
    return out
```

```python
import math
from contextlib import ExitStack

import numpy as np

import concourse.bass as bass
from concourse import mybir

F32 = mybir.dt.float32
F32R = mybir.dt.float32r
ALU = mybir.AluOpType
ACT = mybir.ActivationFunctionType
AX = mybir.AxisListType.X

D, T, FF = 1024, 256, 2816
NF = FF // 128
EPS = 1e-6
UC = 1024
NR, NH, AHEAD = 4, 3, 2

COLS1 = [("ffn1_norm", 8), ("mix_norm", 8), ("ffn2_norm", 8), ("final_norm", 8), ("conv_w", 60),
         ("gdn_norm_w", 1), ("q_norm_w", 1), ("k_norm_w", 1), ("dt_bias", 8), ("a_log", 8)]
COLS2 = [("b_ada", 72), ("g_ffn1", 8), ("g_mix", 8), ("g_ffn2", 8), ("w_dw", 93), ("b_dw", 3), ("ln_g", 3),
         ("ln_b", 3), ("b_pw", 8), ("g_q", 3), ("g_kv", 2), ("b_f", 8), ("b_bg", 24)]


def columns():
    at, out = 0, {}
    for name, n in COLS1 + [(f"{name}{l}", n) for l in range(2) for name, n in COLS2] + [("g_final", 8), ("cc", 16)]:
        out[name] = (at, n)
        at += n
    return out, at


def pieces():
    def ffn(p):
        for j in range(NF):
            yield [(p + "g", k, 128 * j, 128) for k in range(8)]
            yield [(p + "u", k, 128 * j, 128) for k in range(8)]
        for m in range(8):
            yield [(p + "d", k, 128 * m, 128) for k in range(NF)]

    yield from ffn("f1")
    for j in range(12):
        yield [("win", k, 128 * j, 128) for k in range(8)]
    for j in range(12, 16):
        yield [("win", k, 128 * j, 128) for k in range(8)]
    yield [("win", k, 2048, 16) for k in range(8)]
    for j in range(12):
        yield [("win", k, 2064 + 128 * j, 128) for k in range(8)]
    for l in range(2):
        for m in range(72):
            yield [(f"ada{l}", k, 128 * m, 128) for k in range(8)]
    for m in range(8):
        yield [("wout", k, 128 * m, 128) for k in range(8)]
    yield from ffn("f2")
    for l in range(2):
        yield from ffn(f"f1{l}")
        for j in range(4):
            yield [(f"win{l}", k, 1440 + 128 * j, 128) for k in range(8)]
        for c in range(3):
            yield [(f"win{l}", k, 384 + 128 * c, 128) for k in range(8)]
            yield [(f"win{l}", k, 128 * c, 128) for k in range(8)]
        for j in range(5):
            yield [(f"win{l}", k, 768 + 128 * j, 128) for k in range(8)]
        yield [(f"wkr{l}", k, 0, 96) for k in range(8)]
        yield [(f"wv{l}", k, 0, 512) for k in range(2)]
        for h in range(8):
            yield [(f"wuq{l}", k, 96 * h, 96) for k in range(3)] + [(f"wkn{l}", k, 96 * h, 96) for k in range(2)]
        for m in range(8):
            yield [(f"wbg{l}", k, 128 * m, 128) for k in range(8)]
            yield [(f"wbg{l}", k, 1024 + 128 * m, 128) for k in range(8)]
            yield [(f"wbg{l}", k, 2048 + 128 * m, 128) for k in range(8)]
            yield [(f"wpw{l}", k, 128 * m, 128) for k in range(3)] + [(f"wo{l}", k, 128 * m, 128) for k in range(4)]
            yield [(f"wf{l}", k, 128 * m, 128) for k in range(4)]
        for m in range(8):
            yield [(f"wout{l}", k, 128 * m, 128) for k in range(8)]
        yield from ffn(f"f2{l}")


def plan():
    units, at = [], 0
    for group in pieces():
        unit, n = [], 0
        for p in group:
            if n + p[3] > UC:
                units.append((at, n, unit))
                at, unit, n = at + 128 * n, [], 0
            unit.append((p, n))
            n += p[3]
        units.append((at, n, unit))
        at += 128 * n
    return units, at


def const_blocks():
    p, f = np.arange(128)[:, None], np.arange(128)[None, :]
    out = {"ident": p == f, "ones": np.ones((128, 128)), "bd": (p // 64) == (f // 64),
           "LE": p <= f, "GE": p >= f, "GT": p > f, "LT": p < f}
    for l in range(7):
        s = 1 << l
        low = ((p // (2 * s)) == (f // (2 * s))) & ((p // s) % 2 == 1) & ((f // s) % 2 == 0)
        out[f"ML{l}"], out[f"MU{l}"] = low, low.T
    x = np.arange(384)[None, :] - 128 - p
    n = (np.abs(x) <= 64).astype(np.float32) + (x % 4 == 0) + (x % 16 == 0)
    out["mult"] = n
    out["amask"] = np.where(n > 0, 0.0, -1e30)
    return {k: np.asarray(v, np.float32) for k, v in out.items()}


def const_blocks2():
    out = {}
    rot = np.zeros((128, 128))
    for a in range(2):
        for i in range(8):
            lo, hi = 64 + 16 * a + i, 64 + 16 * a + 8 + i
            rot[hi, lo] = -1.0
            rot[lo, hi] = 1.0
    out["rot"] = rot
    t = np.arange(T)
    inv = (1.0 / (np.float32(10000.0) ** (np.arange(8, dtype=np.float32) * np.float32(2.0) / np.float32(16)))).astype(np.float32)
    ar, ac = ((t // 64).astype(np.float32)[:, None] * inv), ((t % 64).astype(np.float32)[:, None] * inv)
    ang = np.concatenate([ar, ar, ac, ac], axis=1).astype(np.float32)
    cos, sin = np.zeros((128, T), np.float32), np.zeros((128, T), np.float32)
    cos[:64] = 1.0
    cos[64:96], sin[64:96] = np.cos(ang).T, np.sin(ang).T
    out["cos"], out["sin"] = cos, sin
    a = 2 * np.pi * np.outer(np.arange(128), np.arange(128)) / 128
    out["cs"] = np.concatenate([np.cos(a), np.sin(a)], axis=1)
    b = 2 * np.pi * np.outer(t, t) / T
    s = 1.0 / math.sqrt(T * 128)
    out["ct"] = (np.cos(b) * s).reshape(2, 128, T).transpose(1, 0, 2).reshape(128, 2 * T)
    out["st"] = (-np.sin(b) * s).reshape(2, 128, T).transpose(1, 0, 2).reshape(128, 2 * T)
    return {k: np.asarray(v, np.float32) for k, v in out.items()}


def t5_buckets():
    rel = np.arange(-255, 256)
    n = np.abs(rel)
    large = 8 + (np.log(np.maximum(n, 1) / 8) / math.log(1024 / 8) * 8).astype(np.int32)
    return (rel > 0).astype(np.int32) * 16 + np.where(n < 8, n, np.minimum(large, 15))


class Slot:

    def __init__(self, ap):
        self.ap, self.free, self.held = ap, [], False

    def done(self, *toks):
        self.free, self.held = list(toks), False


class Ring:
    def __init__(self, aps):
        self.slots, self.n = [Slot(a) for a in aps], 0

    def get(self):
        while self.slots[self.n % len(self.slots)].held:
            self.n += 1
            assert not all(s.held for s in self.slots)
        s = self.slots[self.n % len(self.slots)]
        self.n += 1
        s.held = True
        return s


class Prog:

    def __init__(self, nc, stack):
        self.nc, self.stack = nc, stack
        self.q = {e: [] for e in ("pe", "act", "dve", "pool", "sp")}
        self.count = dict.fromkeys(self.q, 0)
        self.seen = {}
        self.sems = {}
        self.table = None
        for e in ("pe", "act", "dve", "pool"):
            self.sem(e)

    def sem(self, name):
        if name not in self.sems:
            self.sems[name] = self.stack.enter_context(self.nc.semaphore("s_" + name))
            self.count[name] = 0
        return name

    def wait(self, e, toks):
        for t in toks:
            if t is None:
                continue
            if isinstance(t, list):
                self.wait(e, t)
                continue
            name, value = t
            if self.seen.get((e, name), 0) < value:
                self.seen[e, name] = value
                self.q[e].append(lambda eng, s=self.sems[name], v=value: eng.wait_ge(s, v))

    def do(self, e, fn, *toks, sig=True):
        self.wait(e, toks)
        if sig:
            self.count[e] += 1
            self.q[e].append(lambda eng, s=self.sems[e]: fn(eng).then_inc(s, 1))
        else:
            self.q[e].append(fn)
        return (e, self.count[e])

    def dma(self, out, in_, name, *toks, e="sp"):
        self.wait(e, toks)
        self.sem(name)
        self.count[name] += 16
        self.q[e].append(lambda eng, s=self.sems[name]: eng.dma_start(out, in_).then_inc(s, 16))
        return (name, self.count[name])

    def act(self, out, in_, f, *toks, **kw):
        if f in (ACT.Exp, ACT.Ln, ACT.Silu, ACT.Sigmoid):
            table = "natural_log_exp_and_others" if f in (ACT.Exp, ACT.Ln) else f
            if table != self.table and table != f:
                self.q["act"].append(lambda eng: eng.preload_act_table_set(table))
            self.table = table
        return self.do("act", lambda g: g.activation(out, in_, f, **kw), *toks)

    def tt(self, e, out, a, b, op, *toks):
        return self.do(e, lambda g: g.tensor_tensor(out, a, b, op), *toks)

    def ts(self, e, out, a, s1, s2, op0, op1, *toks):
        if s2 is None:
            return self.do(e, lambda g: g.tensor_scalar(out, a, s1, None, op0), *toks)
        return self.do(e, lambda g: g.tensor_scalar(out, a, s1, s2, op0, op1), *toks)

    def stt(self, out, a, s, b, op0, op1, *toks):
        return self.do("dve", lambda g: g.scalar_tensor_tensor(out=out, in0=a, scalar=s, in1=b, op0=op0, op1=op1), *toks)

    def copy(self, e, out, in_, *toks):
        return self.do(e, lambda g: g.tensor_copy(out, in_), *toks)

    def recip(self, out, in_, *toks):
        return self.do("dve", lambda g: g.reciprocal(out, in_), *toks)

    def mm(self, out, w, x, start, stop, *toks, sig=None):
        return self.do("pe", lambda g: g.matmul(out, w, x, start=start, stop=stop), *toks,
                       sig=stop if sig is None else sig)

    def tr(self, out, in_, ident, *toks, sig=True):
        return self.do("pe", lambda g: g.transpose(out, in_, ident), *toks, sig=sig)

    def flush(self):
        nc, q = self.nc, self.q
        with nc.Block() as block:
            @block.sync
            def _(eng):
                for f in q["sp"]:
                    f(eng)

            @block.scalar
            def _(eng):
                for f in q["act"]:
                    f(eng)

            @block.vector
            def _(eng):
                for f in q["dve"]:
                    f(eng)

            @block.gpsimd
            def _(eng):
                for f in q["pool"]:
                    f(eng)

            @block.tensor
            def _(eng):
                for f in q["pe"]:
                    f(eng)


class Weights:

    def __init__(self, P, dram):
        self.P, self.dram = P, dram
        self.units, _ = plan()
        e = P.stack.enter_context
        self.raw = e(P.nc.sbuf_tensor("w_raw", [128, NR, UC], F32))
        self.hi = e(P.nc.sbuf_tensor("w_hi", [128, NH, UC], F32R))
        self.lo = e(P.nc.sbuf_tensor("w_lo", [128, NH, UC], F32R))
        self.split_of = {}
        n = 0
        for u, (_, _, ps) in enumerate(self.units):
            if not ps[0][0][0].startswith("ada"):
                self.split_of[u] = n
                n += 1
        self.splits = sorted(self.split_of)
        self.loaded, self.raw_free, self.landed = 0, {}, {}
        self.nsplit, self.split_tok, self.pe_done = 0, {}, {}
        self.u, self.i = 0, 0
        for _ in range(NR):
            self.load()

    def load(self):
        u = self.loaded
        if u >= len(self.units):
            return
        at, n, _ = self.units[u]
        src = bass.AP(tensor=self.dram.tensor, offset=at, ap=[[n, 128], [1, n]])
        free = self.raw_free[u - NR] if u >= NR else None
        self.landed[u] = self.P.dma(self.raw[:, u % NR, 0:n], src, f"w{u % NR}", free)
        self.loaded += 1

    def split(self):
        if self.nsplit >= len(self.splits):
            return False
        u = self.splits[self.nsplit]
        if u >= self.loaded:
            return False
        s, n = self.nsplit % NH, self.units[u][1]
        raw, hi, lo = self.raw[:, u % NR, 0:n], self.hi[:, s, 0:n], self.lo[:, s, 0:n]
        reader = self.pe_done[self.nsplit - NH] if self.nsplit >= NH else None
        a = self.P.act(hi, raw, ACT.Copy, self.landed[u], reader)
        b = self.P.tt("dve", lo, raw, hi.bitcast(F32), ALU.subtract, a)
        self.split_tok[u] = b
        self.raw_free[u] = b
        self.nsplit += 1
        self.load_more()
        return True

    def load_more(self):
        while self.loaded < len(self.units) and self.loaded - NR in self.raw_free:
            self.load()

    def next(self, key):
        at, n, ps = self.units[self.u]
        p, c = ps[self.i]
        assert p == key, (p, key)
        u, m, last = self.u, p[3], self.i == len(ps) - 1
        if u in self.split_of:
            if self.i == 0:
                while self.nsplit <= self.split_of[u] + AHEAD and self.split():
                    pass
            s = self.split_of[u] % NH
            out = (self.hi[:, s, c:c + m], self.lo[:, s, c:c + m], self.split_tok[u], last)
        else:
            out = (self.raw[:, u % NR, c:c + m], None, self.landed[u], last)
        self.i += 1
        if last:
            self.u, self.i, self.last = u + 1, 0, u
        return out

    def release(self, tok):
        u = self.last
        if u in self.split_of:
            self.pe_done[self.split_of[u]] = tok
        else:
            self.raw_free[u] = tok
            self.load_more()


def build(nc, wstream, cols, consts, consts2, bias, xin, out, taps=None, stop=None):
    with ExitStack() as stack:
        P = Prog(nc, stack)
        program(P, nc, stack, wstream, cols, consts, consts2, bias, xin, out, taps or {}, stop)
        P.flush()


def program(P, nc, stack, wstream, cols, consts, consts2, bias, xin, out, taps, stop):
    ent = stack.enter_context

    def sb(name, shape, dt=F32, st=None):
        return (st or stack).enter_context(nc.sbuf_tensor(name, shape, dt))

    W = Weights(P, wstream)
    X = sb("X", [128, 8, 512])
    UH, UL = sb("UH", [128, 8, 512], F32R), sb("UL", [128, 8, 512], F32R)
    COL, ncol = columns()
    PC = sb("PC", [128, ncol])
    C1 = sb("C1", [128, 256])
    ident, ones = C1[:, 0:128], C1[:, 128:256]
    tmp = sb("TMP", [128, 6, 512])
    TM = Ring([tmp[:, i, :] for i in range(6)])
    ssb = sb("SSB", [128, 3, 512])
    SSR, RBR = Ring([ssb[:, 0, :]]), Ring([ssb[:, i, :] for i in (1, 2)])
    small = sb("SMALL", [128, 8, 8])
    SM = Ring([small[:, i, :] for i in range(8)])
    MOD = sb("MOD", [128, 2, 72, 2])
    DER = sb("DER", [128, 2, 6, 8, 2])
    GP = Ring([ent(nc.psum_tensor(f"G{i}", [128, 512], F32))[:] for i in range(4)])
    MP = Ring([ent(nc.psum_tensor(f"M{i}", [128, 512], F32))[:] for i in range(4)])

    def col(name, k=0, n=1):
        at, _ = COL[name]
        return PC[:, at + k:at + k + n]

    xload = P.dma(X[:], xin.rearrange("p (c t) -> p c t", c=8), "x")
    cload = P.dma(PC[:], cols, "cols")
    c1load = P.dma(C1[:], consts[:, 0:256], "c1")
    tapped = []

    def tap(name, ap, *toks):
        if name in taps:
            tapped.append(P.dma(taps[name], ap, "tap_" + name, *toks))
        if stop == name:
            P.wait("sp", tapped)
            P.flush()
            P.q = {e: [] for e in P.q}
            P.flush = lambda: None

    def every(*engines):
        return [(e, P.count[e]) for e in engines]

    def gemm(keys, xh, xl, m, n, *toks, each=None):
        g = GP.get()
        ps = g.ap[0:m, 0:n]
        for i, key in enumerate(keys):
            wh, wl, ready, last = W.next(key)
            first, end = i == 0, i == len(keys) - 1
            P.mm(ps, wh, xh(i), first, False, ready, *toks, g.free, each and each[i], sig=False)
            P.mm(ps, wh, xl(i), False, False, sig=False)
            t = P.mm(ps, wl, xh(i), False, end, sig=end or last)
            if last:
                W.release(t)
        return g, ps, t

    def cut(hi, lo, src, *toks):
        a = P.act(hi, src, ACT.Copy, *toks)
        b = P.tt("dve", lo, src, hi.bitcast(F32), ALU.subtract, a)
        return a, b

    class Stat:

        def __init__(self, n):
            self.s, self.n, self.tok = SSR.get(), n, None

        def add(self, ap, *toks):
            if self.tok is None:
                self.tok = P.act(self.s.ap[:, 0:self.n], ap, ACT.Square, self.s.free, *toks)
                return self.tok
            t = TM.get()
            a = P.act(t.ap[:, 0:self.n], ap, ACT.Square, t.free, *toks)
            self.tok = P.tt("dve", self.s.ap[:, 0:self.n], self.s.ap[:, 0:self.n], t.ap[:, 0:self.n], ALU.add,
                            a, self.tok)
            t.done(self.tok)
            return a

        def rsqrt(self, count):
            m, r, n = MP.get(), RBR.get(), self.n
            a = P.mm(m.ap[:, 0:n], ones, self.s.ap[:, 0:n], True, True, self.tok, m.free, c1load)
            self.s.done(a)
            b, m_free = rsqrt(r.ap[:, 0:n], m.ap[:, 0:n], 1.0 / count, a, r.free)
            m.done(m_free)
            return r, b

    def rsqrt(out_, ps, scale, *toks):
        a = P.act(out_, ps, ACT.Ln, *toks, scale=scale, bias=EPS)
        return P.act(out_, out_, ACT.Exp, a, scale=-0.5), a

    def norm_to_u(r, rtok, gcol, n, *toks):
        ready = []
        for k in range(8):
            t = TM.get()
            a = P.stt(t.ap[:, 0:n], X[:, k, 0:n], gcol(k), r.ap[:, 0:n], ALU.mult, ALU.mult, rtok, t.free, cload)
            b, c = cut(UH[:, k, 0:n], UL[:, k, 0:n], t.ap[:, 0:n], a, *toks)
            t.done(c)
            ready.append(c)
        r.done(a)
        return ready

    def ada_to_u(r, rtok, A, B, n, *toks):
        ready = []
        for k in range(8):
            t = TM.get()
            for s in range(n // 256):
                c = slice(256 * s, 256 * s + 256)
                a = P.stt(t.ap[:, c], X[:, k, c], A(k, s), r.ap[:, c], ALU.mult, ALU.mult, rtok, t.free)
                b = P.act(UH[:, k, c], t.ap[:, c], ACT.Identity, a, *toks, bias=B(k, s))
                d = P.stt(UL[:, k, c], t.ap[:, c], B(k, s), UH[:, k, c].bitcast(F32), ALU.add, ALU.subtract, b)
            t.done(d)
            ready.append(d)
        r.done(a)
        return ready

    uh = lambda n, s=0: (lambda k: UH[:, k, s:s + n])
    ul = lambda n, s=0: (lambda k: UL[:, k, s:s + n])

    def ffn(pre, n, ready, gate, tag):
        with ExitStack() as st:
            HH, HL = sb("HH" + tag, [128, NF, n], F32R, st), sb("HL" + tag, [128, NF, n], F32R, st)
            cuts = []
            old = every("pe", "act", "dve", "pool")
            for j in range(NF):
                gg, pg, tg = gemm([(pre + "g", k, 128 * j, 128) for k in range(8)], uh(n), ul(n), 128, n, each=ready)
                gu, pu, tu = gemm([(pre + "u", k, 128 * j, 128) for k in range(8)], uh(n), ul(n), 128, n)
                t = TM.get()
                h = t.ap[:, 0:n]
                a = P.act(h, pg, ACT.Silu, tg, t.free)
                gg.done(a)
                b = P.tt("dve", h, h, pu, ALU.mult, a, tu)
                gu.done(b)
                c, d = cut(HH[:, j, :], HL[:, j, :], h, b, old)
                t.done(d)
                cuts.append(d)
            stat = Stat(n)
            for m in range(8):
                g, ps, t = gemm([(pre + "d", k, 128 * m, 128) for k in range(NF)], lambda k: HH[:, k, :],
                                lambda k: HL[:, k, :], 128, n, each=cuts)
                xt = add_to_x(m, ps, n, gate, t)
                g.done(xt)
                stat.add(X[:, m, 0:n], xt)
            return stat, xt

    def add_to_x(m, ps, n, gate, tok):
        if gate is None:
            return P.stt(X[:, m, 0:n], ps, 0.5, X[:, m, 0:n], ALU.mult, ALU.add, tok)
        for s in range(n // 256):
            c = slice(256 * s, 256 * s + 256)
            a = P.stt(X[:, m, c], ps[:, c], gate(m, s), X[:, m, c], ALU.mult, ALU.add, tok)
        return a

    stat = Stat(256)
    for k in range(8):
        stat.add(X[:, k, 0:256], xload)
    r, rt = stat.rsqrt(D)
    ready = norm_to_u(r, rt, lambda k: col("ffn1_norm", k), 256)
    stat, xt = ffn("f1", 256, ready, None, "a")
    tap("x1", X[:, :, 0:256], xt)

    r, rt = stat.rsqrt(D)
    ready = norm_to_u(r, rt, lambda k: col("mix_norm", k), 256, every("pe"))
    mix1(P, nc, stack, sb, W, gemm, cut, rsqrt, tap, every, col, TM, MP, GP, SM, RBR, SSR, X, UH, UL, uh, ul,
         ready, consts, bias, ident, ones, cload, c1load, MOD)
    stat = Stat(256)
    oready = every("act", "dve")
    for m in range(8):
        g, ps, t = gemm([("wout", k, 128 * m, 128) for k in range(8)], uh(256), ul(256), 128, 256, oready)
        a = P.tt("dve", X[:, m, 0:256], X[:, m, 0:256], ps, ALU.add, t)
        g.done(a)
        stat.add(X[:, m, 0:256], a)
    tap("x2", X[:, :, 0:256], a)
    r, rt = stat.rsqrt(D)
    ready = norm_to_u(r, rt, lambda k: col("ffn2_norm", k), 256, every("pe"))
    stat, xt = ffn("f2", 256, ready, None, "b")
    r, rt = stat.rsqrt(D)
    old = every("act")
    for k in range(8):
        a = P.stt(X[:, k, 0:256], X[:, k, 0:256], col("final_norm", k), r.ap[:, 0:256], ALU.mult, ALU.mult, rt, old, xt)
    r.done(a)
    tap("x3", X[:, :, 0:256], a)
    block2(P, nc, stack, sb, W, gemm, cut, rsqrt, tap, every, col, TM, MP, GP, SM, RBR, SSR, X, UH, UL, uh, ul,
           consts2, ident, ones, MOD, DER, Stat, ffn, ada_to_u, add_to_x, a, out)


def mix1(P, nc, stack, sb, W, gemm, cut, rsqrt, tap, every, col, TM, MP, GP, SM, RBR, SSR, X, UH, UL, uh, ul,
         ready, consts, bias, ident, ones, cload, c1load, MOD):
    names = list(const_blocks())
    with ExitStack() as st:
        def tile(name, shape, dt=F32):
            return sb(name, shape, dt, st)

        CN = tile("CN", [128, 19 * 128 + 768])
        old = every("pe", "act", "dve")
        cn = P.dma(CN[:], consts[:, 256:], "cn", old, e="pool")

        def C(name):
            i = names.index(name) - 2
            if name == "mult":
                return CN[:, 19 * 128:19 * 128 + 384]
            if name == "amask":
                return CN[:, 19 * 128 + 384:19 * 128 + 768]
            return CN[:, 128 * i:128 * i + 128]

        CQ = tile("CQ", [128, 12, 256])
        ZG = tile("ZG", [128, 4, 256])
        KT, VT = tile("KT", [128, 2, 512]), tile("VT", [128, 2, 512])
        OS = tile("OS", [128, 4, 256])
        G, BETA = tile("G", [128, 2, 8]), tile("BETA", [128, 2, 8])
        GA = tile("GA", [128, 6, 16])
        win = lambda c, m=128: [("win", k, c, m) for k in range(8)]

        with ExitStack() as s2:
            CV = sb("CV", [128, 12, 260], F32, s2)
            pads = [P.do("pool", lambda g: g.memset(CV[:, :, 0:2], 0.0), old),
                    P.do("pool", lambda g: g.memset(CV[:, :, 258:260], 0.0))]
            w0 = COLW = col("conv_w", 0, 60)
            done = []
            for j in range(12):
                g, ps, t = gemm(win(128 * j), uh(256), ul(256), 128, 256, each=ready)
                a = P.act(CV[:, j, 2:258], ps, ACT.Copy, t, old)
                g.done(a)
                acc = TM.get()
                o = acc.ap[:, 0:256]
                b = P.ts("dve", o, CV[:, j, 0:256], col("conv_w", 5 * j), None, ALU.mult, None, a, acc.free, pads)
                for i in range(1, 5):
                    b = P.stt(o, CV[:, j, i:i + 256], col("conv_w", 5 * j + i), o, ALU.mult, ALU.add, b)
                c = P.act(CQ[:, j, :], o, ACT.Silu, b, old)
                acc.done(c)
                done.append(c)
            for h in range(4):
                g, ps, t = gemm(win(128 * (12 + h)), uh(256), ul(256), 128, 256)
                zt = P.act(ZG[:, h, :], ps, ACT.Silu, t)
                g.done(zt)
            tap("conv", CQ[:], done)

            pc = [W.next(k) for k in win(2048, 16)]
            g = GP.get()
            for i in range(2):
                for k in range(8):
                    wh, wl, rdy, _ = pc[k]
                    x = slice(128 * i, 128 * i + 128)
                    o = g.ap[:, 16 * i:16 * i + 16]
                    P.mm(o, UH[:, k, x], wh, k == 0, False, rdy, g.free, sig=False)
                    P.mm(o, UH[:, k, x], wl, False, False, sig=False)
                    t = P.mm(o, UL[:, k, x], wh, False, k == 7)
            W.release(t)
            AB = g.ap[:, 0:32].rearrange("p (i c) -> p i c", i=2)
            a = [GA[:, i, :].rearrange("p (i c) -> p i c", i=2) for i in range(6)]
            row = lambda name: col(name, 0, 8).unsqueeze(1).broadcast_to([128, 2, 8])
            t1 = P.tt("dve", a[0], AB[:, :, 0:8], row("dt_bias"), ALU.add, t, old)
            t2 = P.act(a[1], a[0], ACT.Abs, t1)
            t3 = P.act(a[2], a[1], ACT.Exp, t2, scale=-1.0)
            t4 = P.act(a[2], a[2], ACT.Ln, t3, bias=1.0)
            t5 = P.act(a[3], row("a_log"), ACT.Exp)
            t6 = P.act(a[4], AB[:, :, 8:16], ACT.Exp, scale=-1.0)
            g.done(t1, t6)
            t7 = P.ts("dve", a[0], a[0], 0.0, None, ALU.max, None, t2)
            t8 = P.tt("dve", a[0], a[0], a[2], ALU.add, t4, t7)
            t9 = P.ts("dve", a[0], a[0], -1.0, None, ALU.mult, None, t8)
            gt = P.tt("dve", G[:], a[0], a[3], ALU.mult, t9, t5)
            t11 = P.ts("dve", a[4], a[4], 1.0, None, ALU.add, None, t6)
            bt = P.recip(BETA[:], a[4], t11)
            tap("g", G[:], gt)
            tap("beta", BETA[:], bt)

            qk = []
            for c in range(4):
                v = CQ[:, 2 * c:2 * c + 2, :]
                s, m, r = TM.get(), MP.get(), RBR.get()
                sq = P.act(s.ap, v, ACT.Square, s.free, done)
                mt = P.mm(m.ap, ones, s.ap, True, True, sq, m.free)
                s.done(mt)
                e, f = rsqrt(r.ap, m.ap, 1.0, mt, r.free)
                m.done(f)
                scale = 128 ** -0.5 if c < 2 else 1.0
                rv = r.ap.rearrange("p (a b) -> p a b", a=2)
                u = P.stt(v, v, scale, rv, ALU.mult, ALU.mult, e)
                r.done(u)
                qk.append(u)
            tap("qk", CQ[:], qk)
            kv = []
            for i in range(2):
                for base, dst in ((4, KT), (8, VT)):
                    m = MP.get()
                    for h in range(4):
                        t = P.tr(m.ap[:, 128 * h:128 * h + 128], CQ[:, base + h, 128 * i:128 * i + 128], ident,
                                 m.free, qk, done, sig=h == 3)
                    u = P.copy("dve", dst[:, i, :], m.ap, t)
                    m.done(u)
                    kv.append(u)
        conv_done = every("act", "dve")

        uq = every("pe")
        with ExitStack() as s2:
            QB = sb("QB", [128, 8, 256], F32, s2)
            VB = sb("VB", [128, 2, 512], F32, s2)
            BW = sb("BW", [128, 8, 384], F32, s2)
            PT = sb("PT", [128, 2, 2, 256], F32, s2)
            PTR = Ring([PT[:, 0], PT[:, 1]])
            bl = P.dma(BW[:], bias, "bw", old, conv_done, e="pool")
            bw = P.tt("dve", BW[:], BW[:], C("amask").unsqueeze(1).broadcast_to([128, 8, 384]), ALU.add, bl, cn)
            qn = []
            for j in range(8):
                g, ps, t = gemm(win(2064 + 128 * j), uh(256), ul(256), 128, 256)
                s, m, r = TM.get(), MP.get(), RBR.get()
                sq = P.act(s.ap[:, 0:256], ps, ACT.Square, s.free, t)
                mt = P.mm(m.ap[:, 0:256], C("bd"), s.ap[:, 0:256], True, True, sq, m.free, cn)
                s.done(mt)
                e, f = rsqrt(r.ap[:, 0:256], m.ap[:, 0:256], 1.0 / 64, mt, r.free)
                m.done(f)
                u = P.stt(QB[:, j, :], ps, col("q_norm_w" if j < 4 else "k_norm_w"), r.ap[:, 0:256],
                          ALU.mult, ALU.mult, e, conv_done)
                if j < 4:
                    u = P.ts("dve", QB[:, j, :], QB[:, j, :], 64 ** -0.5, None, ALU.mult, None, u)
                r.done(u)
                g.done(u)
                qn.append(u)
            vb = []
            mv = [MP.get(), MP.get()]
            for j in range(4):
                g, ps, t = gemm(win(2064 + 128 * (8 + j)), uh(256), ul(256), 128, 256)
                s = TM.get()
                u = P.act(s.ap[:, 0:256], ps, ACT.Copy, s.free, t)
                g.done(u)
                for i in range(2):
                    tv = P.tr(mv[i].ap[:, 128 * j:128 * j + 128], s.ap[:, 128 * i:128 * i + 128], ident,
                              u, mv[i].free)
                s.done(tv)
            for i in range(2):
                u = P.copy("dve", VB[:, i, :], mv[i].ap, tv, conv_done)
                mv[i].done(u)
                vb.append(u)
            uq = every("pe")
            tap("qb", QB[:], qn)
            for c in range(4):
                o = MP.get()
                for h in (2 * c, 2 * c + 1):
                    b = 64 * (h % 2)
                    m, sm = MP.get(), SM.get()
                    for i in range(2):
                        t = P.mm(m.ap[:, 256 * i:256 * i + 256], QB[b:b + 64, c, 128 * i:128 * i + 128],
                                 QB[b:b + 64, 4 + c, :], True, True, qn, m.free)
                    s, s2_ = TM.get(), TM.get()
                    mx = []
                    for i in range(2):
                        w = BW[:, h, 128 * (1 - i):128 * (1 - i) + 256]
                        v = s.ap[:, 256 * i:256 * i + 256]
                        mx.append(P.do("dve", lambda e, v=v, w=w, i=i, m=m, sm=sm: e.tensor_tensor_reduce(
                            v, m.ap[:, 256 * i:256 * i + 256], w, 1.0, -3.0e38, ALU.add, ALU.max,
                            sm.ap[:, i:i + 1]), t, s.free, sm.free, bw))
                    m.done(mx[-1])
                    ng = P.ts("dve", sm.ap[:, 2:4], sm.ap[:, 0:2], -1.0, None, ALU.mult, None, mx)
                    ex = []
                    for i in range(2):
                        v = s.ap[:, 256 * i:256 * i + 256]
                        ex.append(P.act(v, v, ACT.Exp, ng, bias=sm.ap[:, 2 + i:3 + i]))
                    dn = []
                    for i in range(2):
                        n_ = C("mult")[:, 128 * (1 - i):128 * (1 - i) + 256]
                        v, y = s.ap[:, 256 * i:256 * i + 256], s2_.ap[:, 256 * i:256 * i + 256]
                        dn.append(P.do("dve", lambda e, v=v, y=y, n_=n_, i=i, sm=sm: e.tensor_tensor_reduce(
                            y, v, n_, 1.0, 0.0, ALU.mult, ALU.add, sm.ap[:, 4 + i:5 + i]), ex, s2_.free))
                    s.done(dn[-1])
                    rc = P.recip(sm.ap[:, 6:8], sm.ap[:, 4:6], dn)
                    nm = []
                    for i in range(2):
                        y = s2_.ap[:, 256 * i:256 * i + 256]
                        nm.append(P.ts("dve", y, y, sm.ap[:, 6 + i:7 + i], None, ALU.mult, None, rc))
                    sm.done(nm[-1])
                    m, pt = MP.get(), PTR.get()
                    for kc in range(2):
                        for i in range(2):
                            t = P.tr(m.ap[:, 256 * kc + 128 * i:256 * kc + 128 * i + 128],
                                     s2_.ap[:, 256 * i + 128 * kc:256 * i + 128 * kc + 128], ident, nm, m.free)
                    s2_.done(t)
                    ev = P.act(pt.ap, m.ap.rearrange("p (a b) -> p a b", a=2), ACT.Copy, t, pt.free, conv_done)
                    m.done(ev)
                    for kc in range(2):
                        t = P.mm(o.ap[b:b + 64, 0:256], VB[:, kc, 64 * h:64 * h + 64], pt.ap[:, kc, :],
                                 kc == 0, kc == 1, ev, vb, o.free)
                    pt.done(t)
                _, u = cut(UH[:, 4 + c, 0:256], UL[:, 4 + c, 0:256], o.ap[:, 0:256], t, uq)
                o.done(u)
            tap("uswa", UH[:, 4:8, 0:256].bitcast(F32), every("act"))
            swa_done = every("act", "dve", "pe")

        NT = 12
        GT_ = tile("GDN", [128, 2, NT, 512])
        sets = [{n: Slot(GT_[:, i, j, :]) for j, n in enumerate(
            ("gt", "L", "IT", "UU", "T", "P", "Y", "UL", "VB", "KD", "VN", "S"))} for i in range(2)]
        for s in sets:
            for v in s.values():
                v.done(*swa_done)
            s["WT"], s["QG"] = s["L"], s["UU"]
        h4 = lambda ap: ap.rearrange("p (h c) -> p h c", h=4)
        bc = lambda ap: ap.unsqueeze(1).broadcast_to([128, 4, 128])
        cb = lambda ap: ap.unsqueeze(2).broadcast_to([128, 4, 128])
        hs = lambda ap, h: ap[:, 128 * h:128 * h + 128]
        first_o = {}
        state = {}
        ada = ada_maker(P, W, MP, MOD, col, TM, tile, old, cload)
        for order in range(2):
            B = []
            for d in range(2):
                i = order if d == 0 else 1 - order
                b = dict(d=d, i=i, t=sets[d], tri="LE" if d == 0 else "GE", st="GT" if d == 0 else "LT",
                         lm="ML" if d == 0 else "MU", um="MU" if d == 0 else "ML")
                B.append(b)
            for b in B:
                d, i, t = b["d"], b["i"], b["t"]
                free = [v.free for v in t.values()]
                ck = slice(128 * i, 128 * i + 128)
                gcol, bcol = G[:, i, 4 * d:4 * d + 4], BETA[:, i, 4 * d:4 * d + 4]
                gtri = t["gt"].ap
                a = P.tt("dve", h4(gtri), bc(C(b["tri"])), cb(gcol), ALU.mult, gt, free, cn)
                m = MP.get()
                for h in range(4):
                    e = P.mm(hs(m.ap, h), hs(gtri, h), C(b["st"]), True, True, a, m.free, sig=h == 3)
                x = P.act(t["L"].ap, m.ap, ACT.Exp, e)
                m.done(x)
                m = MP.get()
                e = P.mm(m.ap, C(b["st"]), gtri, True, True, m.free)
                y = P.act(t["IT"].ap, m.ap, ACT.Exp, e)
                m.done(y)
                m = MP.get()
                P.mm(m.ap[:, 0:4], C(b["tri"]), gcol, True, True, m.free, sig=False)
                e = P.mm(m.ap[:, 4:8], C(b["st"]), gcol, True, True)
                b["cols"] = SM.get()
                z = P.act(b["cols"].ap, m.ap[:, 0:8], ACT.Exp, e, b["cols"].free)
                m.done(z)
                b["colt"] = z
                xs = P.tt("dve", h4(t["L"].ap), h4(t["L"].ap), bc(C(b["st"])), ALU.mult, x)
                ys = P.tt("dve", h4(t["IT"].ap), h4(t["IT"].ap), bc(C(b["tri"])), ALU.mult, y)
                m = MP.get()
                for h in range(4):
                    k = CQ[:, 4 + h, ck]
                    e = P.mm(hs(m.ap, h), k, k, True, True, m.free, qk, sig=h == 3)
                x = P.tt("dve", t["L"].ap, m.ap, t["L"].ap, ALU.mult, e, xs)
                m.done(x)
                x = P.tt("dve", h4(t["L"].ap), h4(t["L"].ap), cb(bcol), ALU.mult, x, bt)
                m = MP.get()
                for h in range(4):
                    e = P.mm(hs(m.ap, h), CQ[:, 4 + h, ck], CQ[:, h, ck], True, True, m.free, sig=h == 3)
                y = P.tt("dve", t["IT"].ap, m.ap, t["IT"].ap, ALU.mult, e, ys)
                m.done(y)
                b["it"] = y
                m = MP.get()
                for h in range(4):
                    e = P.tr(hs(m.ap, h), hs(t["L"].ap, h), ident, x, m.free, sig=h == 3)
                y = P.act(t["UU"].ap, m.ap, ACT.Copy, e)
                m.done(y)
                b["uu"] = y
                p = P.tt("dve", h4(t["T"].ap), h4(t["L"].ap), bc(C(b["lm"] + "0")), ALU.mult, x)
                p = P.tt("dve", h4(t["T"].ap), bc(ident), h4(t["T"].ap), ALU.subtract, p)
                w = P.tt("dve", h4(t["P"].ap), h4(t["UU"].ap), bc(C(b["um"] + "0")), ALU.mult, y)
                w = P.tt("dve", h4(t["P"].ap), bc(ident), h4(t["P"].ap), ALU.subtract, w)
                b["T"], b["P"] = p, w
                b["vb"] = P.tt("dve", h4(t["VB"].ap), h4(VT[:, i, :]), cb(bcol), ALU.mult, kv, free)
            for lv in range(1, 7):
                for b in B:
                    t = b["t"]
                    ul_ = P.tt("pool", h4(t["UL"].ap), h4(t["UU"].ap), bc(C(f"{b['um']}{lv}")), ALU.mult,
                               b["uu"], b.get("y"))
                    m = MP.get()
                    for h in range(4):
                        e = P.mm(hs(m.ap, h), hs(t["UL"].ap, h), hs(t["T"].ap, h), True, True, ul_, b["T"], m.free,
                                 sig=h == 3)
                    b["y"] = e
                    y = P.act(t["Y"].ap, m.ap, ACT.Copy, e, b.get("z"))
                    m.done(y)
                    b["yt"] = y
                for b in B:
                    t, y = b["t"], b["yt"]
                    if lv < 6:
                        m = MP.get()
                        for h in range(4):
                            e = P.mm(hs(m.ap, h), hs(t["P"].ap, h), hs(t["Y"].ap, h), True, True, y, b["P"], m.free,
                                     sig=h == 3)
                        b["T"] = P.tt("dve", t["T"].ap, t["T"].ap, m.ap, ALU.subtract, e)
                        m.done(b["T"])
                    m = MP.get()
                    for h in range(4):
                        e = P.mm(hs(m.ap, h), hs(t["Y"].ap, h), hs(t["P"].ap, h), True, True, y, b["P"], m.free,
                                 sig=h == 3)
                    b["z"] = e
                    b["P"] = P.tt("dve", t["P"].ap, t["P"].ap, m.ap, ALU.subtract, e)
                    m.done(b["P"])
                ada(8)
            for b in B:
                d, i, t = b["d"], b["i"], b["t"]
                tap(f"P{d}{i}", t["P"].ap, b["P"])
                ck = slice(128 * i, 128 * i + 128)
                bcol = BETA[:, i, 4 * d:4 * d + 4]
                if order == 1:
                    c = P.tt("dve", h4(t["KD"].ap), h4(KT[:, i, :]), cb(bcol), ALU.mult, kv, b.get("vbx"), t["KD"].free)
                    c = P.tt("dve", h4(t["KD"].ap), h4(t["KD"].ap), cb(b["cols"].ap[:, 0:4]), ALU.mult, c, b["colt"])
                    b["cols"].done(c)
                    m = MP.get()
                    for h in range(4):
                        e = P.mm(hs(m.ap, h), hs(t["KD"].ap, h), hs(t["P"].ap, h), True, True, c, b["P"], m.free,
                                 sig=h == 3)
                    wt = P.act(t["WT"].ap, m.ap, ACT.Copy, e, scale=-1.0)
                    m.done(wt)
                    m = MP.get()
                    e = P.mm(m.ap, ones, t["gt"].ap, True, True, m.free)
                    q = P.act(t["QG"].ap, m.ap, ACT.Exp, e)
                    m.done(q)
                    q = P.tt("dve", h4(t["QG"].ap), h4(t["QG"].ap), CQ[:, 0:4, ck], ALU.mult, q)
                    st_ = state[d]
                m = MP.get()
                for h in range(4):
                    e = P.mm(hs(m.ap, h), hs(t["P"].ap, h), hs(t["VB"].ap, h), True, order == 0, b["P"], b["vb"], m.free,
                             sig=order == 0 and h == 3)
                    if order == 1:
                        e = P.mm(hs(m.ap, h), hs(t["WT"].ap, h), hs(t["S"].ap, h), False, True, wt, st_)
                vn = P.act(t["VN"].ap, m.ap, ACT.Copy, e)
                m.done(vn)
                if order == 0:
                    c = P.tt("dve", h4(t["KD"].ap), h4(KT[:, i, :]), cb(b["cols"].ap[:, 4:8]), ALU.mult, kv, b["colt"])
                    b["cols"].done(c)
                    m = MP.get()
                    for h in range(4):
                        e = P.mm(hs(m.ap, h), hs(t["KD"].ap, h), hs(t["VN"].ap, h), True, True, c, vn, m.free,
                                 sig=h == 3)
                    state[d] = P.copy("dve", t["S"].ap, m.ap, e)
                    m.done(state[d])
                m = MP.get()
                for h in range(4):
                    e = P.mm(hs(m.ap, h), hs(t["VN"].ap, h), hs(t["IT"].ap, h), True, order == 0, vn, b["it"], m.free)
                    if order == 1:
                        e = P.mm(hs(m.ap, h), hs(t["S"].ap, h), hs(t["QG"].ap, h), False, True, q, st_)
                if i not in first_o:
                    first_o[i] = P.copy("dve", OS[:, :, ck], h4(m.ap), e)
                else:
                    first_o[i] = P.tt("dve", OS[:, :, ck], OS[:, :, ck], h4(m.ap), ALU.add, e, first_o[i])
                m.done(first_o[i])
                for n_, v in t.items():
                    v.done(every("pe", "act", "dve"))
        tap("os", OS[:], first_o[0], first_o[1])
        for c in range(2):
            v = OS[:, 2 * c:2 * c + 2, :]
            s, m, r = TM.get(), MP.get(), RBR.get()
            sq = P.act(s.ap, v, ACT.Square, s.free, first_o[0], first_o[1])
            mt = P.mm(m.ap, ones, s.ap, True, True, sq, m.free)
            e, f = rsqrt(r.ap, m.ap, 1.0 / 128, mt, r.free)
            m.done(f)
            x2 = s.ap.rearrange("p (a b) -> p a b", a=2)
            u = P.stt(x2, v, col("gdn_norm_w"), r.ap.rearrange("p (a b) -> p a b", a=2), ALU.mult, ALU.mult, e, mt)
            r.done(u)
            u = P.tt("dve", x2, x2, ZG[:, 2 * c:2 * c + 2, :], ALU.mult, u, zt)
            _, w = cut(UH[:, 2 * c:2 * c + 2, 0:256], UL[:, 2 * c:2 * c + 2, 0:256], x2, u, uq)
            s.done(w)
        ada(144)
        tap("ugdn", UH[:, 0:4, 0:256].bitcast(F32), every("act"))


def ada_maker(P, W, MP, MOD, col, TM, tile, old, cload):
    CS = tile("CSIL", [128, 8, 2])
    st = {"n": 0, "tok": None, "m": None}

    def ada(count):
        if st["tok"] is None:
            st["tok"] = P.act(CS[:], col("cc", 0, 16).rearrange("p (k v) -> p k v", k=8), ACT.Silu, old, cload)
        while count > 0 and st["n"] < 144:
            l, m = divmod(st["n"], 72)
            if m % 8 == 0:
                st["m"] = MP.get()
            b = st["m"]
            o = b.ap[:, 2 * (m % 8):2 * (m % 8) + 2]
            for k in range(8):
                w, _, rdy, last = W.next((f"ada{l}", k, 128 * m, 128))
                t = P.mm(o, w, CS[:, k, :], k == 0, k == 7, rdy, st["tok"], b.free)
            W.release(t)
            if m % 8 == 7:
                bias = col(f"b_ada{l}", m - 7, 8).unsqueeze(2).broadcast_to([128, 8, 2])
                u = P.tt("dve", MOD[:, l, m - 7:m + 1, :], b.ap[:, 0:16].rearrange("p (k v) -> p k v", k=8), bias,
                         ALU.add, t, cload)
                b.done(u)
            st["n"] += 1
            count -= 1
    return ada


def block2(P, nc, stack, sb, W, gemm, cut, rsqrt, tap, every, col, TM, MP, GP, SM, RBR, SSR, X, UH, UL, uh, ul,
           consts2, ident, ones, MOD, DER, Stat, ffn, ada_to_u, add_to_x, xt, out):
    old = every("pe", "act", "dve", "pool")
    der = []
    for l in range(2):
        for i, g in enumerate(("g_ffn1", "g_mix", "g_ffn2")):
            sc = MOD[:, l, 24 * i + 8:24 * i + 16, :]
            gv = col(f"{g}{l}", 0, 8).unsqueeze(2).broadcast_to([128, 8, 2])
            a = P.ts("dve", DER[:, l, i], sc, 1.0, None, ALU.add, None, old)
            der.append(P.tt("dve", DER[:, l, i], DER[:, l, i], gv, ALU.mult, a))
            f = 1.0 if i == 1 else 0.5
            der.append(P.ts("dve", DER[:, l, 3 + i], MOD[:, l, 24 * i + 16:24 * i + 24, :], f, None, ALU.mult, None))
    A = lambda l, i: (lambda k, s: DER[:, l, i, k, s:s + 1])
    B = lambda l, i: (lambda k, s: MOD[:, l, 24 * i + k, s:s + 1])
    gate = lambda l, i: (lambda k, s: DER[:, l, 3 + i, k, s:s + 1])
    tap("mod", MOD[:], der)

    stat = Stat(512)
    for k in range(8):
        stat.add(X[:, k, :], xt, der)
    for l in range(2):
        n = 512 if l == 0 else 256
        r, rt = stat.rsqrt(D)
        ready = ada_to_u(r, rt, A(l, 0), B(l, 0), 512, every("pe"), der)
        stat, xt = ffn(f"f1{l}", 512, ready, gate(l, 0), f"c{l}")
        tap(f"y1{l}", X[:], xt)
        r, rt = stat.rsqrt(D)
        ready = ada_to_u(r, rt, A(l, 1), B(l, 1), 512, every("pe"))
        mix2(P, nc, stack, sb, W, gemm, cut, rsqrt, tap, every, col, TM, MP, GP, SM, RBR, X, UH, UL, uh, ul,
             consts2, ident, ones, ready, l, n, Stat, add_to_x, gate)
        stat = mix2.stat
        r, rt = stat.rsqrt(D)
        ready = ada_to_u(r, rt, A(l, 2), B(l, 2), n, every("pe"))
        stat, xt = ffn(f"f2{l}", n, ready, gate(l, 2), f"d{l}")
        tap(f"y3{l}", X[:], xt)
    r, rt = stat.rsqrt(D)
    sq = every("act")
    for k in range(8):
        a = P.stt(X[:, k, 0:256], X[:, k, 0:256], col("g_final", k), r.ap[:, 0:256], ALU.mult, ALU.mult, rt, sq, xt)
        o = P.dma(out[:, 256 * k:256 * k + 256], X[:, k, 0:256], "out", a)
    P.wait("sp", [o])


def mix2(P, nc, stack, sb, W, gemm, cut, rsqrt, tap, every, col, TM, MP, GP, SM, RBR, X, UH, UL, uh, ul,
         consts2, ident, ones, ready, l, n, Stat, add_to_x, gate):
    ns = n // 256
    L = str(l)
    with ExitStack() as st:
        def tile(name, shape, dt=F32, s=None):
            return sb(name + L, shape, dt, s or st)

        old = every("pe", "act", "dve", "pool")
        CVH, CVL = tile("CVH", [128, 3, n], F32R), tile("CVL", [128, 3, n], F32R)
        FOH, FOL = tile("FOH", [128, 4, n], F32R), tile("FOL", [128, 4, n], F32R)
        ATH, ATL = tile("ATH", [128, 4, n], F32R), tile("ATL", [128, 4, n], F32R)
        win = lambda c: [(f"win{l}", k, c, 128) for k in range(8)]
        s3 = ExitStack()
        with s3:
            K2 = tile("K2", [128, 640], F32, s3)
            k2 = P.dma(K2[:], consts2[:, 0:640], "k2" + L, old, e="pool")
            ROT, COS, SIN = K2[0:96, 0:96], K2[0:96, 128:384], K2[0:96, 384:640]
            with ExitStack() as s4:
                K3 = tile("K3", [128, 1280], F32, s4)
                k3 = P.dma(K3[:], consts2[:, 640:1920], "k3" + L, old, e="pool")
                CS = K3[:, 0:256]
                CT = K3[:, 256:768].rearrange("p (i t) -> p i t", i=2)
                ST = K3[:, 768:1280].rearrange("p (i t) -> p i t", i=2)
                AF = tile("AF", [128, 2, 2, 256], F32, s4)
                AR = Ring([AF[:, 0], AF[:, 1]])
                for j in range(4):
                    g, ps, t = gemm(win(1440 + 128 * j), uh(n), ul(n), 128, n, each=ready)
                    z = TM.get()
                    zt = P.act(z.ap[:, 0:n], ps, ACT.Copy, t, z.free)
                    g.done(zt)
                    fm = MP.get()
                    for s in range(ns):
                        m = MP.get()
                        for i in range(2):
                            c = 256 * s + 128 * i
                            e = P.mm(m.ap[:, 256 * i:256 * i + 256], z.ap[:, c:c + 128], CS, True, True, zt, k3, m.free)
                        a = AR.get()
                        at = P.copy("dve", a.ap, m.ap.rearrange("p (i c) -> p i c", i=2), e, a.free, old)
                        m.done(at)
                        o = fm.ap[:, 256 * s:256 * s + 256]
                        for i in range(2):
                            P.mm(o, a.ap[:, i, 0:128], CT[:, i, :], i == 0, False, at, fm.free)
                            e2 = P.mm(o, a.ap[:, i, 128:256], ST[:, i, :], False, i == 1)
                        a.done(e2)
                    z.done(e)
                    _, ft = cut(FOH[:, j, :], FOL[:, j, :], fm.ap[:, 0:n], e2, old)
                    fm.done(ft)
                tap("fo" + L, FOH[:].bitcast(F32), every("act"))
            fdone = every("pe", "act", "dve")
            with ExitStack() as s4:
                VC = tile("VC", [128, 3, ns, 286], F32, s4)
                AC = tile("AC", [128, 3, ns, 256], F32, s4)
                pads = [P.do("pool", lambda g: g.memset(VC[:, :, :, 0:15], 0.0), fdone),
                        P.do("pool", lambda g: g.memset(VC[:, :, :, 271:286], 0.0))]
                sv = lambda ap: ap.rearrange("p (s t) -> p s t", s=ns)
                acc = []
                for c in range(3):
                    g, ps, t = gemm(win(384 + 128 * c), uh(n), ul(n), 128, n)
                    s = TM.get()
                    a = P.act(s.ap[:, 0:n], ps, ACT.Sigmoid, t, s.free)
                    g.done(a)
                    g, ps, t = gemm(win(128 * c), uh(n), ul(n), 128, n)
                    b = P.tt("dve", VC[:, c, :, 15:271], sv(s.ap[:, 0:n]), sv(ps), ALU.mult, a, t, fdone)
                    g.done(b)
                    s.done(b)
                    acc.append(P.ts("dve", AC[:, c], VC[:, c, :, 0:256], col(f"w_dw{l}", 31 * c), col(f"b_dw{l}", c),
                                    ALU.mult, ALU.add, b, pads))
                for i in range(1, 31):
                    for c in range(3):
                        acc[c] = P.stt(AC[:, c], VC[:, c, :, i:i + 256], col(f"w_dw{l}", 31 * c + i), AC[:, c],
                                       ALU.mult, ALU.add, acc[c])
                fl = lambda ap: ap.rearrange("p s t -> p (s t)")
                s, m = TM.get(), MP.get()
                a = P.tt("dve", s.ap[:, 0:n], fl(AC[:, 0]), fl(AC[:, 1]), ALU.add, acc, s.free)
                a = P.tt("dve", s.ap[:, 0:n], s.ap[:, 0:n], fl(AC[:, 2]), ALU.add, a)
                e = P.mm(m.ap[:, 0:n], ones, s.ap[:, 0:n], True, True, a, m.free)
                s.done(e)
                stat = Stat(n)
                for c in range(3):
                    acc[c] = P.stt(fl(AC[:, c]), m.ap[:, 0:n], -1.0 / 384, fl(AC[:, c]), ALU.mult, ALU.add, e)
                    stat.add(fl(AC[:, c]), acc[c])
                m.done(acc[2])
                sq = every("act")
                r, rt = stat.rsqrt(384)
                for c in range(3):
                    a = P.stt(fl(AC[:, c]), fl(AC[:, c]), col(f"ln_g{l}", c), r.ap[:, 0:n], ALU.mult, ALU.mult, rt,
                              sq, acc[c])
                    b = P.act(fl(AC[:, c]), fl(AC[:, c]), ACT.Silu, a, bias=col(f"ln_b{l}", c))
                    _, d = cut(CVH[:, c, :], CVL[:, c, :], fl(AC[:, c]), b, old)
                r.done(a)
                tap("cv" + L, CVH[:].bitcast(F32), every("act"))
            cdone = every("pe", "act", "dve", "pool")
            CQH, CQL = tile("CQH", [128, 3, n], F32R, s3), tile("CQL", [128, 3, n], F32R, s3)
            CKH, CKL = tile("CKH", [128, 2, 512], F32R, s3), tile("CKL", [128, 2, 512], F32R, s3)
            KR = tile("KR", [96, 512], F32, s3)
            V = tile("V", [128, 4, 512], F32, s3)
            QK = tile("QK", [96, 4, 512], F32, s3)
            QR, KRG = Ring([QK[:, 0], QK[:, 1]]), Ring([QK[:, 2], QK[:, 3]])
            PTT = tile("PTT", [128, 2, 4, 256], F32, s3)
            PTR = Ring([PTT[:, 0], PTT[:, 1]])

            def latent(nt, base, name, gname, hi, lo, nn):
                stat, toks = Stat(nn), []
                for j in range(nt):
                    g, ps, t = gemm(win(base + 128 * j), uh(nn), ul(nn), 128, nn)
                    sq = stat.add(ps, t)
                    gc = col(f"{gname}{l}", j)
                    a = P.act(hi[:, j, :], ps, ACT.Copy, cdone, t, scale=gc)
                    b = P.stt(lo[:, j, :], ps, gc, hi[:, j, :].bitcast(F32), ALU.mult, ALU.subtract, a)
                    g.done(sq, b)
                    toks.append(b)
                return stat.rsqrt(128 * nt) + (toks,)

            rq, rqt, cqt = latent(3, 768, "cq", "g_q", CQH, CQL, n)
            rk, rkt, ckt = latent(2, 1152, "ckv", "g_kv", CKH, CKL, 512)
            g, ps, t = gemm([(f"wkr{l}", k, 0, 96) for k in range(8)], uh(512), ul(512), 96, 512)
            a = P.copy("dve", KR[:], ps, t, cdone)
            g.done(a)

            def rope(q, tok):
                m, s = MP.get(), TM.get()
                e = P.mm(m.ap[0:96, 0:256], ROT, q[:, 0:256], True, True, tok, m.free, k2)
                a = P.tt("dve", s.ap[0:96, 0:256], m.ap[0:96, 0:256], SIN, ALU.mult, e, s.free, k2)
                m.done(a)
                b = P.tt("dve", q[:, 0:256], q[:, 0:256], COS, ALU.mult, e)
                c = P.tt("dve", q[:, 0:256], q[:, 0:256], s.ap[0:96, 0:256], ALU.add, a, b)
                s.done(c)
                return c

            kr = rope(KR, a)
            m, sm = MP.get(), SM.get()
            for i in range(4):
                e = P.tr(m.ap[:, 128 * i:128 * i + 128], rk.ap[:, 128 * i:128 * i + 128], ident, rkt, m.free)
            rc = P.copy("dve", sm.ap[:, 0:4], m.ap.rearrange("p (i c) -> p i c", i=4)[:, :, 0:1].rearrange(
                "p i c -> p (i c)"), e, sm.free)
            m.done(rc)
            pc = [W.next((f"wv{l}", k, 0, 512)) for k in range(2)]
            vt = []
            for i in range(4):
                g = GP.get()
                x = slice(128 * i, 128 * i + 128)
                for k in range(2):
                    wh, wl, rdy, _ = pc[k]
                    P.mm(g.ap, CKH[:, k, x], wh, k == 0, False, rdy, ckt, g.free, sig=False)
                    P.mm(g.ap, CKH[:, k, x], wl, False, False, sig=False)
                    t = P.mm(g.ap, CKL[:, k, x], wh, False, k == 1)
                vt.append(P.act(V[:, i, :], g.ap, ACT.Copy, t, rc, cdone, scale=sm.ap[:, i:i + 1]))
                g.done(vt[-1])
            W.release(t)
            sm.done(vt[-1])
            SC = 96 ** -0.5
            for c in range(4):
                o = MP.get()
                for h in (2 * c, 2 * c + 1):
                    b0 = 64 * (h % 2)
                    g, ps, t = gemm([(f"wuq{l}", k, 96 * h, 96) for k in range(3)], lambda k: CQH[:, k, :],
                                    lambda k: CQL[:, k, :], 96, n, cqt)
                    q = QR.get()
                    a = P.tt("dve", q.ap[:, 0:n], ps, rq.ap[0:96, 0:n], ALU.mult, t, rqt, q.free, cdone)
                    g.done(a)
                    qt = rope(q.ap, a)
                    g, ps, t = gemm([(f"wkn{l}", k, 96 * h, 96) for k in range(2)], lambda k: CKH[:, k, :],
                                    lambda k: CKL[:, k, :], 96, 512, ckt)
                    kk = KRG.get()
                    a = P.tt("dve", kk.ap[0:64, :], ps[0:64, :], rk.ap[0:64, :], ALU.mult, t, rkt, kk.free, cdone)
                    g.done(a)
                    kt = P.copy("pool", kk.ap[64:96, :], KR[64:96, :], kk.free, kr, cdone)
                    for s in range(ns):
                        k0, nk = (0, 512) if s == 0 else (256, 256)
                        pt = PTR.get()
                        for i in range(2):
                            m, sm, p = MP.get(), SM.get(), TM.get()
                            qs = 256 * s + 128 * i
                            e = P.mm(m.ap[:, 0:nk], q.ap[:, qs:qs + 128], kk.ap[:, k0:k0 + nk], True, True, qt, a, kt,
                                     m.free)
                            mx = P.do("dve", lambda v, sm=sm, m=m, nk=nk: v.tensor_reduce(
                                sm.ap[:, 0:1], m.ap[:, 0:nk], AX, ALU.max), e, sm.free)
                            mx = P.ts("dve", sm.ap[:, 1:2], sm.ap[:, 0:1], -SC, None, ALU.mult, None, mx)
                            ex = P.act(p.ap[:, 0:nk], m.ap[:, 0:nk], ACT.Exp, mx, p.free, scale=SC,
                                       bias=sm.ap[:, 1:2], accum_out=sm.ap[:, 2:3])
                            m.done(ex)
                            rcp = P.recip(sm.ap[:, 3:4], sm.ap[:, 2:3], ex)
                            nm = P.ts("dve", p.ap[:, 0:nk], p.ap[:, 0:nk], sm.ap[:, 3:4], None, ALU.mult, None, rcp)
                            sm.done(nm)
                            m = MP.get()
                            for kc in range(nk // 128):
                                e = P.tr(m.ap[:, 128 * kc:128 * kc + 128], p.ap[:, 128 * kc:128 * kc + 128], ident, nm,
                                         m.free)
                            p.done(e)
                            ev = P.act(pt.ap[:, 0:nk // 128, 128 * i:128 * i + 128],
                                       m.ap[:, 0:nk].rearrange("p (a b) -> p a b", b=128), ACT.Copy, e, pt.free, cdone)
                            m.done(ev)
                        for kc in range(nk // 128):
                            e = P.mm(o.ap[b0:b0 + 64, 256 * s:256 * s + 256], V[:, k0 // 128 + kc, 64 * h:64 * h + 64],
                                     pt.ap[:, kc, :], kc == 0, kc == nk // 128 - 1, ev, vt, o.free)
                        pt.done(e)
                    q.done(e)
                    kk.done(e)
                _, u = cut(ATH[:, c, :], ATL[:, c, :], o.ap[:, 0:n], e, old)
                o.done(u)
            rq.done(u)
            rk.done(u)
            tap("at" + L, ATH[:].bitcast(F32), every("act"))
        adone = every("pe", "act", "dve", "pool")
        YH, YL = tile("YH", [128, 8, n], F32R), tile("YL", [128, 8, n], F32R)
        yt = []
        for m in range(8):
            sig = []
            for b in range(3):
                g, ps, t = gemm([(f"wbg{l}", k, 1024 * b + 128 * m, 128) for k in range(8)], uh(n), ul(n), 128, n)
                s = TM.get()
                a = P.act(s.ap[:, 0:n], ps, ACT.Sigmoid, t, s.free, bias=col(f"b_bg{l}", 8 * b + m))
                g.done(a)
                sig.append((s, a))
            v = [s.ap[:, 0:n] for s, _ in sig]
            g, ps, t = gemm([(f"wpw{l}", k, 128 * m, 128) for k in range(3)], lambda k: CVH[:, k, :],
                            lambda k: CVL[:, k, :], 128, n, adone)
            a0 = P.stt(v[0], ps, col(f"b_pw{l}", m), v[0], ALU.add, ALU.mult, t, sig[0][1])
            g.done(a0)
            g, ps, t = gemm([(f"wo{l}", k, 128 * m, 128) for k in range(4)], lambda k: ATH[:, k, :],
                            lambda k: ATL[:, k, :], 128, n)
            a1 = P.tt("dve", v[1], ps, v[1], ALU.mult, t, sig[1][1])
            g.done(a1)
            g, ps, t = gemm([(f"wf{l}", k, 128 * m, 128) for k in range(4)], lambda k: FOH[:, k, :],
                            lambda k: FOL[:, k, :], 128, n)
            a2 = P.stt(v[2], ps, col(f"b_f{l}", m), v[2], ALU.add, ALU.mult, t, sig[2][1])
            g.done(a2)
            a0 = P.tt("dve", v[0], v[0], v[1], ALU.add, a0, a1)
            a0 = P.tt("dve", v[0], v[0], v[2], ALU.add, a0, a2)
            _, u = cut(YH[:, m, :], YL[:, m, :], v[0], a0, adone)
            for s, _ in sig:
                s.done(u)
            yt.append(u)
        stat = Stat(n)
        for m in range(8):
            g, ps, t = gemm([(f"wout{l}", k, 128 * m, 128) for k in range(8)], lambda k: YH[:, k, :],
                            lambda k: YL[:, k, :], 128, n, each=yt)
            a = add_to_x(m, ps, n, gate(l, 1), t)
            g.done(a)
            stat.add(X[:, m, 0:n], a)
        mix2.stat = stat
        tap("y2" + L, X[:], a)


def host_arrays(inputs):
    a = {k: np.asarray(v, dtype=np.asarray(v).dtype) for k, v in inputs.items()}
    wt = {"f1g": a["ffn1_w_gate"][0], "f1u": a["ffn1_w_up"][0], "f1d": a["ffn1_w_down"][0],
          "f2g": a["ffn2_w_gate"][0], "f2u": a["ffn2_w_up"][0], "f2d": a["ffn2_w_down"][0],
          "win": a["w_in"][0], "wout": a["w_out"][0]}
    for l in range(2):
        for f in (1, 2):
            wt[f"f{f}{l}g"], wt[f"f{f}{l}u"], wt[f"f{f}{l}d"] = (
                a[f"w1_ffn{f}_2"][l], a[f"w3_ffn{f}_2"][l], a[f"w2_ffn{f}_2"][l])
        wt[f"ada{l}"], wt[f"win{l}"], wt[f"wpw{l}"] = a["w_ada_2"][l], a["w_in_2"][l], a["w_pw_conv_2"][l]
        wt[f"wuq{l}"], wt[f"wo{l}"], wt[f"wf{l}"] = a["w_uq_2"][l], a["w_o_mla_2"][l], a["w_fourier_2"][l]
        wt[f"wbg{l}"], wt[f"wout{l}"] = a["w_bgate_2"][l], a["w_out_2"][l]
        wt[f"wkr{l}"] = np.concatenate([np.zeros((1024, 64), np.float32), a["w_in_2"][l][:, 1408:1440]], axis=1)
        kv = a["w_ukv_2"][l].reshape(256, 8, 128)
        wt[f"wkn{l}"] = np.concatenate([kv[:, :, :64], np.zeros((256, 8, 32), np.float32)], axis=2).reshape(256, 768)
        wt[f"wv{l}"] = kv[:, :, 64:].reshape(256, 512)
    units, total = plan()
    stream = np.empty(total, np.float32)
    for at, n, ps in units:
        u = stream[at:at + 128 * n].reshape(128, n)
        for (name, k, m0, m), c in ps:
            u[:, c:c + m] = wt[name][128 * k:128 * k + 128, m0:m0 + m]

    def fm(v):
        v = np.asarray(v)
        return v.reshape(-1, 128).T

    c1 = {"ffn1_norm": fm(a["ffn1_norm"][0]), "mix_norm": fm(a["mix_norm"][0]), "ffn2_norm": fm(a["ffn2_norm"][0]),
          "final_norm": fm(a["final_norm"][0]),
          "conv_w": a["conv_w"][0].reshape(12, 128, 5).transpose(1, 0, 2).reshape(128, 60),
          "gdn_norm_w": fm(a["gdn_norm_w"][0]), "q_norm_w": np.tile(a["q_norm_w"][0], 2)[:, None],
          "k_norm_w": np.tile(a["k_norm_w"][0], 2)[:, None],
          "dt_bias": np.broadcast_to(a["dt_bias"][0].reshape(1, 8), (128, 8)),
          "a_log": np.broadcast_to(a["a_log"][0].reshape(1, 8), (128, 8)),
          "g_final": fm(a["g_final_2"]),
          "cc": np.stack([fm(a["c_2"][0]), fm(a["c_ctx_2"])], axis=2).reshape(128, 16)}
    for l in range(2):
        for name, src in (("b_ada", "b_ada_2"), ("g_ffn1", "g_ffn1_2"), ("g_mix", "g_mix_2"), ("g_ffn2", "g_ffn2_2"),
                          ("b_dw", "b_dw_2"), ("ln_g", "ln_g_conv_2"), ("ln_b", "ln_b_conv_2"), ("b_pw", "b_pw_conv_2"),
                          ("g_q", "g_qnorm_2"), ("g_kv", "g_kvnorm_2"), ("b_f", "b_fourier_2"), ("b_bg", "b_bgate_2")):
            c1[f"{name}{l}"] = fm(a[src][l])
        c1[f"w_dw{l}"] = a["w_dw_2"][l].T.reshape(3, 128, 31).transpose(1, 0, 2).reshape(128, 93)
    COL, ncol = columns()
    cols = np.empty((128, ncol), np.float32)
    for name, (at, n) in COL.items():
        cols[:, at:at + n] = c1[name]
    strip = a["rel_bias"][t5_buckets()]
    idx = np.clip(np.arange(384)[None, :] - 128 - np.arange(128)[:, None], -255, 255) + 255
    bias = np.ascontiguousarray(strip[idx].transpose(0, 2, 1))
    xt = a["x"][0].T.reshape(8, 128, 256).transpose(1, 0, 2)
    ct = a["ctx_2"][0].T.reshape(8, 128, 256).transpose(1, 0, 2)
    xin = np.ascontiguousarray(np.concatenate([xt, ct], axis=2).reshape(128, 4096))
    return {"in_w": stream, "in_cols": cols, "in_bias": bias, "in_x": xin,
            "in_consts": np.concatenate(list(const_blocks().values()), axis=1),
            "in_consts2": np.concatenate(list(const_blocks2().values()), axis=1)}


def kernel(**inputs):
    import concourse.bacc as bacc
    from concourse.bass_utils import run_bass_kernel_spmd

    arrays = host_arrays(inputs)
    nc = bacc.Bacc("TRN2", target_bir_lowering=False, num_devices=1)
    ap = {n: nc.dram_tensor(n, v.shape, F32, kind="ExternalInput").ap() for n, v in arrays.items()}
    out = nc.dram_tensor("out_x", (128, 2048), F32, kind="ExternalOutput").ap()
    build(nc, ap["in_w"], ap["in_cols"], ap["in_consts"], ap["in_consts2"], ap["in_bias"], ap["in_x"], out)
    r = run_bass_kernel_spmd(nc, [arrays], core_ids=[0])
    y = r.results[0]["out_x"].reshape(128, 8, 256).transpose(2, 1, 0).reshape(1, 256, 1024)
    return np.ascontiguousarray(y)
```

```python
import math
from contextlib import ExitStack

import numpy as np

import concourse.bass as bass
from concourse import mybir

F32 = mybir.dt.float32
F32R = mybir.dt.float32r
ALU = mybir.AluOpType
ACT = mybir.ActivationFunctionType
AX = mybir.AxisListType.X

D, T, FF = 1024, 256, 2816
NF = FF // 128
EPS = 1e-6
UC = 1024
NR, NH, AHEAD = 4, 3, 2

COLS1 = [("ffn1_norm", 8), ("mix_norm", 8), ("ffn2_norm", 8), ("final_norm", 8), ("conv_w", 60),
         ("gdn_norm_w", 1), ("q_norm_w", 1), ("k_norm_w", 1), ("dt_bias", 8), ("a_log", 8)]
COLS2 = [("b_ada", 72), ("g_ffn1", 8), ("g_mix", 8), ("g_ffn2", 8), ("w_dw", 93), ("b_dw", 3), ("ln_g", 3),
         ("ln_b", 3), ("b_pw", 8), ("g_q", 3), ("g_kv", 2), ("b_f", 8), ("b_bg", 24)]


def columns():
    at, out = 0, {}
    for name, n in COLS1 + [(f"{name}{l}", n) for l in range(2) for name, n in COLS2] + [("g_final", 8), ("cc", 16)]:
        out[name] = (at, n)
        at += n
    return out, at


def pieces():
    def ffn(p):
        for j in range(NF):
            yield [(p + "g", k, 128 * j, 128) for k in range(8)]
            yield [(p + "u", k, 128 * j, 128) for k in range(8)]
        for m in range(8):
            yield [(p + "d", k, 128 * m, 128) for k in range(NF)]

    yield from ffn("f1")
    for j in range(12):
        yield [("win", k, 128 * j, 128) for k in range(8)]
    for j in range(12, 16):
        yield [("win", k, 128 * j, 128) for k in range(8)]
    yield [("win", k, 2048, 16) for k in range(8)]
    for j in range(12):
        yield [("win", k, 2064 + 128 * j, 128) for k in range(8)]
    for l in range(2):
        for m in range(18):
            yield [(f"ada{l}", k, 512 * m, 512) for k in range(8)]
    for m in range(8):
        yield [("wout", k, 128 * m, 128) for k in range(8)]
    yield from ffn("f2")
    for l in range(2):
        yield from ffn(f"f1{l}")
        for c in range(3):
            yield [(f"win{l}", k, 384 + 128 * c, 128) for k in range(8)]
            yield [(f"win{l}", k, 128 * c, 128) for k in range(8)]
        for j in range(5):
            yield [(f"win{l}", k, 768 + 128 * j, 128) for k in range(8)]
        yield [(f"wkr{l}", k, 0, 96) for k in range(8)]
        yield [(f"wv{l}", k, 0, 512) for k in range(2)]
        for h in range(8):
            yield [(f"wuq{l}", k, 96 * h, 96) for k in range(3)] + [(f"wkn{l}", k, 96 * h, 96) for k in range(2)]
        for j in range(4):
            yield [(f"win{l}", k, 1440 + 128 * j, 128) for k in range(8)]
        for m in range(8):
            yield [(f"wbg{l}", k, 128 * m, 128) for k in range(8)]
            yield [(f"wbg{l}", k, 1024 + 128 * m, 128) for k in range(8)]
            yield [(f"wbg{l}", k, 2048 + 128 * m, 128) for k in range(8)]
            yield [(f"wpw{l}", k, 128 * m, 128) for k in range(3)] + [(f"wo{l}", k, 128 * m, 128) for k in range(4)]
            yield [(f"wf{l}", k, 128 * m, 128) for k in range(4)]
        for m in range(8):
            yield [(f"wout{l}", k, 128 * m, 128) for k in range(8)]
        yield from ffn(f"f2{l}")


def plan():
    units, at = [], 0
    for group in pieces():
        unit, n = [], 0
        for p in group:
            if n + p[3] > UC:
                units.append((at, n, unit))
                at, unit, n = at + 128 * n, [], 0
            unit.append((p, n))
            n += p[3]
        units.append((at, n, unit))
        at += 128 * n
    return units, at


def const_blocks():
    p, f = np.arange(128)[:, None], np.arange(128)[None, :]
    out = {"ident": p == f, "ones": np.ones((128, 128)),
           "LE": p <= f, "GE": p >= f, "GT": p > f, "LT": p < f}
    for l in range(7):
        s = 1 << l
        low = ((p // (2 * s)) == (f // (2 * s))) & ((p // s) % 2 == 1) & ((f // s) % 2 == 0)
        out[f"ML{l}"], out[f"MU{l}"] = low, low.T
    x = np.arange(384)[None, :] - 128 - p
    n = (np.abs(x) <= 64).astype(np.float32) + (x % 4 == 0) + (x % 16 == 0)
    out["bd"] = (p // 64) == (f // 64)
    out["mult"] = n
    out["amask"] = np.where(n > 0, 0.0, -1e30)
    return {k: np.asarray(v, np.float32) for k, v in out.items()}


def const_blocks2():
    out = {}
    rot = np.zeros((128, 128))
    for a in range(2):
        for i in range(8):
            lo, hi = 64 + 16 * a + i, 64 + 16 * a + 8 + i
            rot[hi, lo] = -1.0
            rot[lo, hi] = 1.0
    out["rot"] = rot
    t = np.arange(T)
    inv = (1.0 / (np.float32(10000.0) ** (np.arange(8, dtype=np.float32) * np.float32(2.0) / np.float32(16)))).astype(np.float32)
    ar, ac = ((t // 64).astype(np.float32)[:, None] * inv), ((t % 64).astype(np.float32)[:, None] * inv)
    ang = np.concatenate([ar, ar, ac, ac], axis=1).astype(np.float32)
    cos, sin = np.zeros((128, T), np.float32), np.zeros((128, T), np.float32)
    cos[:64] = 1.0
    cos[64:96], sin[64:96] = np.cos(ang).T, np.sin(ang).T
    out["cos"], out["sin"] = cos, sin
    a = 2 * np.pi * np.outer(np.arange(128), np.arange(128)) / 128
    out["cs"] = np.concatenate([np.cos(a), np.sin(a)], axis=1)
    b = 2 * np.pi * np.outer(t, t) / T
    s = 1.0 / math.sqrt(T * 128)
    out["ct"] = (np.cos(b) * s).reshape(2, 128, T).transpose(1, 0, 2).reshape(128, 2 * T)
    out["st"] = (-np.sin(b) * s).reshape(2, 128, T).transpose(1, 0, 2).reshape(128, 2 * T)
    return {k: np.asarray(v, np.float32) for k, v in out.items()}


def t5_buckets():
    rel = np.arange(-255, 256)
    n = np.abs(rel)
    large = 8 + (np.log(np.maximum(n, 1) / 8) / math.log(1024 / 8) * 8).astype(np.int32)
    return (rel > 0).astype(np.int32) * 16 + np.where(n < 8, n, np.minimum(large, 15))


class Slot:

    def __init__(self, ap):
        self.ap, self.free, self.held = ap, [], False

    def done(self, *toks):
        self.free, self.held = list(toks), False


class Ring:
    def __init__(self, aps):
        self.slots, self.n = [Slot(a) for a in aps], 0

    def get(self):
        while self.slots[self.n % len(self.slots)].held:
            self.n += 1
            assert not all(s.held for s in self.slots)
        s = self.slots[self.n % len(self.slots)]
        self.n += 1
        s.held = True
        return s


def rounds(gens, width):
    gens, active = iter(gens), []
    while True:
        while len(active) < width:
            g = next(gens, None)
            if g is None:
                break
            active.append(g)
        if not active:
            return
        for g in list(active):
            if next(g, active) is active:
                active.remove(g)
        yield


def run(*gens, width=3):
    for _ in rounds(gens, width):
        pass


def beside(main, *others):
    run(main, *others, width=1 + len(others))


class Prog:

    def __init__(self, nc, stack):
        self.nc, self.stack = nc, stack
        self.q = {e: [] for e in ("pe", "act", "dve", "pool", "sp")}
        self.count = dict.fromkeys(self.q, 0)
        self.seen = {}
        self.sems = {}
        self.table = None
        for e in ("pe", "act", "dve", "pool"):
            self.sem(e)

    def sem(self, name):
        if name not in self.sems:
            self.sems[name] = self.stack.enter_context(self.nc.semaphore("s_" + name))
            self.count[name] = 0
        return name

    def wait(self, e, toks):
        for t in toks:
            if t is None:
                continue
            if isinstance(t, list):
                self.wait(e, t)
                continue
            name, value = t
            if self.seen.get((e, name), 0) < value:
                self.seen[e, name] = value
                self.q[e].append(lambda eng, s=self.sems[name], v=value: eng.wait_ge(s, v))

    def do(self, e, fn, *toks, sig=True):
        self.wait(e, toks)
        if sig:
            self.count[e] += 1
            self.q[e].append(lambda eng, s=self.sems[e]: fn(eng).then_inc(s, 1))
        else:
            self.q[e].append(fn)
        return (e, self.count[e])

    def dma(self, out, in_, name, *toks, e="sp"):
        self.wait(e, toks)
        self.sem(name)
        self.count[name] += 16
        self.q[e].append(lambda eng, s=self.sems[name]: eng.dma_start(out, in_).then_inc(s, 16))
        return (name, self.count[name])

    def act(self, out, in_, f, *toks, **kw):
        if f in (ACT.Exp, ACT.Ln, ACT.Silu, ACT.Sigmoid):
            table = "natural_log_exp_and_others" if f in (ACT.Exp, ACT.Ln) else f
            if table != self.table and table != f:
                self.q["act"].append(lambda eng: eng.preload_act_table_set(table))
            self.table = table
        return self.do("act", lambda g: g.activation(out, in_, f, **kw), *toks)

    def tt(self, e, out, a, b, op, *toks):
        return self.do(e, lambda g: g.tensor_tensor(out, a, b, op), *toks)

    def ts(self, e, out, a, s1, s2, op0, op1, *toks):
        if s2 is None:
            return self.do(e, lambda g: g.tensor_scalar(out, a, s1, None, op0), *toks)
        return self.do(e, lambda g: g.tensor_scalar(out, a, s1, s2, op0, op1), *toks)

    def stt(self, out, a, s, b, op0, op1, *toks):
        return self.do("dve", lambda g: g.scalar_tensor_tensor(out=out, in0=a, scalar=s, in1=b, op0=op0, op1=op1), *toks)

    def copy(self, e, out, in_, *toks):
        return self.do(e, lambda g: g.tensor_copy(out, in_), *toks)

    def ttr(self, out, a, b, init, op0, op1, acc, *toks):
        return self.do("dve", lambda g: g.tensor_tensor_reduce(out, a, b, 1.0, init, op0, op1, acc), *toks)

    def rmax(self, out, in_, *toks):
        return self.do("dve", lambda g: g.tensor_reduce(out, in_, AX, ALU.max), *toks)

    def recip(self, out, in_, *toks):
        return self.do("dve", lambda g: g.reciprocal(out, in_), *toks)

    def mm(self, out, w, x, start, stop, *toks, sig=None):
        return self.do("pe", lambda g: g.matmul(out, w, x, start=start, stop=stop), *toks,
                       sig=stop if sig is None else sig)

    def tr(self, out, in_, ident, *toks, sig=True):
        return self.do("pe", lambda g: g.transpose(out, in_, ident), *toks, sig=sig)

    def flush(self):
        nc, q = self.nc, self.q
        with nc.Block() as block:
            @block.sync
            def _(eng):
                for f in q["sp"]:
                    f(eng)

            @block.scalar
            def _(eng):
                for f in q["act"]:
                    f(eng)

            @block.vector
            def _(eng):
                for f in q["dve"]:
                    f(eng)

            @block.gpsimd
            def _(eng):
                for f in q["pool"]:
                    f(eng)

            @block.tensor
            def _(eng):
                for f in q["pe"]:
                    f(eng)


class Weights:

    def __init__(self, P, dram):
        self.P, self.dram = P, dram
        self.units, _ = plan()
        e = P.stack.enter_context
        self.raw = e(P.nc.sbuf_tensor("w_raw", [128, NR, UC], F32))
        self.hi = e(P.nc.sbuf_tensor("w_hi", [128, NH, UC], F32R))
        self.lo = e(P.nc.sbuf_tensor("w_lo", [128, NH, UC], F32R))
        self.loaded, self.raw_free, self.landed = 0, {}, {}
        self.nsplit, self.split_tok, self.pe_done = 0, {}, {}
        self.u, self.i = 0, 0
        for _ in range(NR):
            self.load()

    def load(self):
        u = self.loaded
        if u >= len(self.units):
            return
        at, n, _ = self.units[u]
        src = bass.AP(tensor=self.dram.tensor, offset=at, ap=[[n, 128], [1, n]])
        free = self.raw_free[u - NR] if u >= NR else None
        self.landed[u] = self.P.dma(self.raw[:, u % NR, 0:n], src, f"w{u % NR}", free)
        self.loaded += 1

    def split(self):
        u = self.nsplit
        if u >= len(self.units):
            return
        s, n = u % NH, self.units[u][1]
        raw, hi, lo = self.raw[:, u % NR, 0:n], self.hi[:, s, 0:n], self.lo[:, s, 0:n]
        reader = self.pe_done[u - NH] if u >= NH else None
        a = self.P.act(hi, raw, ACT.Copy, self.landed[u], reader)
        pool = self.units[u][2][0][0][0].startswith("ada") and u % 5 < 2
        b = self.P.tt("pool" if pool else "dve", lo, raw, hi.bitcast(F32), ALU.subtract, a)
        self.split_tok[u] = b
        self.raw_free[u] = b
        self.nsplit += 1
        self.load()

    def next(self, key):
        at, n, ps = self.units[self.u]
        p, c = ps[self.i]
        assert p == key, (p, key)
        u, m, last = self.u, p[3], self.i == len(ps) - 1
        if self.i == 0:
            while self.nsplit < min(u + AHEAD + 1, len(self.units)):
                self.split()
        out = (self.hi[:, u % NH, c:c + m], self.lo[:, u % NH, c:c + m], self.split_tok[u], last)
        self.i += 1
        if last:
            self.u, self.i, self.last = u + 1, 0, u
        return out

    def release(self, tok):
        self.pe_done[self.last] = tok


def build(nc, wstream, cols, consts, consts2, bias, xin, out, taps=None, stop=None):
    with ExitStack() as stack:
        P = Prog(nc, stack)
        program(P, nc, stack, wstream, cols, consts, consts2, bias, xin, out, taps or {}, stop)
        P.flush()


def program(P, nc, stack, wstream, cols, consts, consts2, bias, xin, out, taps, stop):
    ent = stack.enter_context

    def sb(name, shape, dt=F32, st=None):
        return (st or stack).enter_context(nc.sbuf_tensor(name, shape, dt))

    W = Weights(P, wstream)
    X = sb("X", [128, 8, 512])
    UH, UL = sb("UH", [128, 8, 512], F32R), sb("UL", [128, 8, 512], F32R)
    COL, ncol = columns()
    PC = sb("PC", [128, ncol])
    C1 = sb("C1", [128, 256])
    ident, ones = C1[:, 0:128], C1[:, 128:256]
    tmp = sb("TMP", [128, 7, 512])
    TM = Ring([tmp[:, i, :] for i in range(7)])
    ssb = sb("SSB", [128, 3, 512])
    SSR, RBR = Ring([ssb[:, 0, :]]), Ring([ssb[:, i, :] for i in (1, 2)])
    small = sb("SMALL", [128, 8, 8])
    SM = Ring([small[:, i, :] for i in range(8)])
    MOD = sb("MOD", [128, 2, 72, 2])
    MP = GP = Ring([ent(nc.psum_tensor(f"B{i}", [128, 512], F32))[:] for i in range(8)])

    def col(name, k=0, n=1):
        at, _ = COL[name]
        return PC[:, at + k:at + k + n]

    xload = P.dma(X[:], xin.rearrange("p (c t) -> p c t", c=8), "x")
    cload = P.dma(PC[:], cols, "cols")
    c1load = P.dma(C1[:], consts[:, 0:256], "c1")
    tapped = []

    def tap(name, ap, *toks):
        if name in taps:
            tapped.append(P.dma(taps[name], ap, "tap_" + name, *toks))
        if stop == name:
            P.wait("sp", tapped)
            P.flush()
            P.q = {e: [] for e in P.q}
            P.flush = lambda: None

    def every(*engines):
        return [(e, P.count[e]) for e in engines]

    def gemm(keys, xh, xl, m, n, *toks, each=None):
        g = GP.get()
        ps = g.ap[0:m, 0:n]
        for i, key in enumerate(keys):
            wh, wl, ready, last = W.next(key)
            first, end = i == 0, i == len(keys) - 1
            P.mm(ps, wh, xh(i), first, False, ready, *toks, g.free, each and each[i], sig=False)
            P.mm(ps, wh, xl(i), False, False, sig=False)
            t = P.mm(ps, wl, xh(i), False, end, sig=end or last)
            if last:
                W.release(t)
        return g, ps, t

    def cut(hi, lo, src, *toks):
        a = P.act(hi, src, ACT.Copy, *toks)
        b = P.tt("dve", lo, src, hi.bitcast(F32), ALU.subtract, a)
        return a, b

    class Stat:

        def __init__(self, n):
            self.s, self.n, self.tok = SSR.get(), n, None

        def add(self, ap, *toks):
            if self.tok is None:
                self.tok = P.act(self.s.ap[:, 0:self.n], ap, ACT.Square, self.s.free, *toks)
                return self.tok
            t = TM.get()
            a = P.act(t.ap[:, 0:self.n], ap, ACT.Square, t.free, *toks)
            self.tok = P.tt("dve", self.s.ap[:, 0:self.n], self.s.ap[:, 0:self.n], t.ap[:, 0:self.n], ALU.add,
                            a, self.tok)
            t.done(self.tok)
            return a

        def rsqrt(self, count, ring=RBR):
            m, r, n = MP.get(), ring.get(), self.n
            a = P.mm(m.ap[:, 0:n], ones, self.s.ap[:, 0:n], True, True, self.tok, m.free, c1load)
            self.s.done(a)
            b, m_free = rsqrt(r.ap[:, 0:n], m.ap[:, 0:n], 1.0 / count, a, r.free)
            m.done(m_free)
            return r, b

    def rsqrt(out_, ps, scale, *toks):
        a = P.act(out_, ps, ACT.Ln, *toks, scale=scale, bias=EPS)
        return P.act(out_, out_, ACT.Exp, a, scale=-0.5), a

    def norm_to_u(r, rtok, gcol, n, *toks):
        ready = []
        for k in range(8):
            t = TM.get()
            a = P.stt(t.ap[:, 0:n], X[:, k, 0:n], gcol(k), r.ap[:, 0:n], ALU.mult, ALU.mult, rtok, t.free, cload)
            b, c = cut(UH[:, k, 0:n], UL[:, k, 0:n], t.ap[:, 0:n], a, *toks)
            t.done(c)
            ready.append(c)
        r.done(a)
        return ready

    def ada_to_u(r, rtok, A, B, n, *toks):
        ready = []
        for k in range(8):
            t = TM.get()
            for s in range(n // 256):
                c = slice(256 * s, 256 * s + 256)
                a = P.stt(t.ap[:, c], X[:, k, c], A(k, s), r.ap[:, c], ALU.mult, ALU.mult, rtok, t.free)
                b = P.act(UH[:, k, c], t.ap[:, c], ACT.Identity, a, *toks, bias=B(k, s))
                d = P.stt(UL[:, k, c], t.ap[:, c], B(k, s), UH[:, k, c].bitcast(F32), ALU.add, ALU.subtract, b)
            t.done(d)
            ready.append(d)
        r.done(a)
        return ready

    uh = lambda n, s=0: (lambda k: UH[:, k, s:s + n])
    ul = lambda n, s=0: (lambda k: UL[:, k, s:s + n])

    def ffn(pre, n, ready, gate, tag):
        with ExitStack() as st:
            HH, HL = sb("HH" + tag, [128, NF, n], F32R, st), sb("HL" + tag, [128, NF, n], F32R, st)
            cuts = []
            old = every("pe", "act", "dve", "pool")
            for j in range(NF):
                gg, pg, tg = gemm([(pre + "g", k, 128 * j, 128) for k in range(8)], uh(n), ul(n), 128, n, each=ready)
                gu, pu, tu = gemm([(pre + "u", k, 128 * j, 128) for k in range(8)], uh(n), ul(n), 128, n)
                t = TM.get()
                h = t.ap[:, 0:n]
                a = P.act(h, pg, ACT.Silu, tg, t.free)
                gg.done(a)
                b = P.tt("dve", h, h, pu, ALU.mult, a, tu)
                gu.done(b)
                c, d = cut(HH[:, j, :], HL[:, j, :], h, b, old)
                t.done(d)
                cuts.append(d)
            stat = Stat(n)
            for m in range(8):
                g, ps, t = gemm([(pre + "d", k, 128 * m, 128) for k in range(NF)], lambda k: HH[:, k, :],
                                lambda k: HL[:, k, :], 128, n, each=cuts)
                xt = add_to_x(m, ps, n, gate, t)
                g.done(xt)
                stat.add(X[:, m, 0:n], xt)
            return stat, xt

    def add_to_x(m, ps, n, gate, tok):
        if gate is None:
            return P.stt(X[:, m, 0:n], ps, 0.5, X[:, m, 0:n], ALU.mult, ALU.add, tok)
        for s in range(n // 256):
            c = slice(256 * s, 256 * s + 256)
            a = P.stt(X[:, m, c], ps[:, c], gate(m, s), X[:, m, c], ALU.mult, ALU.add, tok)
        return a

    stat = Stat(256)
    for k in range(8):
        stat.add(X[:, k, 0:256], xload)
    r, rt = stat.rsqrt(D)
    ready = norm_to_u(r, rt, lambda k: col("ffn1_norm", k), 256)
    stat, xt = ffn("f1", 256, ready, None, "a")
    tap("x1", X[:, :, 0:256], xt)

    r, rt = stat.rsqrt(D)
    ready = norm_to_u(r, rt, lambda k: col("mix_norm", k), 256, every("pe"))
    mix1(P, nc, stack, sb, W, gemm, cut, rsqrt, tap, every, col, TM, MP, GP, SM, RBR, SSR, X, UH, UL, uh, ul,
         ready, consts, bias, ident, ones, cload, c1load, MOD)
    stat = Stat(256)
    oready = every("act", "dve")
    for m in range(8):
        g, ps, t = gemm([("wout", k, 128 * m, 128) for k in range(8)], uh(256), ul(256), 128, 256, oready)
        a = P.tt("dve", X[:, m, 0:256], X[:, m, 0:256], ps, ALU.add, t)
        g.done(a)
        stat.add(X[:, m, 0:256], a)
    tap("x2", X[:, :, 0:256], a)
    r, rt = stat.rsqrt(D)
    ready = norm_to_u(r, rt, lambda k: col("ffn2_norm", k), 256, every("pe"))
    stat, xt = ffn("f2", 256, ready, None, "b")
    r, rt = stat.rsqrt(D)
    old = every("act")
    for k in range(8):
        a = P.stt(X[:, k, 0:256], X[:, k, 0:256], col("final_norm", k), r.ap[:, 0:256], ALU.mult, ALU.mult, rt, old, xt)
    r.done(a)
    tap("x3", X[:, :, 0:256], a)
    block2(P, nc, stack, sb, W, gemm, cut, rsqrt, tap, every, col, TM, MP, GP, SM, RBR, SSR, X, UH, UL, uh, ul,
           consts2, ident, ones, MOD, Stat, ffn, ada_to_u, add_to_x, a, out)


def mix1(P, nc, stack, sb, W, gemm, cut, rsqrt, tap, every, col, TM, MP, GP, SM, RBR, SSR, X, UH, UL, uh, ul,
         ready, consts, bias, ident, ones, cload, c1load, MOD):
    names = list(const_blocks())
    with ExitStack() as st:
        def tile(name, shape, dt=F32):
            return sb(name, shape, dt, st)

        CN = tile("CN", [128, 18 * 128])
        old = every("pe", "act", "dve")
        cn = P.dma(CN[:], consts[:, 256:2560], "cn", old, e="pool")

        def C(name):
            i = names.index(name) - 2
            return CN[:, 128 * i:128 * i + 128]

        CQ = tile("CQ", [128, 12, 256])
        ZG = tile("ZG", [128, 4, 256])
        KT, VT = tile("KT", [128, 2, 512]), tile("VT", [128, 2, 512])
        OS = tile("OS", [128, 4, 256])
        G, BETA = tile("G", [128, 2, 8]), tile("BETA", [128, 2, 8])
        GA = tile("GA", [128, 6, 16])
        CS, CSR = tile("CSIL", [128, 8, 2]), tile("CSR", [128, 8, 4], F32R)
        win = lambda c, m=128: [("win", k, c, m) for k in range(8)]
        csi = P.act(CS[:], col("cc", 0, 16).rearrange("p (k v) -> p k v", k=8), ACT.Silu, old, cload)
        _, csr = cut(CSR[:, :, 0:2], CSR[:, :, 2:4], CS[:], csi)

        with ExitStack() as s2:
            CV = sb("CV", [128, 12, 260], F32, s2)
            pads = [P.do("pool", lambda g: g.memset(CV[:, :, 0:2], 0.0), old),
                    P.do("pool", lambda g: g.memset(CV[:, :, 258:260], 0.0))]
            done, zts = [None] * 12, []

            def conv(j):
                g, ps, t = gemm(win(128 * j), uh(256), ul(256), 128, 256, each=ready)
                a = P.act(CV[:, j, 2:258], ps, ACT.Copy, t, old)
                g.done(a)
                yield
                acc = TM.get()
                o = acc.ap[:, 0:256]
                b = P.ts("dve", o, CV[:, j, 0:256], col("conv_w", 5 * j), None, ALU.mult, None, a, acc.free, pads)
                for i in range(1, 5):
                    b = P.stt(o, CV[:, j, i:i + 256], col("conv_w", 5 * j + i), o, ALU.mult, ALU.add, b)
                yield
                c = P.act(CQ[:, j, :], o, ACT.Silu, b, old)
                acc.done(c)
                done[j] = c

            def gates(h):
                g, ps, t = gemm(win(128 * (12 + h)), uh(256), ul(256), 128, 256)
                yield
                zts.append(P.act(ZG[:, h, :], ps, ACT.Silu, t))
                g.done(zts[-1])

            run(*[conv(j) for j in range(12)], *[gates(h) for h in range(4)])
            tap("conv", CQ[:], done)

            pc = [W.next(k) for k in win(2048, 16)]
            g = GP.get()
            for i in range(2):
                for k in range(8):
                    wh, wl, rdy, _ = pc[k]
                    x = slice(128 * i, 128 * i + 128)
                    o = g.ap[:, 16 * i:16 * i + 16]
                    P.mm(o, UH[:, k, x], wh, k == 0, False, rdy, g.free, sig=False)
                    P.mm(o, UH[:, k, x], wl, False, False, sig=False)
                    t = P.mm(o, UL[:, k, x], wh, False, k == 7)
            W.release(t)
            AB = g.ap[:, 0:32].rearrange("p (i c) -> p i c", i=2)
            a = [GA[:, i, :].rearrange("p (i c) -> p i c", i=2) for i in range(6)]
            row = lambda name: col(name, 0, 8).unsqueeze(1).broadcast_to([128, 2, 8])
            t1 = P.tt("dve", a[0], AB[:, :, 0:8], row("dt_bias"), ALU.add, t, old)
            t2 = P.act(a[1], a[0], ACT.Abs, t1)
            t3 = P.act(a[2], a[1], ACT.Exp, t2, scale=-1.0)
            t4 = P.act(a[2], a[2], ACT.Ln, t3, bias=1.0)
            t5 = P.act(a[3], row("a_log"), ACT.Exp)
            t6 = P.act(a[4], AB[:, :, 8:16], ACT.Exp, scale=-1.0)
            g.done(t1, t6)
            t7 = P.ts("dve", a[0], a[0], 0.0, None, ALU.max, None, t2)
            t8 = P.tt("dve", a[0], a[0], a[2], ALU.add, t4, t7)
            t9 = P.ts("dve", a[0], a[0], -1.0, None, ALU.mult, None, t8)
            gt = P.tt("dve", G[:], a[0], a[3], ALU.mult, t9, t5)
            t11 = P.ts("dve", a[4], a[4], 1.0, None, ALU.add, None, t6)
            bt = P.recip(BETA[:], a[4], t11)
            tap("g", G[:], gt)
            tap("beta", BETA[:], bt)
            conv_done = every("act", "dve")

        qk, kv, qn, vb, sv = [], [], [None] * 8, [], {}
        with ExitStack() as s2:
            QB = sb("QB", [128, 8, 256], F32, s2)
            VB = sb("VB", [128, 2, 512], F32, s2)
            BW = sb("BW", [128, 8, 384], F32, s2)
            PT = sb("PT", [128, 3, 2, 256], F32, s2)
            CB = sb("CB", [128, 128 + 768], F32, s2)
            bd, mult, amask = CB[:, 0:128], CB[:, 128:512], CB[:, 512:896]
            PTR = Ring([PT[:, i] for i in range(3)])
            cbl = P.dma(CB[:], consts[:, 2560:3456], "cb", old, conv_done, e="pool")
            bl = P.dma(BW[:], bias, "bw", old, conv_done, e="pool")
            bw = P.tt("pool", BW[:], BW[:], amask.unsqueeze(1).broadcast_to([128, 8, 384]), ALU.add, bl, cbl)

            def unit(c):
                v = CQ[:, 2 * c:2 * c + 2, :]
                s, r = TM.get(), TM.get()
                sq = P.act(s.ap, v, ACT.Square, s.free, done)
                yield
                m = MP.get()
                mt = P.mm(m.ap, ones, s.ap, True, True, sq, m.free)
                s.done(mt)
                e, f = rsqrt(r.ap, m.ap, 1.0, mt, r.free)
                m.done(f)
                yield
                u = P.stt(v, v, 128 ** -0.5 if c < 2 else 1.0, r.ap.rearrange("p (a b) -> p a b", a=2),
                          ALU.mult, ALU.mult, e)
                r.done(u)
                qk.append(u)

            def by_token(i, base, dst):
                m = MP.get()
                for h in range(4):
                    t = P.tr(m.ap[:, 128 * h:128 * h + 128], CQ[:, base + h, 128 * i:128 * i + 128], ident,
                             m.free, qk, done, sig=h == 3)
                yield
                u = P.copy("dve", dst[:, i, :], m.ap, t, old)
                m.done(u)
                kv.append(u)

            def attn_qk(j):
                g, ps, t = gemm(win(2064 + 128 * j), uh(256), ul(256), 128, 256)
                s, r = TM.get(), TM.get()
                sq = P.act(s.ap[:, 0:256], ps, ACT.Square, s.free, t)
                yield
                m = MP.get()
                mt = P.mm(m.ap[:, 0:256], bd, s.ap[:, 0:256], True, True, sq, m.free, cbl)
                s.done(mt)
                e, f = rsqrt(r.ap[:, 0:256], m.ap[:, 0:256], 1.0 / 64, mt, r.free)
                m.done(f)
                yield
                u = P.stt(QB[:, j, :], ps, col("q_norm_w" if j < 4 else "k_norm_w"), r.ap[:, 0:256],
                          ALU.mult, ALU.mult, e, conv_done)
                if j < 4:
                    u = P.ts("dve", QB[:, j, :], QB[:, j, :], 64 ** -0.5, None, ALU.mult, None, u)
                r.done(u)
                g.done(u)
                qn[j] = u

            def attn_v(j):
                g, ps, t = gemm(win(2064 + 128 * (8 + j)), uh(256), ul(256), 128, 256)
                s = TM.get()
                u = P.act(s.ap[:, 0:256], ps, ACT.Copy, s.free, t)
                g.done(u)
                yield
                m = MP.get()
                for i in range(2):
                    tv = P.tr(m.ap[:, 128 * i:128 * i + 128], s.ap[:, 128 * i:128 * i + 128], ident, u, m.free)
                s.done(tv)
                yield
                u = P.act(VB[:, :, 128 * j:128 * j + 128], m.ap[:, 0:256].rearrange("p (i c) -> p i c", i=2), ACT.Copy,
                          tv, conv_done)
                m.done(u)
                vb.append(u)

            run(*[attn_qk(j) for j in range(8)], *[unit(c) for c in range(4)], *[attn_v(j) for j in range(4)],
                *[by_token(i, b, d) for i in range(2) for b, d in ((4, KT), (8, VT))])
            uq = every("pe")
            tap("qk", CQ[:], qk)
            tap("qb", QB[:], qn)

            def band(c):
                o, pts = None, []
                for h in (2 * c, 2 * c + 1):
                    b = 64 * (h % 2)
                    m, sm = MP.get(), SM.get()
                    for i in range(2):
                        t = P.mm(m.ap[:, 256 * i:256 * i + 256], QB[b:b + 64, c, 128 * i:128 * i + 128],
                                 QB[b:b + 64, 4 + c, :], True, True, qn, m.free)
                    s, y = TM.get(), TM.get()
                    mx = []
                    for i in range(2):
                        w = BW[:, h, 128 * (1 - i):128 * (1 - i) + 256]
                        mx.append(P.ttr(s.ap[:, 256 * i:256 * i + 256], m.ap[:, 256 * i:256 * i + 256], w, -3.0e38,
                                        ALU.add, ALU.max, sm.ap[:, i:i + 1], t, s.free, sm.free, bw))
                    m.done(mx[-1])
                    ng = P.ts("dve", sm.ap[:, 2:4], sm.ap[:, 0:2], -1.0, None, ALU.mult, None, mx)
                    yield
                    ex = []
                    for i in range(2):
                        v = s.ap[:, 256 * i:256 * i + 256]
                        ex.append(P.act(v, v, ACT.Exp, ng, bias=sm.ap[:, 2 + i:3 + i]))
                    yield
                    dn = []
                    for i in range(2):
                        dn.append(P.ttr(y.ap[:, 256 * i:256 * i + 256], s.ap[:, 256 * i:256 * i + 256],
                                        mult[:, 128 * (1 - i):128 * (1 - i) + 256], 0.0, ALU.mult, ALU.add,
                                        sm.ap[:, 4 + i:5 + i], ex, y.free))
                    s.done(dn[-1])
                    rc = P.recip(sm.ap[:, 6:8], sm.ap[:, 4:6], dn)
                    nm = []
                    for i in range(2):
                        v = y.ap[:, 256 * i:256 * i + 256]
                        nm.append(P.ts("dve", v, v, sm.ap[:, 6 + i:7 + i], None, ALU.mult, None, rc))
                    sm.done(nm[-1])
                    yield
                    m, pt = MP.get(), PTR.get()
                    for kc in range(2):
                        for i in range(2):
                            t = P.tr(m.ap[:, 256 * kc + 128 * i:256 * kc + 128 * i + 128],
                                     y.ap[:, 256 * i + 128 * kc:256 * i + 128 * kc + 128], ident, nm, m.free)
                    y.done(t)
                    ev = P.act(pt.ap, m.ap.rearrange("p (a b) -> p a b", a=2), ACT.Copy, t, pt.free, conv_done)
                    m.done(ev)
                    yield
                    o = o or MP.get()
                    for kc in range(2):
                        t = P.mm(o.ap[b:b + 64, 0:256], VB[:, kc, 64 * h:64 * h + 64], pt.ap[:, kc, :],
                                 kc == 0, kc == 1, ev, vb, o.free)
                    pt.done(t)
                yield
                _, u = cut(UH[:, 4 + c, 0:256], UL[:, 4 + c, 0:256], o.ap[:, 0:256], t, uq)
                o.done(u)

            ada = modulation(P, W, MP, MOD, col, TM, CSR, csr, ident, cload)
            beside(rounds([band(c) for c in range(4)], 3), limited(ada, 40))
            tap("uswa", UH[:, 4:8, 0:256].bitcast(F32), every("act"))
            swa_done = every("act", "dve", "pe", "pool")

        GT_ = tile("GDN", [128, 4, 7, 512])
        h4 = lambda ap: ap.rearrange("p (h c) -> p h c", h=4)
        bc = lambda ap: ap.unsqueeze(1).broadcast_to([128, 4, 128])
        cb = lambda ap: ap.unsqueeze(2).broadcast_to([128, 4, 128])
        hs = lambda ap, h: ap[:, 128 * h:128 * h + 128]
        S = [CQ[:, 8 + 2 * d:10 + 2 * d, :].rearrange("p a b -> p (a b)") for d in range(2)]
        first_o, state = {}, {}

        def per_head(w, x, *toks, out=None):
            m = MP.get()
            for h in range(4):
                e = P.mm(hs(m.ap, h), w(h), x(h), True, True, *toks, m.free, sig=h == 3)
            return m, e

        def delta(order, d):
            i = order if d == 0 else 1 - order
            n = 2 * order + d
            tri, st_, lm, um = ("LE", "GT", "ML", "MU") if d == 0 else ("GE", "LT", "MU", "ML")
            gq, IT, UU, T_, P_, Y, UL_ = (GT_[:, n, j, :] for j in range(7))
            ck = slice(128 * i, 128 * i + 128)
            gcol, bcol = G[:, i, 4 * d:4 * d + 4], BETA[:, i, 4 * d:4 * d + 4]
            a = P.tt("dve", h4(gq), bc(C(tri)), cb(gcol), ALU.mult, gt, swa_done, cn)
            yield
            m, e = per_head(lambda h: hs(gq, h), lambda h: C(st_), a)
            x = P.act(T_, m.ap, ACT.Exp, e, swa_done)
            m.done(x)
            m = MP.get()
            e = P.mm(m.ap, C(st_), gq, True, True, m.free)
            y = P.act(IT, m.ap, ACT.Exp, e)
            m.done(y)
            m, cols = MP.get(), SM.get()
            P.mm(m.ap[:, 0:4], C(tri), gcol, True, True, m.free, sig=False)
            e = P.mm(m.ap[:, 4:8], C(st_), gcol, True, True)
            colt = P.act(cols.ap, m.ap[:, 0:8], ACT.Exp, e, cols.free)
            m.done(colt)
            q = None
            if order == 1:
                m = MP.get()
                e = P.mm(m.ap, ones, gq, True, True, m.free)
                q = P.act(gq, m.ap, ACT.Exp, e)
                m.done(q)
            yield
            if order == 1:
                q = P.tt("dve", h4(gq), h4(gq), CQ[:, 0:4, ck], ALU.mult, q, qk)
            xs = P.tt("dve", h4(T_), h4(T_), bc(C(st_)), ALU.mult, x)
            ys = P.tt("dve", h4(IT), h4(IT), bc(C(tri)), ALU.mult, y)
            yield
            m, e = per_head(lambda h: CQ[:, 4 + h, ck], lambda h: CQ[:, 4 + h, ck], qk)
            x = P.tt("dve", T_, m.ap, T_, ALU.mult, e, xs)
            m.done(x)
            x = P.tt("dve", h4(T_), h4(T_), cb(bcol), ALU.mult, x, bt)
            yield
            m, e = per_head(lambda h: CQ[:, 4 + h, ck], lambda h: CQ[:, h, ck])
            it = P.tt("dve", IT, m.ap, IT, ALU.mult, e, ys)
            m.done(it)
            yield
            m = MP.get()
            for h in range(4):
                e = P.tr(hs(m.ap, h), hs(T_, h), ident, x, m.free, sig=h == 3)
            uu = P.act(UU, m.ap, ACT.Copy, e, swa_done)
            m.done(uu)
            yield
            p = P.tt("dve", h4(T_), h4(T_), bc(C(lm + "0")), ALU.mult, x, e)
            p = P.tt("dve", h4(T_), bc(ident), h4(T_), ALU.subtract, p)
            w = P.tt("dve", h4(P_), h4(UU), bc(C(um + "0")), ALU.mult, uu)
            w = P.tt("dve", h4(P_), bc(ident), h4(P_), ALU.subtract, w)
            ye, ze = None, None
            for lv in range(1, 7):
                ul_ = P.tt("pool", h4(UL_), h4(UU), bc(C(f"{um}{lv}")), ALU.mult, uu, ye, swa_done)
                yield
                m, ye = per_head(lambda h: hs(UL_, h), lambda h: hs(T_, h), ul_, p)
                y = P.act(Y, m.ap, ACT.Copy, ye, ze, swa_done)
                m.done(y)
                yield
                if lv < 6:
                    m, e = per_head(lambda h: hs(P_, h), lambda h: hs(Y, h), y, w)
                    p = P.tt("dve", T_, T_, m.ap, ALU.subtract, e)
                    m.done(p)
                m, ze = per_head(lambda h: hs(Y, h), lambda h: hs(P_, h), y, w)
                w = P.tt("dve", P_, P_, m.ap, ALU.subtract, ze)
                m.done(w)
            VB_, KD, VN, WT = Y, UL_, T_, UU
            yield
            vbt = P.tt("dve", h4(VB_), h4(VT[:, i, :]), cb(bcol), ALU.mult, kv, ze)
            if order == 1:
                c = P.tt("pool", h4(KD), h4(KT[:, i, :]), cb(bcol), ALU.mult, kv, ye)
                c = P.tt("pool", h4(KD), h4(KD), cb(cols.ap[:, 0:4]), ALU.mult, c, colt)
                cols.done(c)
                yield
                m, e = per_head(lambda h: hs(KD, h), lambda h: hs(P_, h), c, w)
                wt = P.act(WT, m.ap, ACT.Copy, e, ul_, scale=-1.0)
                m.done(wt)
            else:
                c = P.tt("pool", h4(KD), h4(KT[:, i, :]), cb(cols.ap[:, 4:8]), ALU.mult, kv, colt, ye)
                cols.done(c)
            yield
            sd = state.get(d)
            m = MP.get()
            for h in range(4):
                e = P.mm(hs(m.ap, h), hs(P_, h), hs(VB_, h), True, order == 0, w, vbt, m.free)
                if order == 1:
                    e = P.mm(hs(m.ap, h), hs(WT, h), hs(S[d], h), False, True, wt, sd)
            vn = P.act(VN, m.ap, ACT.Copy, e)
            m.done(vn)
            yield
            if order == 0:
                m, e = per_head(lambda h: hs(KD, h), lambda h: hs(VN, h), c, vn)
                state[d] = P.copy("dve", S[d], m.ap, e, kv)
                m.done(state[d])
            m = MP.get()
            for h in range(4):
                e = P.mm(hs(m.ap, h), hs(VN, h), hs(IT, h), True, order == 0, vn, it, m.free)
                if order == 1:
                    e = P.mm(hs(m.ap, h), hs(S[d], h), hs(gq, h), False, True, q, sd)
            yield
            if i not in first_o:
                first_o[i] = P.copy("dve", OS[:, :, ck], h4(m.ap), e)
            else:
                first_o[i] = P.tt("dve", OS[:, :, ck], OS[:, :, ck], h4(m.ap), ALU.add, e, first_o[i])
            m.done(first_o[i])

        beside(rounds([delta(o, d) for o in range(2) for d in range(2)], 4), ada)
        tap("os", OS[:], first_o[0], first_o[1])

        def finish(c):
            v = OS[:, 2 * c:2 * c + 2, :]
            s, m, r = TM.get(), MP.get(), TM.get()
            sq = P.act(s.ap, v, ACT.Square, s.free, first_o[0], first_o[1])
            mt = P.mm(m.ap, ones, s.ap, True, True, sq, m.free)
            e, f = rsqrt(r.ap, m.ap, 1.0 / 128, mt, r.free)
            m.done(f)
            yield
            x2 = s.ap.rearrange("p (a b) -> p a b", a=2)
            u = P.stt(x2, v, col("gdn_norm_w"), r.ap.rearrange("p (a b) -> p a b", a=2), ALU.mult, ALU.mult, e, mt)
            r.done(u)
            u = P.tt("dve", x2, x2, ZG[:, 2 * c:2 * c + 2, :], ALU.mult, u, zts)
            _, w = cut(UH[:, 2 * c:2 * c + 2, 0:256], UL[:, 2 * c:2 * c + 2, 0:256], x2, u, uq)
            s.done(w)

        run(finish(0), finish(1))
        tap("ugdn", UH[:, 0:4, 0:256].bitcast(F32), every("act"))


def limited(gen, n):
    for _ in range(n):
        if next(gen, gen) is gen:
            return
        yield


def modulation(P, W, MP, MOD, col, TM, CSR, csr, ident, cload):
    for l in range(2):
        for m in range(18):
            b = MP.get()
            for k in range(8):
                wh, wl, rdy, last = W.next((f"ada{l}", k, 512 * m, 512))
                P.mm(b.ap[0:4, :], CSR[:, k, :], wh, k == 0, False, rdy, csr, b.free, sig=False)
                t = P.mm(b.ap[0:4, :], CSR[:, k, :], wl, False, k == 7, sig=last)
                if last:
                    W.release(t)
                    if k < 7:
                        yield
            s = TM.get()
            a = P.act(s.ap[0:4, :], b.ap[0:4, :], ACT.Copy, t, s.free)
            b.done(a)
            yield
            b = MP.get()
            for j in range(4):
                t = P.tr(b.ap[:, 4 * j:4 * j + 4], s.ap[0:4, 128 * j:128 * j + 128], ident[0:4, 0:4], a, b.free)
            s.done(t)
            yield
            bias = col(f"b_ada{l}", 4 * m, 4).unsqueeze(2).broadcast_to([128, 4, 2])
            q = b.ap[:, 0:16].rearrange("p (j v) -> p j v", j=4)
            o = MOD[:, l, 4 * m:4 * m + 4, :]
            u = P.tt("dve", o, q[:, :, 0:2], bias, ALU.add, t, cload)
            u = P.tt("dve", o, o, q[:, :, 2:4], ALU.add, u)
            b.done(u)


def block2(P, nc, stack, sb, W, gemm, cut, rsqrt, tap, every, col, TM, MP, GP, SM, RBR, SSR, X, UH, UL, uh, ul,
           consts2, ident, ones, MOD, Stat, ffn, ada_to_u, add_to_x, xt, out):
    old = every("pe", "act", "dve", "pool")
    DER = sb("DER", [128, 2, 6, 8, 2])
    der = []
    for l in range(2):
        for i, g in enumerate(("g_ffn1", "g_mix", "g_ffn2")):
            sc = MOD[:, l, 24 * i + 8:24 * i + 16, :]
            gv = col(f"{g}{l}", 0, 8).unsqueeze(2).broadcast_to([128, 8, 2])
            a = P.ts("dve", DER[:, l, i], sc, 1.0, None, ALU.add, None, old)
            der.append(P.tt("dve", DER[:, l, i], DER[:, l, i], gv, ALU.mult, a))
            f = 1.0 if i == 1 else 0.5
            der.append(P.ts("dve", DER[:, l, 3 + i], MOD[:, l, 24 * i + 16:24 * i + 24, :], f, None, ALU.mult, None))
    A = lambda l, i: (lambda k, s: DER[:, l, i, k, s:s + 1])
    B = lambda l, i: (lambda k, s: MOD[:, l, 24 * i + k, s:s + 1])
    gate = lambda l, i: (lambda k, s: DER[:, l, 3 + i, k, s:s + 1])
    tap("mod", MOD[:], der)

    stat = Stat(512)
    for k in range(8):
        stat.add(X[:, k, :], xt, der)
    for l in range(2):
        n = 512 if l == 0 else 256
        r, rt = stat.rsqrt(D)
        ready = ada_to_u(r, rt, A(l, 0), B(l, 0), 512, every("pe"), der)
        stat, xt = ffn(f"f1{l}", 512, ready, gate(l, 0), f"c{l}")
        tap(f"y1{l}", X[:], xt)
        r, rt = stat.rsqrt(D)
        ready = ada_to_u(r, rt, A(l, 1), B(l, 1), 512, every("pe"))
        mix2(P, nc, stack, sb, W, gemm, cut, rsqrt, tap, every, col, TM, MP, GP, SM, RBR, X, UH, UL, uh, ul,
             consts2, ident, ones, ready, l, n, Stat, add_to_x, gate)
        stat = mix2.stat
        r, rt = stat.rsqrt(D)
        ready = ada_to_u(r, rt, A(l, 2), B(l, 2), n, every("pe"))
        stat, xt = ffn(f"f2{l}", n, ready, gate(l, 2), f"d{l}")
        tap(f"y3{l}", X[:], xt)
    r, rt = stat.rsqrt(D)
    sq = every("act")
    for k in range(8):
        a = P.stt(X[:, k, 0:256], X[:, k, 0:256], col("g_final", k), r.ap[:, 0:256], ALU.mult, ALU.mult, rt, sq, xt)
        o = P.dma(out[:, 256 * k:256 * k + 256], X[:, k, 0:256], "out", a)
    P.wait("sp", [o])


def mix2(P, nc, stack, sb, W, gemm, cut, rsqrt, tap, every, col, TM, MP, GP, SM, RBR, X, UH, UL, uh, ul,
         consts2, ident, ones, ready, l, n, Stat, add_to_x, gate):
    ns = n // 256
    L = str(l)
    with ExitStack() as st:
        def tile(name, shape, dt=F32, s=None):
            return sb(name + L, shape, dt, s or st)

        old = every("pe", "act", "dve", "pool")
        CVH, CVL = tile("CVH", [128, 3, n], F32R), tile("CVL", [128, 3, n], F32R)
        ATH, ATL = tile("ATH", [128, 4, n], F32R), tile("ATL", [128, 4, n], F32R)
        win = lambda c: [(f"win{l}", k, c, 128) for k in range(8)]
        with ExitStack() as s3:
            K2 = tile("K2", [128, 640], F32, s3)
            k2 = P.dma(K2[:], consts2[:, 0:640], "k2" + L, old, e="pool")
            ROT, COS, SIN = K2[0:96, 0:96], K2[0:96, 128:384], K2[0:96, 384:640]
            VC = tile("VC", [128, 3, ns, 286], F32, s3)
            AC = tile("AC", [128, 3, ns, 256], F32, s3)
            CQH, CQL = tile("CQH", [128, 3, n], F32R, s3), tile("CQL", [128, 3, n], F32R, s3)
            CKH, CKL = tile("CKH", [128, 2, 512], F32R, s3), tile("CKL", [128, 2, 512], F32R, s3)
            KR = tile("KR", [96, 512], F32, s3)
            V = tile("V", [128, 4, 512], F32, s3)
            QK = tile("QK", [96, 4, 512], F32, s3)
            QR, KRG = Ring([QK[:, 0], QK[:, 1]]), Ring([QK[:, 2], QK[:, 3]])
            PTT = tile("PTT", [128, 2, 4, 256], F32, s3)
            PTR = Ring([PTT[:, 0], PTT[:, 1]])
            pads = [P.do("pool", lambda g: g.memset(VC[:, :, :, 0:15], 0.0), old),
                    P.do("pool", lambda g: g.memset(VC[:, :, :, 271:286], 0.0))]
            sv = lambda ap: ap.rearrange("p (s t) -> p s t", s=ns)
            fl = lambda ap: ap.rearrange("p s t -> p (s t)")
            acc = []

            for c in range(3):
                g, ps, t = gemm(win(384 + 128 * c), uh(n), ul(n), 128, n, each=ready)
                s = TM.get()
                a = P.act(s.ap[:, 0:n], ps, ACT.Sigmoid, t, s.free)
                g.done(a)
                g, ps, t = gemm(win(128 * c), uh(n), ul(n), 128, n)
                b = P.tt("dve", VC[:, c, :, 15:271], sv(s.ap[:, 0:n]), sv(ps), ALU.mult, a, t, old)
                g.done(b)
                s.done(b)
                acc.append(P.ts("dve", AC[:, c], VC[:, c, :, 0:256], col(f"w_dw{l}", 31 * c), col(f"b_dw{l}", c),
                                ALU.mult, ALU.add, b, pads))

            def taps_():
                for i in range(1, 31):
                    for c in range(3):
                        acc[c] = P.stt(AC[:, c], VC[:, c, :, i:i + 256], col(f"w_dw{l}", 31 * c + i), AC[:, c],
                                       ALU.mult, ALU.add, acc[c])
                    if i % 2 == 0:
                        yield
                s, m = TM.get(), MP.get()
                a = P.tt("dve", s.ap[:, 0:n], fl(AC[:, 0]), fl(AC[:, 1]), ALU.add, acc, s.free)
                a = P.tt("dve", s.ap[:, 0:n], s.ap[:, 0:n], fl(AC[:, 2]), ALU.add, a)
                yield
                e = P.mm(m.ap[:, 0:n], ones, s.ap[:, 0:n], True, True, a, m.free)
                s.done(e)
                yield
                stat = Stat(n)
                for c in range(3):
                    acc[c] = P.stt(fl(AC[:, c]), m.ap[:, 0:n], -1.0 / 384, fl(AC[:, c]), ALU.mult, ALU.add, e)
                    stat.add(fl(AC[:, c]), acc[c])
                m.done(acc[2])
                sq = every("act")
                yield
                r, rt = stat.rsqrt(384, TM)
                yield
                for c in range(3):
                    a = P.stt(fl(AC[:, c]), fl(AC[:, c]), col(f"ln_g{l}", c), r.ap[:, 0:n], ALU.mult, ALU.mult, rt,
                              sq, acc[c])
                    b = P.act(fl(AC[:, c]), fl(AC[:, c]), ACT.Silu, a, bias=col(f"ln_b{l}", c))
                    cut(CVH[:, c, :], CVL[:, c, :], fl(AC[:, c]), b, old)
                r.done(a)

            def latent(nt, base, gname, hi, lo, nn, got):
                stat, toks = Stat(nn), []
                for j in range(nt):
                    g, ps, t = gemm(win(base + 128 * j), uh(nn), ul(nn), 128, nn)
                    sq = stat.add(ps, t)
                    gc = col(f"{gname}{l}", j)
                    a = P.act(hi[:, j, :], ps, ACT.Copy, old, t, scale=gc)
                    b = P.stt(lo[:, j, :], ps, gc, hi[:, j, :].bitcast(F32), ALU.mult, ALU.subtract, a)
                    g.done(sq, b)
                    toks.append(b)
                    yield
                got.extend(stat.rsqrt(128 * nt) + (toks,))

            def rope(q, tok):
                m, s = MP.get(), TM.get()
                e = P.mm(m.ap[0:96, 0:256], ROT, q[:, 0:256], True, True, tok, m.free, k2)
                a = P.tt("dve", s.ap[0:96, 0:256], m.ap[0:96, 0:256], SIN, ALU.mult, e, s.free, k2)
                m.done(a)
                b = P.tt("dve", q[:, 0:256], q[:, 0:256], COS, ALU.mult, e)
                c = P.tt("dve", q[:, 0:256], q[:, 0:256], s.ap[0:96, 0:256], ALU.add, a, b)
                s.done(c)
                return c

            SC = 96 ** -0.5

            def attention():
                gq, gk = [], []
                yield from latent(3, 768, "g_q", CQH, CQL, n, gq)
                yield from latent(2, 1152, "g_kv", CKH, CKL, 512, gk)
                (rq, rqt, cqt), (rk, rkt, ckt) = gq, gk
                g, ps, t = gemm([(f"wkr{l}", k, 0, 96) for k in range(8)], uh(512), ul(512), 96, 512)
                a = P.copy("dve", KR[:], ps, t, old)
                g.done(a)
                m, sm = MP.get(), SM.get()
                for i in range(4):
                    e = P.tr(m.ap[:, 128 * i:128 * i + 128], rk.ap[:, 128 * i:128 * i + 128], ident, rkt, m.free)
                rc = P.copy("dve", sm.ap[:, 0:4], m.ap.rearrange("p (i c) -> p i c", i=4)[:, :, 0:1].rearrange(
                    "p i c -> p (i c)"), e, sm.free)
                m.done(rc)
                yield
                pc = [W.next((f"wv{l}", k, 0, 512)) for k in range(2)]
                vt = []
                for i in range(4):
                    g = GP.get()
                    x = slice(128 * i, 128 * i + 128)
                    for k in range(2):
                        wh, wl, rdy, _ = pc[k]
                        P.mm(g.ap, CKH[:, k, x], wh, k == 0, False, rdy, ckt, g.free, sig=False)
                        P.mm(g.ap, CKH[:, k, x], wl, False, False, sig=False)
                        t = P.mm(g.ap, CKL[:, k, x], wh, False, k == 1)
                    vt.append(P.act(V[:, i, :], g.ap, ACT.Copy, t, rc, old, scale=sm.ap[:, i:i + 1]))
                    g.done(vt[-1])
                W.release(t)
                sm.done(vt[-1])
                kr = rope(KR, a)
                yield
                out = {}

                def head(h):
                    c, b0 = h // 2, 64 * (h % 2)
                    g, ps, t = gemm([(f"wuq{l}", k, 96 * h, 96) for k in range(3)], lambda k: CQH[:, k, :],
                                    lambda k: CQL[:, k, :], 96, n, cqt)
                    q = QR.get()
                    a = P.tt("dve", q.ap[:, 0:n], ps, rq.ap[0:96, 0:n], ALU.mult, t, rqt, q.free, old)
                    g.done(a)
                    g, ps, t = gemm([(f"wkn{l}", k, 96 * h, 96) for k in range(2)], lambda k: CKH[:, k, :],
                                    lambda k: CKL[:, k, :], 96, 512, ckt)
                    kk = KRG.get()
                    ka = P.tt("dve", kk.ap[0:64, :], ps[0:64, :], rk.ap[0:64, :], ALU.mult, t, rkt, kk.free, old)
                    g.done(ka)
                    kt = P.copy("pool", kk.ap[64:96, :], KR[64:96, :], kk.free, kr, old)
                    yield
                    qt = rope(q.ap, a)
                    yield
                    for s in range(ns):
                        k0, nk = (0, 512) if s == 0 else (256, 256)
                        soft = []
                        for i in range(2):
                            m, sm, p = MP.get(), SM.get(), TM.get()
                            qs = 256 * s + 128 * i
                            e = P.mm(m.ap[:, 0:nk], q.ap[:, qs:qs + 128], kk.ap[:, k0:k0 + nk], True, True, qt, ka, kt,
                                     m.free)
                            mx = P.rmax(sm.ap[:, 0:1], m.ap[:, 0:nk], e, sm.free)
                            mx = P.ts("dve", sm.ap[:, 1:2], sm.ap[:, 0:1], -SC, None, ALU.mult, None, mx)
                            ex = P.act(p.ap[:, 0:nk], m.ap[:, 0:nk], ACT.Exp, mx, p.free, scale=SC,
                                       bias=sm.ap[:, 1:2], accum_out=sm.ap[:, 2:3])
                            m.done(ex)
                            soft.append((sm, p, ex))
                        yield
                        for i, (sm, p, ex) in enumerate(soft):
                            rcp = P.recip(sm.ap[:, 3:4], sm.ap[:, 2:3], ex)
                            nm = P.ts("dve", p.ap[:, 0:nk], p.ap[:, 0:nk], sm.ap[:, 3:4], None, ALU.mult, None, rcp)
                            sm.done(nm)
                            soft[i] = (p, nm)
                        yield
                        pt = PTR.get()
                        for i, (p, nm) in enumerate(soft):
                            m = MP.get()
                            for kc in range(nk // 128):
                                e = P.tr(m.ap[:, 128 * kc:128 * kc + 128], p.ap[:, 128 * kc:128 * kc + 128], ident, nm,
                                         m.free)
                            p.done(e)
                            ev = P.act(pt.ap[:, 0:nk // 128, 128 * i:128 * i + 128],
                                       m.ap[:, 0:nk].rearrange("p (a b) -> p a b", b=128), ACT.Copy, e, pt.free, old)
                            m.done(ev)
                        yield
                        if c not in out:
                            out[c] = MP.get()
                        o = out[c]
                        for kc in range(nk // 128):
                            e = P.mm(o.ap[b0:b0 + 64, 256 * s:256 * s + 256], V[:, k0 // 128 + kc, 64 * h:64 * h + 64],
                                     pt.ap[:, kc, :], kc == 0, kc == nk // 128 - 1, ev, vt, o.free)
                        pt.done(e)
                    q.done(e)
                    kk.done(e)
                    yield
                    if h % 2:
                        _, u = cut(ATH[:, c, :], ATL[:, c, :], o.ap[:, 0:n], e, old)
                        o.done(u)

                yield from rounds([head(h) for h in range(8)], 2)
                rq.done(*every("dve"))
                rk.done(*every("dve"))

            beside(attention(), taps_())
            tap("at" + L, ATH[:].bitcast(F32), every("act"))
            tap("cv" + L, CVH[:].bitcast(F32), every("act"))
        fold = every("pe", "act", "dve", "pool")
        FOH, FOL = tile("FOH", [128, 4, n], F32R), tile("FOL", [128, 4, n], F32R)
        with ExitStack() as s4:
            K3 = tile("K3", [128, 1280], F32, s4)
            k3 = P.dma(K3[:], consts2[:, 640:1920], "k3" + L, fold, e="pool")
            CS = K3[:, 0:256]
            CT = K3[:, 256:768].rearrange("p (i t) -> p i t", i=2)
            ST = K3[:, 768:1280].rearrange("p (i t) -> p i t", i=2)
            AF = tile("AF", [128, 4, 2, 256], F32, s4)
            AR = Ring([AF[:, i] for i in range(4)])

            def fourier(j):
                g, ps, t = gemm(win(1440 + 128 * j), uh(n), ul(n), 128, n)
                z = TM.get()
                zt = P.act(z.ap[:, 0:n], ps, ACT.Copy, t, z.free)
                g.done(zt)
                yield
                half = []
                for s in range(ns):
                    m, a = MP.get(), AR.get()
                    for i in range(2):
                        c = 256 * s + 128 * i
                        e = P.mm(m.ap[:, 256 * i:256 * i + 256], z.ap[:, c:c + 128], CS, True, True, zt, k3, m.free)
                    at = P.copy("dve", a.ap, m.ap.rearrange("p (i c) -> p i c", i=2), e, a.free, fold)
                    m.done(at)
                    half.append((a, at))
                z.done(e)
                yield
                fm = MP.get()
                for s, (a, at) in enumerate(half):
                    o = fm.ap[:, 256 * s:256 * s + 256]
                    for i in range(2):
                        P.mm(o, a.ap[:, i, 0:128], CT[:, i, :], i == 0, False, at, fm.free)
                        e2 = P.mm(o, a.ap[:, i, 128:256], ST[:, i, :], False, i == 1)
                    a.done(e2)
                _, ft = cut(FOH[:, j, :], FOL[:, j, :], fm.ap[:, 0:n], e2, fold)
                fm.done(ft)

            run(*[fourier(j) for j in range(4)], width=2)
            tap("fo" + L, FOH[:].bitcast(F32), every("act"))
        adone = every("pe", "act", "dve", "pool")
        YH, YL = tile("YH", [128, 8, n], F32R), tile("YL", [128, 8, n], F32R)
        yt = []
        for m in range(8):
            sig = []
            for b in range(3):
                g, ps, t = gemm([(f"wbg{l}", k, 1024 * b + 128 * m, 128) for k in range(8)], uh(n), ul(n), 128, n)
                s = TM.get()
                a = P.act(s.ap[:, 0:n], ps, ACT.Sigmoid, t, s.free, bias=col(f"b_bg{l}", 8 * b + m))
                g.done(a)
                sig.append((s, a))
            v = [s.ap[:, 0:n] for s, _ in sig]
            g, ps, t = gemm([(f"wpw{l}", k, 128 * m, 128) for k in range(3)], lambda k: CVH[:, k, :],
                            lambda k: CVL[:, k, :], 128, n, adone)
            a0 = P.stt(v[0], ps, col(f"b_pw{l}", m), v[0], ALU.add, ALU.mult, t, sig[0][1])
            g.done(a0)
            g, ps, t = gemm([(f"wo{l}", k, 128 * m, 128) for k in range(4)], lambda k: ATH[:, k, :],
                            lambda k: ATL[:, k, :], 128, n)
            a1 = P.tt("dve", v[1], ps, v[1], ALU.mult, t, sig[1][1])
            g.done(a1)
            g, ps, t = gemm([(f"wf{l}", k, 128 * m, 128) for k in range(4)], lambda k: FOH[:, k, :],
                            lambda k: FOL[:, k, :], 128, n)
            a2 = P.stt(v[2], ps, col(f"b_f{l}", m), v[2], ALU.add, ALU.mult, t, sig[2][1])
            g.done(a2)
            a0 = P.tt("dve", v[0], v[0], v[1], ALU.add, a0, a1)
            a0 = P.tt("dve", v[0], v[0], v[2], ALU.add, a0, a2)
            _, u = cut(YH[:, m, :], YL[:, m, :], v[0], a0, adone)
            for s, _ in sig:
                s.done(u)
            yt.append(u)
        stat = Stat(n)
        for m in range(8):
            g, ps, t = gemm([(f"wout{l}", k, 128 * m, 128) for k in range(8)], lambda k: YH[:, k, :],
                            lambda k: YL[:, k, :], 128, n, each=yt)
            a = add_to_x(m, ps, n, gate(l, 1), t)
            g.done(a)
            stat.add(X[:, m, 0:n], a)
        mix2.stat = stat
        tap("y2" + L, X[:], a)


def host_arrays(inputs):
    a = {k: np.asarray(v, dtype=np.asarray(v).dtype) for k, v in inputs.items()}
    wt = {"f1g": a["ffn1_w_gate"][0], "f1u": a["ffn1_w_up"][0], "f1d": a["ffn1_w_down"][0],
          "f2g": a["ffn2_w_gate"][0], "f2u": a["ffn2_w_up"][0], "f2d": a["ffn2_w_down"][0],
          "win": a["w_in"][0], "wout": a["w_out"][0]}
    for l in range(2):
        for f in (1, 2):
            wt[f"f{f}{l}g"], wt[f"f{f}{l}u"], wt[f"f{f}{l}d"] = (
                a[f"w1_ffn{f}_2"][l], a[f"w3_ffn{f}_2"][l], a[f"w2_ffn{f}_2"][l])
        wt[f"ada{l}"], wt[f"win{l}"], wt[f"wpw{l}"] = a["w_ada_2"][l], a["w_in_2"][l], a["w_pw_conv_2"][l]
        wt[f"wuq{l}"], wt[f"wo{l}"], wt[f"wf{l}"] = a["w_uq_2"][l], a["w_o_mla_2"][l], a["w_fourier_2"][l]
        wt[f"wbg{l}"], wt[f"wout{l}"] = a["w_bgate_2"][l], a["w_out_2"][l]
        wt[f"wkr{l}"] = np.concatenate([np.zeros((1024, 64), np.float32), a["w_in_2"][l][:, 1408:1440]], axis=1)
        kv = a["w_ukv_2"][l].reshape(256, 8, 128)
        wt[f"wkn{l}"] = np.concatenate([kv[:, :, :64], np.zeros((256, 8, 32), np.float32)], axis=2).reshape(256, 768)
        wt[f"wv{l}"] = kv[:, :, 64:].reshape(256, 512)
    units, total = plan()
    stream = np.empty(total, np.float32)
    for at, n, ps in units:
        u = stream[at:at + 128 * n].reshape(128, n)
        for (name, k, m0, m), c in ps:
            u[:, c:c + m] = wt[name][128 * k:128 * k + 128, m0:m0 + m]

    def fm(v):
        v = np.asarray(v)
        return v.reshape(-1, 128).T

    c1 = {"ffn1_norm": fm(a["ffn1_norm"][0]), "mix_norm": fm(a["mix_norm"][0]), "ffn2_norm": fm(a["ffn2_norm"][0]),
          "final_norm": fm(a["final_norm"][0]),
          "conv_w": a["conv_w"][0].reshape(12, 128, 5).transpose(1, 0, 2).reshape(128, 60),
          "gdn_norm_w": fm(a["gdn_norm_w"][0]), "q_norm_w": np.tile(a["q_norm_w"][0], 2)[:, None],
          "k_norm_w": np.tile(a["k_norm_w"][0], 2)[:, None],
          "dt_bias": np.broadcast_to(a["dt_bias"][0].reshape(1, 8), (128, 8)),
          "a_log": np.broadcast_to(a["a_log"][0].reshape(1, 8), (128, 8)),
          "g_final": fm(a["g_final_2"]),
          "cc": np.stack([fm(a["c_2"][0]), fm(a["c_ctx_2"])], axis=2).reshape(128, 16)}
    for l in range(2):
        for name, src in (("b_ada", "b_ada_2"), ("g_ffn1", "g_ffn1_2"), ("g_mix", "g_mix_2"), ("g_ffn2", "g_ffn2_2"),
                          ("b_dw", "b_dw_2"), ("ln_g", "ln_g_conv_2"), ("ln_b", "ln_b_conv_2"), ("b_pw", "b_pw_conv_2"),
                          ("g_q", "g_qnorm_2"), ("g_kv", "g_kvnorm_2"), ("b_f", "b_fourier_2"), ("b_bg", "b_bgate_2")):
            c1[f"{name}{l}"] = fm(a[src][l])
        c1[f"w_dw{l}"] = a["w_dw_2"][l].T.reshape(3, 128, 31).transpose(1, 0, 2).reshape(128, 93)
    COL, ncol = columns()
    cols = np.empty((128, ncol), np.float32)
    for name, (at, n) in COL.items():
        cols[:, at:at + n] = c1[name]
    strip = a["rel_bias"][t5_buckets()]
    idx = np.clip(np.arange(384)[None, :] - 128 - np.arange(128)[:, None], -255, 255) + 255
    bias = np.ascontiguousarray(strip[idx].transpose(0, 2, 1))
    xt = a["x"][0].T.reshape(8, 128, 256).transpose(1, 0, 2)
    ct = a["ctx_2"][0].T.reshape(8, 128, 256).transpose(1, 0, 2)
    xin = np.ascontiguousarray(np.concatenate([xt, ct], axis=2).reshape(128, 4096))
    return {"in_w": stream, "in_cols": cols, "in_bias": bias, "in_x": xin,
            "in_consts": np.concatenate(list(const_blocks().values()), axis=1),
            "in_consts2": np.concatenate(list(const_blocks2().values()), axis=1)}


def kernel(**inputs):
    import concourse.bacc as bacc
    from concourse.bass_utils import run_bass_kernel_spmd

    arrays = host_arrays(inputs)
    nc = bacc.Bacc("TRN2", target_bir_lowering=False, num_devices=1)
    ap = {n: nc.dram_tensor(n, v.shape, F32, kind="ExternalInput").ap() for n, v in arrays.items()}
    out = nc.dram_tensor("out_x", (128, 2048), F32, kind="ExternalOutput").ap()
    build(nc, ap["in_w"], ap["in_cols"], ap["in_consts"], ap["in_consts2"], ap["in_bias"], ap["in_x"], out)
    r = run_bass_kernel_spmd(nc, [arrays], core_ids=[0])
    y = r.results[0]["out_x"].reshape(128, 8, 256).transpose(2, 1, 0).reshape(1, 256, 1024)
    return np.ascontiguousarray(y)
```

```python
import math
from contextlib import ExitStack

import numpy as np

import concourse.bass as bass
from concourse import mybir

F32 = mybir.dt.float32
F32R = mybir.dt.float32r
ALU = mybir.AluOpType
ACT = mybir.ActivationFunctionType
AX = mybir.AxisListType.X

D, T, FF = 1024, 256, 2816
NF = FF // 128
EPS = 1e-6
UC = 1024
NR, NH, AHEAD = 4, 3, 2

TAPS, WIDTH, WIDTH1 = (3, 4), 8, 6
FILL = {"mix1": 3, "swa": 20, "gdn": 16, "f2": 3, "f10": 6, "in_f10": 0, "conv0": 4, "lat0": 2, "head0": 4, "f20": 4,
        "f11": 4, "in_f11": 20, "conv1": 4, "lat1": 2, "head1": 1, "f21": 0}

COLS1 = [("ffn1_norm", 8), ("mix_norm", 8), ("ffn2_norm", 8), ("final_norm", 8), ("conv_w", 60),
         ("gdn_norm_w", 1), ("q_norm_w", 1), ("k_norm_w", 1), ("dt_bias", 8), ("a_log", 8)]
COLS2 = [("b_ada", 72), ("g_ffn1", 8), ("g_mix", 8), ("g_ffn2", 8), ("w_dw", 93), ("b_dw", 3), ("ln_g", 3),
         ("ln_b", 3), ("b_pw", 8), ("g_q", 3), ("g_kv", 2), ("b_f", 8), ("b_bg", 24)]


def columns():
    at, out = 0, {}
    for name, n in COLS1 + [(f"{name}{l}", n) for l in range(2) for name, n in COLS2] + [("g_final", 8), ("cc", 16)]:
        out[name] = (at, n)
        at += n
    return out, at


def pieces():
    adas = iter([(l, m, k) for l in range(2) for m in range(18) for k in range(0, 8, 2)])

    def fill(n, name):
        for l, m, k in [next(adas) for _ in range(n)]:
            yield [(f"{name}{l}", k, 512 * m, 512), (f"{name}{l}", k + 1, 512 * m, 512)]

    def ffn(p, between, beside=0):
        yield [(p + x, k, 0, 128) for k in range(8) for x in "gu"]
        yield from fill(between, "adr")
        for j in range(1, NF):
            yield from fill(j <= beside, "ada")
            yield [(p + "g", k, 128 * j, 128) for k in range(8)]
            yield [(p + "u", k, 128 * j, 128) for k in range(8)]
        for m in range(8):
            yield [(p + "d", k, 128 * m, 128) for k in range(NF)]

    yield from ffn("f1", 0)
    yield [("win", k, 128 * j, 128) for k in range(8) for j in range(2)]
    yield from fill(FILL["mix1"], "adr")
    for j in range(2, 12):
        yield [("win", k, 128 * j, 128) for k in range(8)]
        if j < 10:
            c = 128 * (12 + (j - 2) // 2) if j % 2 == 0 else 2064 + 128 * (8 + (j - 3) // 2)
            yield [("win", k, c, 128) for k in range(8)]
    yield [("win", k, 2048, 16) for k in range(8)]
    for j in range(8):
        yield [("win", k, 2064 + 128 * j, 128) for k in range(8)]
    yield from fill(FILL["swa"], "adr")
    yield from fill(FILL["gdn"], "adr")
    for m in range(8):
        yield [("wout", k, 128 * m, 128) for k in range(8)]
    yield from ffn("f2", FILL["f2"])
    for l in range(2):
        yield from ffn(f"f1{l}", FILL[f"f1{l}"], FILL[f"in_f1{l}"])
        yield [(f"win{l}", k, c, 128) for k in range(8) for c in (384, 0)]
        yield from fill(FILL[f"conv{l}"], "adr")
        for c in range(1, 3):
            yield [(f"win{l}", k, 384 + 128 * c, 128) for k in range(8)]
            yield [(f"win{l}", k, 128 * c, 128) for k in range(8)]
        for j in range(5):
            yield from fill(FILL[f"lat{l}"], "adr")
            yield [(f"win{l}", k, 768 + 128 * j, 128) for k in range(8)]
        yield [(f"wkr{l}", k, 0, 96) for k in range(8)]
        yield [(f"wv{l}", k, 0, 512) for k in range(2)]
        for h in range(8):
            if l and h % 2:
                yield [(f"win{l}", k, 1440 + 128 * (h // 2), 128) for k in range(8)]
            yield from fill(FILL[f"head{l}"], "adr")
            yield [(f"wuq{l}", k, 96 * h, 96) for k in range(3)] + [(f"wkn{l}", k, 96 * h, 96) for k in range(2)]
        for j in range(0 if l else 4):
            yield [(f"win{l}", k, 1440 + 128 * j, 128) for k in range(8)]
        for m in range(8):
            yield [(f"wbg{l}", k, 128 * m, 128) for k in range(8)]
            yield [(f"wbg{l}", k, 1024 + 128 * m, 128) for k in range(8)]
            yield [(f"wbg{l}", k, 2048 + 128 * m, 128) for k in range(8)]
            yield [(f"wpw{l}", k, 128 * m, 128) for k in range(3)] + [(f"wo{l}", k, 128 * m, 128) for k in range(4)]
            yield [(f"wf{l}", k, 128 * m, 128) for k in range(4)]
        for m in range(8):
            yield [(f"wout{l}", k, 128 * m, 128) for k in range(8)]
        yield from ffn(f"f2{l}", FILL[f"f2{l}"])
    assert next(adas, None) is None


def plan():
    units, at = [], 0
    for group in pieces():
        unit, n = [], 0
        for p in group:
            if n + p[3] > UC:
                units.append((at, n, unit))
                at, unit, n = at + 128 * n, [], 0
            unit.append((p, n))
            n += p[3]
        units.append((at, n, unit))
        at += 128 * n
    return units, at


def const_blocks():
    p, f = np.arange(128)[:, None], np.arange(128)[None, :]
    out = {"ident": p == f, "ones": np.ones((128, 128)),
           "LE": p <= f, "GE": p >= f, "GT": p > f, "LT": p < f}
    for l in range(7):
        s = 1 << l
        low = ((p // (2 * s)) == (f // (2 * s))) & ((p // s) % 2 == 1) & ((f // s) % 2 == 0)
        out[f"ML{l}"], out[f"MU{l}"] = low, low.T
    x = np.arange(384)[None, :] - 128 - p
    n = (np.abs(x) <= 64).astype(np.float32) + (x % 4 == 0) + (x % 16 == 0)
    out["bd"] = (p // 64) == (f // 64)
    out["mult"] = n
    out["amask"] = np.where(n > 0, 0.0, -1e30)
    return {k: np.asarray(v, np.float32) for k, v in out.items()}


def const_blocks2():
    out = {}
    rot = np.zeros((128, 128))
    for a in range(2):
        for i in range(8):
            lo, hi = 64 + 16 * a + i, 64 + 16 * a + 8 + i
            rot[hi, lo] = -1.0
            rot[lo, hi] = 1.0
    out["rot"] = rot
    t = np.arange(T)
    inv = (1.0 / (np.float32(10000.0) ** (np.arange(8, dtype=np.float32) * np.float32(2.0) / np.float32(16)))).astype(np.float32)
    ar, ac = ((t // 64).astype(np.float32)[:, None] * inv), ((t % 64).astype(np.float32)[:, None] * inv)
    ang = np.concatenate([ar, ar, ac, ac], axis=1).astype(np.float32)
    cos, sin = np.zeros((128, T), np.float32), np.zeros((128, T), np.float32)
    cos[:64] = 1.0
    cos[64:96], sin[64:96] = np.cos(ang).T, np.sin(ang).T
    out["cos"], out["sin"] = cos, sin
    a = 2 * np.pi * np.outer(np.arange(128), np.arange(128)) / 128
    out["cs"] = np.concatenate([np.cos(a), np.sin(a)], axis=1)
    b = 2 * np.pi * np.outer(t, t) / T
    s = 1.0 / math.sqrt(T * 128)
    out["ct"] = (np.cos(b) * s).reshape(2, 128, T).transpose(1, 0, 2).reshape(128, 2 * T)
    out["st"] = (-np.sin(b) * s).reshape(2, 128, T).transpose(1, 0, 2).reshape(128, 2 * T)
    return {k: np.asarray(v, np.float32) for k, v in out.items()}


def t5_buckets():
    rel = np.arange(-255, 256)
    n = np.abs(rel)
    large = 8 + (np.log(np.maximum(n, 1) / 8) / math.log(1024 / 8) * 8).astype(np.int32)
    return (rel > 0).astype(np.int32) * 16 + np.where(n < 8, n, np.minimum(large, 15))


class Slot:

    def __init__(self, ap):
        self.ap, self.free, self.held = ap, [], False

    def done(self, *toks):
        self.free, self.held = list(toks), False


class Ring:
    def __init__(self, aps):
        self.slots, self.n = [Slot(a) for a in aps], 0

    def get(self):
        while self.slots[self.n % len(self.slots)].held:
            self.n += 1
            assert not all(s.held for s in self.slots)
        s = self.slots[self.n % len(self.slots)]
        self.n += 1
        s.held = True
        return s

    def room(self, n=1):
        while sum(not s.held for s in self.slots) < n:
            yield


def rounds(gens, width, start=8):
    gens, active = iter(gens), []
    for turns in range(5000):
        for _ in range(min(start, width - len(active))):
            g = next(gens, None)
            if g is not None:
                active.append(g)
        if not active:
            return
        for g in list(active):
            if next(g, active) is active:
                active.remove(g)
        yield
    assert False, "no generator comes on"


def run(*gens, width=3):
    for _ in rounds(gens, width):
        pass


def beside(main, *others):
    run(main, *others, width=1 + len(others))


class Prog:

    def __init__(self, nc, stack):
        self.nc, self.stack = nc, stack
        self.q = {e: [] for e in ("pe", "act", "dve", "pool", "sp")}
        self.count = dict.fromkeys(self.q, 0)
        self.seen = {}
        self.sems = {}
        self.table = None
        for e in ("pe", "act", "dve", "pool"):
            self.sem(e)

    def sem(self, name):
        if name not in self.sems:
            self.sems[name] = self.stack.enter_context(self.nc.semaphore("s_" + name))
            self.count[name] = 0
        return name

    def wait(self, e, toks):
        for t in toks:
            if t is None:
                continue
            if isinstance(t, list):
                self.wait(e, t)
                continue
            name, value = t
            if self.seen.get((e, name), 0) < value:
                self.seen[e, name] = value
                self.q[e].append(lambda eng, s=self.sems[name], v=value: eng.wait_ge(s, v))

    def do(self, e, fn, *toks, sig=True):
        self.wait(e, toks)
        if sig:
            self.count[e] += 1
            self.q[e].append(lambda eng, s=self.sems[e]: fn(eng).then_inc(s, 1))
        else:
            self.q[e].append(fn)
        return (e, self.count[e])

    def dma(self, out, in_, name, *toks, e="sp"):
        self.wait(e, toks)
        self.sem(name)
        self.count[name] += 16
        self.q[e].append(lambda eng, s=self.sems[name]: eng.dma_start(out, in_).then_inc(s, 16))
        return (name, self.count[name])

    def exp_table(self):
        if self.table != "exp":
            self.q["act"].append(lambda eng: eng.preload_act_table_set("natural_log_exp_and_others"))
        self.table = "exp"

    def act(self, out, in_, f, *toks, **kw):
        if f in (ACT.Exp, ACT.Ln):
            self.exp_table()
        elif f in (ACT.Silu, ACT.Sigmoid):
            self.table = f
        return self.do("act", lambda g: g.activation(out, in_, f, **kw), *toks)

    def tt(self, e, out, a, b, op, *toks):
        return self.do(e, lambda g: g.tensor_tensor(out, a, b, op), *toks)

    def ts(self, e, out, a, s1, s2, op0, op1, *toks):
        if s2 is None:
            return self.do(e, lambda g: g.tensor_scalar(out, a, s1, None, op0), *toks)
        return self.do(e, lambda g: g.tensor_scalar(out, a, s1, s2, op0, op1), *toks)

    def stt(self, out, a, s, b, op0, op1, *toks):
        return self.do("dve", lambda g: g.scalar_tensor_tensor(out=out, in0=a, scalar=s, in1=b, op0=op0, op1=op1), *toks)

    def copy(self, e, out, in_, *toks):
        return self.do(e, lambda g: g.tensor_copy(out, in_), *toks)

    def ttr(self, out, a, b, init, op0, op1, acc, *toks):
        return self.do("dve", lambda g: g.tensor_tensor_reduce(out, a, b, 1.0, init, op0, op1, acc), *toks)

    def rmax(self, out, in_, *toks):
        return self.do("dve", lambda g: g.tensor_reduce(out, in_, AX, ALU.max), *toks)

    def recip(self, out, in_, *toks):
        return self.do("dve", lambda g: g.reciprocal(out, in_), *toks)

    def mm(self, out, w, x, start, stop, *toks, sig=None):
        return self.do("pe", lambda g: g.matmul(out, w, x, start=start, stop=stop), *toks,
                       sig=stop if sig is None else sig)

    def tr(self, out, in_, ident, *toks, sig=True):
        return self.do("pe", lambda g: g.transpose(out, in_, ident), *toks, sig=sig)

    def flush(self):
        nc, q = self.nc, self.q
        with nc.Block() as block:
            @block.sync
            def _(eng):
                for f in q["sp"]:
                    f(eng)

            @block.scalar
            def _(eng):
                for f in q["act"]:
                    f(eng)

            @block.vector
            def _(eng):
                for f in q["dve"]:
                    f(eng)

            @block.gpsimd
            def _(eng):
                for f in q["pool"]:
                    f(eng)

            @block.tensor
            def _(eng):
                for f in q["pe"]:
                    f(eng)


class Weights:

    def __init__(self, P, dram):
        self.P, self.dram = P, dram
        self.units, _ = plan()
        e = P.stack.enter_context
        self.raw = e(P.nc.sbuf_tensor("w_raw", [128, NR, UC], F32))
        self.hi = e(P.nc.sbuf_tensor("w_hi", [128, NH, UC], F32R))
        self.lo = e(P.nc.sbuf_tensor("w_lo", [128, NH, UC], F32R))
        self.loaded, self.raw_free, self.landed = 0, {}, {}
        self.nsplit, self.split_tok, self.pe_done = 0, {}, {}
        self.u, self.i, self.cuts, self.slot = 0, 0, [], {}
        for _ in range(NR):
            self.load()

    def head(self):
        return self.units[self.u][2][self.i][0]

    def kind(self, u):
        return self.units[u][2][0][0][0][:3] if u < len(self.units) else None

    def pump(self):
        while self.loaded < len(self.units) and self.loaded - NR in self.raw_free:
            self.load()

    def load(self):
        u = self.loaded
        at, n, _ = self.units[u]
        src = bass.AP(tensor=self.dram.tensor, offset=at, ap=[[n, 128], [1, n]])
        free = self.raw_free[u - NR] if u >= NR else None
        self.landed[u] = self.P.dma(self.raw[:, u % NR, 0:n], src, f"w{u % NR}", free)
        self.loaded += 1

    def split(self):
        u = self.nsplit
        if u >= len(self.units):
            return
        if self.kind(u) == "adr":
            self.nsplit += 1
            return
        s, n = len(self.cuts) % NH, self.units[u][1]
        raw, hi, lo = self.raw[:, u % NR, 0:n], self.hi[:, s, 0:n], self.lo[:, s, 0:n]
        reader = self.pe_done[self.cuts[-NH]] if len(self.cuts) >= NH else None
        self.cuts.append(u)
        self.slot[u] = s
        a = self.P.act(hi, raw, ACT.Copy, self.landed[u], reader)
        b = self.P.tt("dve", lo, raw, hi.bitcast(F32), ALU.subtract, a)
        self.split_tok[u] = b
        self.raw_free[u] = b
        self.nsplit += 1
        self.pump()

    def ahead(self):
        while self.nsplit < min(self.u + AHEAD + 1, len(self.units)) and self.nsplit in self.landed and (
                len(self.cuts) < NH or self.cuts[-NH] in self.pe_done):
            self.split()

    def next(self, key):
        at, n, ps = self.units[self.u]
        p, c = ps[self.i]
        assert p == key, (p, key)
        u, m, last = self.u, p[3], self.i == len(ps) - 1
        if self.i == 0:
            self.ahead()
        if self.kind(u) == "adr":
            out = (self.raw[:, u % NR, c:c + m], None, self.landed[u], last)
        else:
            s = self.slot[u]
            out = (self.hi[:, s, c:c + m], self.lo[:, s, c:c + m], self.split_tok[u], last)
        self.i += 1
        if last:
            self.u, self.i, self.last = u + 1, 0, u
        return out

    def release(self, tok, u=None):
        u = self.last if u is None else u
        self.pe_done[u] = tok
        if self.kind(u) == "adr":
            self.raw_free[u] = tok
            self.pump()


def build(nc, wstream, cols, consts, consts2, bias, xin, out):
    with ExitStack() as stack:
        P = Prog(nc, stack)
        program(P, nc, stack, wstream, cols, consts, consts2, bias, xin, out)
        P.flush()


def program(P, nc, stack, wstream, cols, consts, consts2, bias, xin, out):
    ent = stack.enter_context

    def sb(name, shape, dt=F32, st=None):
        return (st or stack).enter_context(nc.sbuf_tensor(name, shape, dt))

    X = sb("X", [128, 8, 512])
    UH, UL = sb("UH", [128, 8, 512], F32R), sb("UL", [128, 8, 512], F32R)
    COL, ncol = columns()
    PC = sb("PC", [128, ncol])
    C1 = sb("C1", [128, 256])
    ident, ones = C1[:, 0:128], C1[:, 128:256]
    tmp = sb("TMP", [128, 7, 512])
    TM = Ring([tmp[:, i, :] for i in range(7)])
    ssb = sb("SSB", [128, 3, 512])
    SSR, RBR = Ring([ssb[:, 0, :]]), Ring([ssb[:, i, :] for i in (1, 2)])
    small = sb("SMALL", [128, 8, 8])
    SM = Ring([small[:, i, :] for i in range(8)])
    MOD = sb("MOD", [128, 2, 72, 2])
    MP = GP = Ring([ent(nc.psum_tensor(f"B{i}", [128, 512], F32))[:] for i in range(8)])

    def col(name, k=0, n=1):
        at, _ = COL[name]
        return PC[:, at + k:at + k + n]

    xs = xin.rearrange("p (c t) -> p c t", c=8)
    xload = P.dma(X[:, :, 0:256], xs[:, :, 0:256], "x")
    cload = P.dma(PC[:], cols, "cols")
    c1load = P.dma(C1[:], consts[:, 0:256], "c1")
    W = Weights(P, wstream)
    xload2 = P.dma(X[:, :, 256:512], xs[:, :, 256:512], "x2")

    def every(*engines):
        return [(e, P.count[e]) for e in engines]

    def fetch(keys):
        return [(W.next(key), W.last if W.i == 0 else None) for key in keys]

    def pair(pieces, n, ready):
        gs = [GP.get(), GP.get()]
        for i, ((wh, wl, rdy, last), u) in enumerate(pieces):
            g, k = gs[i % 2], i // 2
            P.mm(g.ap[:, 0:n], wh, UH[:, k, 0:n], k == 0, False, rdy, g.free, ready[k], sig=False)
            P.mm(g.ap[:, 0:n], wh, UL[:, k, 0:n], False, False, sig=False)
            t = P.mm(g.ap[:, 0:n], wl, UH[:, k, 0:n], False, k == 7, sig=True)
            if last:
                W.release(t, u)
        W.ahead()
        return [(g, g.ap[:, 0:n], t) for g in gs]

    def turn(key):
        while W.head() != key:
            ada.advance()
            ada.fill(1)
            yield

    def gemm(keys, xh, xl, m, n, *toks, each=None):
        ada.advance()
        ada.fill()
        g = GP.get()
        ps = g.ap[0:m, 0:n]
        for i, key in enumerate(keys):
            wh, wl, ready, last = W.next(key)
            first, end = i == 0, i == len(keys) - 1
            P.mm(ps, wh, xh(i), first, False, ready, *toks, g.free, each and each[i], sig=False)
            P.mm(ps, wh, xl(i), False, False, sig=False)
            t = P.mm(ps, wl, xh(i), False, end, sig=end or last)
            if last:
                W.release(t)
        return g, ps, t

    def cut(hi, lo, src, *toks):
        a = P.act(hi, src, ACT.Copy, *toks)
        b = P.tt("dve", lo, src, hi.bitcast(F32), ALU.subtract, a)
        return a, b

    class Stat:

        def __init__(self, n):
            self.s, self.n, self.tok, self.late = SSR.get(), n, None, None

        def add(self, ap, *toks):
            if self.tok is None:
                self.tok = P.act(self.s.ap[:, 0:self.n], ap, ACT.Square, self.s.free, *toks)
                return self.tok
            self.settle()
            t = TM.get()
            a = P.act(t.ap[:, 0:self.n], ap, ACT.Square, t.free, *toks)
            self.late = (t, a)
            return a

        def settle(self):
            if self.late:
                t, a = self.late
                self.tok = P.tt("dve", self.s.ap[:, 0:self.n], self.s.ap[:, 0:self.n], t.ap[:, 0:self.n], ALU.add,
                                a, self.tok)
                t.done(self.tok)

        def rsqrt(self, count, ring=RBR, between=0):
            m, r, n = MP.get(), ring.get(), self.n
            t, a = self.late
            P.mm(m.ap[:, 0:n], ones, self.s.ap[:, 0:n], True, False, self.tok, m.free, c1load)
            ada.fill(between and 1)
            a = P.mm(m.ap[:, 0:n], ones, t.ap[:, 0:n], False, True, a)
            self.s.done(a)
            t.done(a)
            b, m_free = rsqrt(r.ap[:, 0:n], m.ap[:, 0:n], 1.0 / count, a, r.free)
            m.done(m_free)
            if between:
                ada.fill(between - 1)
            return r, b

    def rsqrt(out_, ps, scale, *toks):
        a = P.act(out_, ps, ACT.Ln, *toks, scale=scale, bias=EPS)
        return P.act(out_, out_, ACT.Exp, a, scale=-0.5), a

    def norm_to_u(r, rtok, gcol, n, *toks):
        ready, work = [], []

        def low():
            k, t, b = work.pop(0)
            ready.append(P.tt("dve", UL[:, k, 0:n], t.ap[:, 0:n], UH[:, k, 0:n].bitcast(F32), ALU.subtract, b))
            t.done(ready[-1])

        for k in range(8):
            t = TM.get()
            a = P.stt(t.ap[:, 0:n], X[:, k, 0:n], gcol(k), r.ap[:, 0:n], ALU.mult, ALU.mult, rtok, t.free, cload)
            work.append((k, t, P.act(UH[:, k, 0:n], t.ap[:, 0:n], ACT.Copy, a, *toks)))
            if k:
                low()
            if k == 5:
                W.ahead()
        low()
        r.done(a)
        return ready

    def ada_to_u(r, rtok, A, B, n, *toks):
        ready, work = [], []

        def low():
            k, t, b = work.pop(0)
            for s in range(n // 256):
                c = slice(256 * s, 256 * s + 256)
                d = P.stt(UL[:, k, c], t.ap[:, c], B(k, s), UH[:, k, c].bitcast(F32), ALU.add, ALU.subtract, b[s])
            t.done(d)
            ready.append(d)

        for k in range(8):
            t, b = TM.get(), []
            for s in range(n // 256):
                c = slice(256 * s, 256 * s + 256)
                a = P.stt(t.ap[:, c], X[:, k, c], A(k, s), r.ap[:, c], ALU.mult, ALU.mult, rtok, t.free, list(toks))
                b.append(P.act(UH[:, k, c], t.ap[:, c], ACT.Identity, a, *toks, bias=B(k, s)))
            work.append((k, t, b))
            if k:
                low()
            if k == 5:
                W.ahead()
        low()
        r.done(a)
        return ready

    uh = lambda n, s=0: (lambda k: UH[:, k, s:s + n])
    ul = lambda n, s=0: (lambda k: UL[:, k, s:s + n])

    def first_of(pre):
        return [(pre + x, k, 0, 128) for k in range(8) for x in "gu"]

    def ffn(pre, n, pieces, ready, gate, tag):
        with ExitStack() as st:
            HH, HL = sb("HH" + tag, [128, NF, n], F32R, st), sb("HL" + tag, [128, NF, n], F32R, st)
            cuts = []
            old = every("pe", "act", "dve", "pool")
            for j in range(NF):
                if j == 0:
                    (gg, pg, tg), (gu, pu, tu) = pair(pieces, n, ready)
                else:
                    gg, pg, tg = gemm([(pre + "g", k, 128 * j, 128) for k in range(8)], uh(n), ul(n), 128, n)
                    gu, pu, tu = gemm([(pre + "u", k, 128 * j, 128) for k in range(8)], uh(n), ul(n), 128, n)
                t = TM.get()
                h = t.ap[:, 0:n]
                a = P.act(h, pg, ACT.Silu, tg, t.free)
                gg.done(a)
                b = P.tt("dve", h, h, pu, ALU.mult, a, tu)
                gu.done(b)
                c, d = cut(HH[:, j, :], HL[:, j, :], h, b, old)
                t.done(d)
                cuts.append(d)
            P.exp_table()
            stat = Stat(n)
            for m in range(8):
                g, ps, t = gemm([(pre + "d", k, 128 * m, 128) for k in range(NF)], lambda k: HH[:, k, :],
                                lambda k: HL[:, k, :], 128, n, each=cuts)
                xt = add_to_x(m, ps, n, gate, t)
                g.done(xt)
                stat.add(X[:, m, 0:n], xt)
            return stat, xt

    def add_to_x(m, ps, n, gate, tok):
        if gate is None:
            return P.stt(X[:, m, 0:n], ps, 0.5, X[:, m, 0:n], ALU.mult, ALU.add, tok)
        for s in range(n // 256):
            c = slice(256 * s, 256 * s + 256)
            a = P.stt(X[:, m, c], ps[:, c], gate(m, s), X[:, m, c], ALU.mult, ALU.add, tok)
        return a

    ada = Modulation(P, W, MP, MOD, col, TM, sb, ident, cload, c1load, cut)

    stat = Stat(256)
    for k in range(8):
        stat.add(X[:, k, 0:256], xload)
    first = fetch(first_of("f1"))
    r, rt = stat.rsqrt(D)
    ready = norm_to_u(r, rt, lambda k: col("ffn1_norm", k), 256)
    stat, xt = ffn("f1", 256, first, ready, None, "a")

    first = fetch([("win", k, 128 * j, 128) for k in range(8) for j in range(2)])
    r, rt = stat.rsqrt(D, between=FILL["mix1"])
    ready = norm_to_u(r, rt, lambda k: col("mix_norm", k), 256, every("pe"))
    mix1(P, nc, stack, sb, W, gemm, pair, turn, ada, cut, rsqrt, every, col, TM, MP, GP, SM, RBR, SSR, X, UH, UL, uh, ul,
         ready, consts, bias, ident, ones, cload, c1load, MOD, first)
    stat = Stat(256)
    oready = every("act", "dve")
    for m in range(8):
        g, ps, t = gemm([("wout", k, 128 * m, 128) for k in range(8)], uh(256), ul(256), 128, 256, oready)
        a = P.tt("dve", X[:, m, 0:256], X[:, m, 0:256], ps, ALU.add, t)
        g.done(a)
        stat.add(X[:, m, 0:256], a)
    first = fetch(first_of("f2"))
    r, rt = stat.rsqrt(D, between=FILL["f2"])
    ready = norm_to_u(r, rt, lambda k: col("ffn2_norm", k), 256, every("pe"))
    stat, xt = ffn("f2", 256, first, ready, None, "b")
    first = fetch(first_of("f10"))
    r, rt = stat.rsqrt(D, between=FILL["f10"] // 2)
    old = every("act")
    for k in range(8):
        a = P.stt(X[:, k, 0:256], X[:, k, 0:256], col("final_norm", k), r.ap[:, 0:256], ALU.mult, ALU.mult, rt, old, xt)
    r.done(a)
    block2(P, nc, stack, sb, W, gemm, pair, turn, ada, cut, rsqrt, every, col, TM, MP, GP, SM, RBR, SSR, X, UH, UL, uh, ul,
           consts2, ident, ones, MOD, Stat, ffn, ada_to_u, add_to_x, a, out, fetch, first_of, first, xload2)


def mix1(P, nc, stack, sb, W, gemm, pair, turn, ada, cut, rsqrt, every, col, TM, MP, GP, SM, RBR, SSR, X, UH, UL, uh, ul,
         ready, consts, bias, ident, ones, cload, c1load, MOD, first):
    names = list(const_blocks())
    with ExitStack() as st:
        def tile(name, shape, dt=F32):
            return sb(name, shape, dt, st)

        CN = tile("CN", [128, 18 * 128])
        old = every("pe", "act", "dve")
        cn = P.dma(CN[:], consts[:, 256:2560], "cn", old, e="pool")

        def C(name):
            i = names.index(name) - 2
            return CN[:, 128 * i:128 * i + 128]

        CQ = tile("CQ", [128, 12, 256])
        ZG = tile("ZG", [128, 4, 256])
        KT, VT = tile("KT", [128, 2, 512]), tile("VT", [128, 2, 512])
        OS = tile("OS", [128, 4, 256])
        G, BETA = tile("G", [128, 2, 8]), tile("BETA", [128, 2, 8])
        GA = tile("GA", [128, 6, 16])
        win = lambda c, m=128: [("win", k, c, m) for k in range(8)]

        qk, kv, qn, vb, uq = [], [], [None] * 8, [], []
        with ExitStack() as s2:
            CV = sb("CV", [128, 12, 260], F32, s2)
            QB = sb("QB", [128, 8, 256], F32, s2)
            VB = sb("VB", [128, 2, 512], F32, s2)
            BW = sb("BW", [128, 8, 384], F32, s2)
            PT = sb("PT", [128, 3, 2, 256], F32, s2)
            CB = sb("CB", [128, 128 + 768], F32, s2)
            bd, mult, amask = CB[:, 0:128], CB[:, 128:512], CB[:, 512:896]
            PTR = Ring([PT[:, i] for i in range(3)])
            cbl = P.dma(CB[:], consts[:, 2560:3456], "cb", old, e="pool")
            bl = P.dma(BW[:], bias, "bw", old, e="pool")
            pads = [P.do("pool", lambda g: g.memset(CV[:, :, 0:2], 0.0), old),
                    P.do("pool", lambda g: g.memset(CV[:, :, 258:260], 0.0))]
            bw = P.tt("pool", BW[:], BW[:], amask.unsqueeze(1).broadcast_to([128, 8, 384]), ALU.add, bl, cbl)
            done, zts = [None] * 12, []
            first = pair(first, 256, ready)

            def conv(j):
                if j > 1:
                    yield from turn(win(128 * j)[0])
                    yield from MP.room()
                g, ps, t = first[j] if j < 2 else gemm(win(128 * j), uh(256), ul(256), 128, 256)
                a = P.act(CV[:, j, 2:258], ps, ACT.Copy, t, old)
                g.done(a)
                yield
                yield from TM.room()
                acc = TM.get()
                o = acc.ap[:, 0:256]
                b = P.act(o, CV[:, j, 0:256], ACT.Copy, a, acc.free, pads, scale=col("conv_w", 5 * j))
                for i in range(1, 5):
                    b = P.stt(o, CV[:, j, i:i + 256], col("conv_w", 5 * j + i), o, ALU.mult, ALU.add, b)
                yield
                c = P.act(CQ[:, j, :], o, ACT.Silu, b, old)
                acc.done(c)
                done[j] = c

            def gates(h):
                yield from turn(win(128 * (12 + h))[0])
                yield from MP.room()
                g, ps, t = gemm(win(128 * (12 + h)), uh(256), ul(256), 128, 256)
                yield
                zts.append(P.act(ZG[:, h, :], ps, ACT.Silu, t))
                g.done(zts[-1])

            made = {}

            def decay():
                yield from turn(win(2048, 16)[0])
                yield from MP.room()
                pc = [W.next(k) for k in win(2048, 16)]
                g = GP.get()
                for i in range(2):
                    for k in range(8):
                        wh, wl, rdy, _ = pc[k]
                        x = slice(128 * i, 128 * i + 128)
                        o = g.ap[:, 16 * i:16 * i + 16]
                        P.mm(o, UH[:, k, x], wh, k == 0, False, rdy, g.free, sig=False)
                        P.mm(o, UH[:, k, x], wl, False, False, sig=False)
                        t = P.mm(o, UL[:, k, x], wh, False, k == 7)
                W.release(t)
                yield
                AB = g.ap[:, 0:32].rearrange("p (i c) -> p i c", i=2)
                a = [GA[:, i, :].rearrange("p (i c) -> p i c", i=2) for i in range(6)]
                row = lambda name: col(name, 0, 8).unsqueeze(1).broadcast_to([128, 2, 8])
                t1 = P.tt("dve", a[0], AB[:, :, 0:8], row("dt_bias"), ALU.add, t, old)
                t2 = P.act(a[1], a[0], ACT.Abs, t1)
                t3 = P.act(a[2], a[1], ACT.Exp, t2, scale=-1.0)
                t4 = P.act(a[2], a[2], ACT.Ln, t3, bias=1.0)
                t5 = P.act(a[3], row("a_log"), ACT.Exp)
                t6 = P.act(a[4], AB[:, :, 8:16], ACT.Exp, scale=-1.0)
                g.done(t1, t6)
                yield
                t7 = P.ts("dve", a[0], a[0], 0.0, None, ALU.max, None, t2)
                t8 = P.tt("dve", a[0], a[0], a[2], ALU.add, t4, t7)
                t9 = P.ts("dve", a[0], a[0], -1.0, None, ALU.mult, None, t8)
                made["g"] = P.tt("dve", G[:], a[0], a[3], ALU.mult, t9, t5)
                t11 = P.ts("dve", a[4], a[4], 1.0, None, ALU.add, None, t6)
                made["b"] = P.recip(BETA[:], a[4], t11)

            def unit(c):
                while not all(done[2 * c:2 * c + 2]):
                    yield
                yield from TM.room(2)
                v = CQ[:, 2 * c:2 * c + 2, :]
                s, r = TM.get(), TM.get()
                sq = P.act(s.ap, v, ACT.Square, s.free, done[2 * c], done[2 * c + 1])
                yield
                yield from MP.room()
                m = MP.get()
                mt = P.mm(m.ap, ones, s.ap, True, True, sq, m.free)
                s.done(mt)
                e, f = rsqrt(r.ap, m.ap, 1.0, mt, r.free)
                m.done(f)
                yield
                u = P.stt(v, v, 128 ** -0.5 if c < 2 else 1.0, r.ap.rearrange("p (a b) -> p a b", a=2),
                          ALU.mult, ALU.mult, e)
                r.done(u)
                qk.append(u)

            def by_token(i, base, dst):
                while len(qk) < 4 or not all(done):
                    yield
                yield from MP.room()
                m = MP.get()
                for h in range(4):
                    t = P.tr(m.ap[:, 128 * h:128 * h + 128], CQ[:, base + h, 128 * i:128 * i + 128], ident,
                             m.free, qk, done, sig=h == 3)
                yield
                u = P.copy("dve", dst[:, i, :], m.ap, t, old)
                m.done(u)
                kv.append(u)

            def attn_qk(j):
                yield from turn(win(2064 + 128 * j)[0])
                yield from MP.room(2)
                yield from TM.room(2)
                g, ps, t = gemm(win(2064 + 128 * j), uh(256), ul(256), 128, 256)
                s, r = TM.get(), TM.get()
                sq = P.act(s.ap[:, 0:256], ps, ACT.Square, s.free, t)
                yield
                yield from MP.room()
                m = MP.get()
                mt = P.mm(m.ap[:, 0:256], bd, s.ap[:, 0:256], True, True, sq, m.free, cbl)
                s.done(mt)
                e, f = rsqrt(r.ap[:, 0:256], m.ap[:, 0:256], 1.0 / 64, mt, r.free)
                m.done(f)
                yield
                u = P.stt(QB[:, j, :], ps, col("q_norm_w" if j < 4 else "k_norm_w"), r.ap[:, 0:256],
                          ALU.mult, ALU.mult, e, old)
                if j < 4:
                    u = P.ts("dve", QB[:, j, :], QB[:, j, :], 64 ** -0.5, None, ALU.mult, None, u)
                r.done(u)
                g.done(u)
                qn[j] = u

            def attn_v(j):
                yield from turn(win(2064 + 128 * (8 + j))[0])
                yield from MP.room(2)
                yield from TM.room()
                g, ps, t = gemm(win(2064 + 128 * (8 + j)), uh(256), ul(256), 128, 256)
                s = TM.get()
                u = P.act(s.ap[:, 0:256], ps, ACT.Copy, s.free, t)
                g.done(u)
                yield
                yield from MP.room()
                m = MP.get()
                for i in range(2):
                    tv = P.tr(m.ap[:, 128 * i:128 * i + 128], s.ap[:, 128 * i:128 * i + 128], ident, u, m.free)
                s.done(tv)
                yield
                u = P.act(VB[:, :, 128 * j:128 * j + 128], m.ap[:, 0:256].rearrange("p (i c) -> p i c", i=2), ACT.Copy,
                          tv, old)
                m.done(u)
                vb.append(u)

            def band(c):
                while not all(qn) or len(vb) < 4:
                    yield
                if not uq:
                    uq.extend(every("pe"))
                o, pts = None, []
                for h in (2 * c, 2 * c + 1):
                    b = 64 * (h % 2)
                    yield from MP.room()
                    yield from SM.room()
                    yield from TM.room(2)
                    m, sm = MP.get(), SM.get()
                    for i in range(2):
                        t = P.mm(m.ap[:, 256 * i:256 * i + 256], QB[b:b + 64, c, 128 * i:128 * i + 128],
                                 QB[b:b + 64, 4 + c, :], True, True, qn, m.free)
                    s, y = TM.get(), TM.get()
                    mx = []
                    for i in range(2):
                        w = BW[:, h, 128 * (1 - i):128 * (1 - i) + 256]
                        mx.append(P.ttr(s.ap[:, 256 * i:256 * i + 256], m.ap[:, 256 * i:256 * i + 256], w, -3.0e38,
                                        ALU.add, ALU.max, sm.ap[:, i:i + 1], t, s.free, sm.free, bw))
                    m.done(mx[-1])
                    ng = P.ts("dve", sm.ap[:, 2:4], sm.ap[:, 0:2], -1.0, None, ALU.mult, None, mx)
                    yield
                    ex = []
                    for i in range(2):
                        v = s.ap[:, 256 * i:256 * i + 256]
                        ex.append(P.act(v, v, ACT.Exp, ng, bias=sm.ap[:, 2 + i:3 + i]))
                    yield
                    dn = []
                    for i in range(2):
                        dn.append(P.ttr(y.ap[:, 256 * i:256 * i + 256], s.ap[:, 256 * i:256 * i + 256],
                                        mult[:, 128 * (1 - i):128 * (1 - i) + 256], 0.0, ALU.mult, ALU.add,
                                        sm.ap[:, 4 + i:5 + i], ex, y.free))
                    s.done(dn[-1])
                    rc = P.recip(sm.ap[:, 6:8], sm.ap[:, 4:6], dn)
                    nm = []
                    for i in range(2):
                        v = y.ap[:, 256 * i:256 * i + 256]
                        nm.append(P.ts("dve", v, v, sm.ap[:, 6 + i:7 + i], None, ALU.mult, None, rc))
                    sm.done(nm[-1])
                    yield
                    yield from PTR.room()
                    yield from MP.room()
                    m, pt = MP.get(), PTR.get()
                    for kc in range(2):
                        for i in range(2):
                            t = P.tr(m.ap[:, 256 * kc + 128 * i:256 * kc + 128 * i + 128],
                                     y.ap[:, 256 * i + 128 * kc:256 * i + 128 * kc + 128], ident, nm, m.free)
                    y.done(t)
                    ev = P.act(pt.ap, m.ap.rearrange("p (a b) -> p a b", a=2), ACT.Copy, t, pt.free, old)
                    m.done(ev)
                    yield
                    if not o:
                        yield from MP.room()
                        o = MP.get()
                    for kc in range(2):
                        t = P.mm(o.ap[b:b + 64, 0:256], VB[:, kc, 64 * h:64 * h + 64], pt.ap[:, kc, :],
                                 kc == 0, kc == 1, ev, vb, o.free)
                    pt.done(t)
                yield
                _, u = cut(UH[:, 4 + c, 0:256], UL[:, 4 + c, 0:256], o.ap[:, 0:256], t, uq)
                o.done(u)

            tasks = [conv(0), conv(1)]
            for j in range(2, 12):
                tasks.append(conv(j))
                if j < 10:
                    tasks.append(attn_v((j - 3) // 2) if j % 2 else gates((j - 2) // 2))
            tasks.append(decay())
            for j in range(8):
                tasks.append(attn_qk(j))
                if j % 2:
                    tasks.append(unit(j // 2))
            tasks += [by_token(i, b, d) for i in range(2) for b, d in ((4, KT), (8, VT))]
            tasks += [band(c) for c in range(4)]
            beside(rounds(tasks, WIDTH1, 1), ada.steps(FILL["swa"]))
            gt, bt = made["g"], made["b"]
            swa_done = every("act", "dve", "pe", "pool")

        GT_ = tile("GDN", [128, 4, 7, 512])
        h4 = lambda ap: ap.rearrange("p (h c) -> p h c", h=4)
        bc = lambda ap: ap.unsqueeze(1).broadcast_to([128, 4, 128])
        cb = lambda ap: ap.unsqueeze(2).broadcast_to([128, 4, 128])
        hs = lambda ap, h: ap[:, 128 * h:128 * h + 128]
        S = [CQ[:, 8 + 2 * d:10 + 2 * d, :].rearrange("p a b -> p (a b)") for d in range(2)]
        first_o, state = {}, {}

        def per_head(w, x, *toks, out=None):
            m = MP.get()
            for h in range(4):
                e = P.mm(hs(m.ap, h), w(h), x(h), True, True, *toks, m.free, sig=h == 3)
            return m, e

        def delta(order, d):
            i = order if d == 0 else 1 - order
            n = 2 * order + d
            tri, st_, lm, um = ("LE", "GT", "ML", "MU") if d == 0 else ("GE", "LT", "MU", "ML")
            gq, IT, UU, T_, P_, Y, UL_ = (GT_[:, n, j, :] for j in range(7))
            ck = slice(128 * i, 128 * i + 128)
            gcol, bcol = G[:, i, 4 * d:4 * d + 4], BETA[:, i, 4 * d:4 * d + 4]
            a = P.tt("dve", h4(gq), bc(C(tri)), cb(gcol), ALU.mult, gt, swa_done, cn)
            yield
            m, e = per_head(lambda h: hs(gq, h), lambda h: C(st_), a)
            x = P.act(T_, m.ap, ACT.Exp, e, swa_done)
            m.done(x)
            m = MP.get()
            e = P.mm(m.ap, C(st_), gq, True, True, m.free)
            y = P.act(IT, m.ap, ACT.Exp, e)
            m.done(y)
            m, cols = MP.get(), SM.get()
            P.mm(m.ap[:, 0:4], C(tri), gcol, True, True, m.free, sig=False)
            e = P.mm(m.ap[:, 4:8], C(st_), gcol, True, True)
            colt = P.act(cols.ap, m.ap[:, 0:8], ACT.Exp, e, cols.free)
            m.done(colt)
            q = None
            if order == 1:
                m = MP.get()
                e = P.mm(m.ap, ones, gq, True, True, m.free)
                q = P.act(gq, m.ap, ACT.Exp, e)
                m.done(q)
            yield
            if order == 1:
                q = P.tt("dve", h4(gq), h4(gq), CQ[:, 0:4, ck], ALU.mult, q, qk)
            xs = P.tt("dve", h4(T_), h4(T_), bc(C(st_)), ALU.mult, x)
            ys = P.tt("dve", h4(IT), h4(IT), bc(C(tri)), ALU.mult, y)
            yield
            m, e = per_head(lambda h: CQ[:, 4 + h, ck], lambda h: CQ[:, 4 + h, ck], qk)
            x = P.tt("dve", T_, m.ap, T_, ALU.mult, e, xs)
            m.done(x)
            x = P.tt("dve", h4(T_), h4(T_), cb(bcol), ALU.mult, x, bt)
            yield
            m, e = per_head(lambda h: CQ[:, 4 + h, ck], lambda h: CQ[:, h, ck])
            it = P.tt("dve", IT, m.ap, IT, ALU.mult, e, ys)
            m.done(it)
            yield
            m = MP.get()
            for h in range(4):
                e = P.tr(hs(m.ap, h), hs(T_, h), ident, x, m.free, sig=h == 3)
            uu = P.act(UU, m.ap, ACT.Copy, e, swa_done)
            m.done(uu)
            yield
            p = P.tt("dve", h4(T_), h4(T_), bc(C(lm + "0")), ALU.mult, x, e)
            p = P.tt("dve", h4(T_), bc(ident), h4(T_), ALU.subtract, p)
            w = P.tt("dve", h4(P_), h4(UU), bc(C(um + "0")), ALU.mult, uu)
            w = P.tt("dve", h4(P_), bc(ident), h4(P_), ALU.subtract, w)
            ye, ze = None, None
            for lv in range(1, 7):
                ul_ = P.tt("pool", h4(UL_), h4(UU), bc(C(f"{um}{lv}")), ALU.mult, uu, ye, swa_done)
                yield
                m, ye = per_head(lambda h: hs(UL_, h), lambda h: hs(T_, h), ul_, p)
                y = P.act(Y, m.ap, ACT.Copy, ye, ze, swa_done)
                m.done(y)
                yield
                if lv < 6:
                    m, e = per_head(lambda h: hs(P_, h), lambda h: hs(Y, h), y, w)
                    p = P.tt("dve", T_, T_, m.ap, ALU.subtract, e)
                    m.done(p)
                m, ze = per_head(lambda h: hs(Y, h), lambda h: hs(P_, h), y, w)
                w = P.tt("dve", P_, P_, m.ap, ALU.subtract, ze)
                m.done(w)
            VB_, KD, VN, WT = Y, UL_, T_, UU
            yield
            vbt = P.tt("dve", h4(VB_), h4(VT[:, i, :]), cb(bcol), ALU.mult, kv, ze)
            if order == 1:
                c = P.tt("pool", h4(KD), h4(KT[:, i, :]), cb(bcol), ALU.mult, kv, ye)
                c = P.tt("pool", h4(KD), h4(KD), cb(cols.ap[:, 0:4]), ALU.mult, c, colt)
                cols.done(c)
                yield
                m, e = per_head(lambda h: hs(KD, h), lambda h: hs(P_, h), c, w)
                wt = P.act(WT, m.ap, ACT.Copy, e, ul_, scale=-1.0)
                m.done(wt)
            else:
                c = P.tt("pool", h4(KD), h4(KT[:, i, :]), cb(cols.ap[:, 4:8]), ALU.mult, kv, colt, ye)
                cols.done(c)
            yield
            sd = state.get(d)
            m = MP.get()
            for h in range(4):
                e = P.mm(hs(m.ap, h), hs(P_, h), hs(VB_, h), True, order == 0, w, vbt, m.free)
                if order == 1:
                    e = P.mm(hs(m.ap, h), hs(WT, h), hs(S[d], h), False, True, wt, sd)
            vn = P.act(VN, m.ap, ACT.Copy, e)
            m.done(vn)
            yield
            if order == 0:
                m, e = per_head(lambda h: hs(KD, h), lambda h: hs(VN, h), c, vn)
                state[d] = P.copy("dve", S[d], m.ap, e, kv)
                m.done(state[d])
            m = MP.get()
            for h in range(4):
                e = P.mm(hs(m.ap, h), hs(VN, h), hs(IT, h), True, order == 0, vn, it, m.free)
                if order == 1:
                    e = P.mm(hs(m.ap, h), hs(S[d], h), hs(gq, h), False, True, q, sd)
            yield
            if i not in first_o:
                first_o[i] = P.copy("dve", OS[:, :, ck], h4(m.ap), e)
            else:
                first_o[i] = P.tt("dve", OS[:, :, ck], OS[:, :, ck], h4(m.ap), ALU.add, e, first_o[i])
            m.done(first_o[i])

        beside(rounds([delta(o, d) for o in range(2) for d in range(2)], 4), ada.steps(FILL["gdn"] - 5))

        def finish(c):
            v = OS[:, 2 * c:2 * c + 2, :]
            s, m, r = TM.get(), MP.get(), TM.get()
            sq = P.act(s.ap, v, ACT.Square, s.free, first_o[0], first_o[1])
            mt = P.mm(m.ap, ones, s.ap, True, True, sq, m.free)
            e, f = rsqrt(r.ap, m.ap, 1.0 / 128, mt, r.free)
            m.done(f)
            yield
            x2 = s.ap.rearrange("p (a b) -> p a b", a=2)
            u = P.stt(x2, v, col("gdn_norm_w"), r.ap.rearrange("p (a b) -> p a b", a=2), ALU.mult, ALU.mult, e, mt)
            r.done(u)
            u = P.tt("dve", x2, x2, ZG[:, 2 * c:2 * c + 2, :], ALU.mult, u, zts)
            _, w = cut(UH[:, 2 * c:2 * c + 2, 0:256], UL[:, 2 * c:2 * c + 2, 0:256], x2, u, uq)
            s.done(w)

        run(finish(0), finish(1))


class Modulation:

    def __init__(self, P, W, MP, MOD, col, TM, sb, ident, cload, c1load, cut):
        self.P, self.W, self.MP, self.MOD, self.col, self.TM, self.ident = P, W, MP, MOD, col, TM, ident
        self.cs, self.cr, self.bank, self.count = sb("CSIL", [128, 8, 4]), sb("CSR", [128, 8, 4], F32R), None, 0
        self.summed, self.rows = [], []
        self.loads = [cload, c1load]
        zero = P.do("pool", lambda g: g.memset(self.cs[:, :, 2:4], 0.0))
        a = P.act(self.cs[:, :, 0:2], col("cc", 0, 16).rearrange("p (k v) -> p k v", k=8), ACT.Silu, cload)
        self.ready = [*cut(self.cr[:, :, 0:2], self.cr[:, :, 2:4], self.cs[:, :, 0:2], a), a, zero]

    def fill(self, most=1000):
        P, W = self.P, self.W
        while most and W.kind(W.u) in ("ada", "adr"):
            most -= 1
            at = W.units[W.u][2][0][0]
            l, m, k = int(at[0][3]), at[2] // 512, at[1]
            self.bank = self.bank or self.MP.get()
            o = self.bank.ap[0:4, :]
            for i in (k, k + 1):
                wh, wl, rdy, last = W.next((at[0], i, 512 * m, 512))
                if wl is None:
                    t = P.mm(o, self.cs[:, i, :], wh, i == 0, i == 7, rdy, self.ready, self.bank.free, sig=last)
                else:
                    P.mm(o, self.cr[:, i, :], wh, i == 0, False, rdy, self.ready, self.bank.free, sig=False)
                    t = P.mm(o, self.cr[:, i, :], wl, False, i == 7, sig=last)
            W.release(t)
            self.count += 1
            if k == 6:
                self.summed.append((l, m, self.bank, t))
                self.bank = None

    def advance(self):
        P = self.P
        if self.rows:
            l, m, s, a = self.rows.pop(0)
            b = self.MP.get()
            for j in range(4):
                t = P.tr(b.ap[:, 4 * j:4 * j + 4], s.ap[0:4, 128 * j:128 * j + 128], self.ident[0:4, 0:4], a, b.free,
                         self.loads)
            s.done(t)
            bias = self.col(f"b_ada{l}", 4 * m, 4).unsqueeze(2).broadcast_to([128, 4, 2])
            q = b.ap[:, 0:16].rearrange("p (j v) -> p j v", j=4)
            o = self.MOD[:, l, 4 * m:4 * m + 4, :]
            u = P.tt("dve", o, q[:, :, 0:2], bias, ALU.add, t, self.loads)
            self.done = P.tt("dve", o, o, q[:, :, 2:4], ALU.add, u)
            b.done(self.done)
        if self.summed:
            l, m, b, t = self.summed.pop(0)
            s = self.TM.get()
            a = P.act(s.ap[0:4, :], b.ap[0:4, :], ACT.Copy, t, s.free)
            b.done(a)
            self.rows.append((l, m, s, a))

    def finish(self, upto):
        while any((l, m) < upto for l, m, *_ in self.rows + self.summed):
            self.advance()

    def steps(self, n):
        for _ in range(n):
            while self.W.kind(self.W.u) not in ("ada", "adr"):
                yield
            self.advance()
            self.fill(1)
            yield


def block2(P, nc, stack, sb, W, gemm, pair, turn, ada, cut, rsqrt, every, col, TM, MP, GP, SM, RBR, SSR, X, UH, UL, uh, ul,
           consts2, ident, ones, MOD, Stat, ffn, ada_to_u, add_to_x, xt, out, fetch, first_of, first, xload2):
    old = every("pe", "act", "dve", "pool")
    DER = sb("DER", [128, 2, 6, 8, 2])

    def derive(l, i, name):
        ada.finish((l, 6 * (i + 1)))
        assert ada.count >= 72 * l + 24 * (i + 1)
        gv = col(f"{name}{l}", 0, 8).unsqueeze(2).broadcast_to([128, 8, 2])
        a = P.ts("dve", DER[:, l, i], MOD[:, l, 24 * i + 8:24 * i + 16, :], 1.0, None, ALU.add, None, ada.done)
        b = P.tt("dve", DER[:, l, i], DER[:, l, i], gv, ALU.mult, a)
        f = 1.0 if i == 1 else 0.5
        return [b, P.ts("dve", DER[:, l, 3 + i], MOD[:, l, 24 * i + 16:24 * i + 24, :], f, None, ALU.mult, None)]

    A = lambda l, i: (lambda k, s: DER[:, l, i, k, s:s + 1])
    B = lambda l, i: (lambda k, s: MOD[:, l, 24 * i + k, s:s + 1])
    gate = lambda l, i: (lambda k, s: DER[:, l, 3 + i, k, s:s + 1])

    stat = Stat(512)
    for k in range(8):
        stat.add(X[:, k, :], xt, xload2)
    for l in range(2):
        n = 512 if l == 0 else 256
        if l:
            first = fetch(first_of("f11"))
        made = derive(l, 0, "g_ffn1")
        r, rt = stat.rsqrt(D, between=FILL["f11"] if l else FILL["f10"] - FILL["f10"] // 2)
        ready = ada_to_u(r, rt, A(l, 0), B(l, 0), 512, every("pe"), made)
        stat, xt = ffn(f"f1{l}", 512, first, ready, gate(l, 0), f"c{l}")
        first = fetch([(f"win{l}", k, c, 128) for k in range(8) for c in (384, 0)])
        made = derive(l, 1, "g_mix")
        r, rt = stat.rsqrt(D, between=FILL[f"conv{l}"])
        ready = ada_to_u(r, rt, A(l, 1), B(l, 1), 512, every("pe"), made)
        mix2(P, nc, stack, sb, W, gemm, pair, turn, ada, cut, rsqrt, every, col, TM, MP, GP, SM, RBR, X, UH, UL, uh, ul,
             consts2, ident, ones, ready, l, n, Stat, add_to_x, gate, first)
        stat = mix2.stat
        first = fetch(first_of(f"f2{l}"))
        made = derive(l, 2, "g_ffn2")
        r, rt = stat.rsqrt(D, between=FILL[f"f2{l}"])
        ready = ada_to_u(r, rt, A(l, 2), B(l, 2), n, every("pe"), made)
        stat, xt = ffn(f"f2{l}", n, first, ready, gate(l, 2), f"d{l}")
    r, rt = stat.rsqrt(D)
    sq = every("act")
    for k in range(8):
        a = P.stt(X[:, k, 0:256], X[:, k, 0:256], col("g_final", k), r.ap[:, 0:256], ALU.mult, ALU.mult, rt, sq, xt)
        o = P.dma(out[:, 256 * k:256 * k + 256], X[:, k, 0:256], "out", a)
    P.wait("sp", [o])


def mix2(P, nc, stack, sb, W, gemm, pair, turn, ada, cut, rsqrt, every, col, TM, MP, GP, SM, RBR, X, UH, UL, uh, ul,
         consts2, ident, ones, ready, l, n, Stat, add_to_x, gate, first):
    ns = n // 256
    L = str(l)
    with ExitStack() as st:
        def tile(name, shape, dt=F32, s=None):
            return sb(name + L, shape, dt, s or st)

        old = every("pe", "act", "dve", "pool")
        CVH, CVL = tile("CVH", [128, 3, n], F32R), tile("CVL", [128, 3, n], F32R)
        ATH, ATL = tile("ATH", [128, 4, n], F32R), tile("ATL", [128, 4, n], F32R)
        win = lambda c: [(f"win{l}", k, c, 128) for k in range(8)]
        if l:
            FOH, FOL = tile("FOH", [128, 4, n], F32R), tile("FOL", [128, 4, n], F32R)

        def fourier_setup(s4):
            fold = every("pe", "act", "dve", "pool")
            K3 = tile("K3", [128, 1280], F32, s4)
            k3 = P.dma(K3[:], consts2[:, 640:1920], "k3" + L, fold, e="pool")
            AF = tile("AF", [128, 4, 2, 256], F32, s4)
            return K3, k3, Ring([AF[:, i] for i in range(4)]), fold

        def fourier(j, K3, k3, AR, fold):
            CS = K3[:, 0:256]
            CT = K3[:, 256:768].rearrange("p (i t) -> p i t", i=2)
            ST = K3[:, 768:1280].rearrange("p (i t) -> p i t", i=2)
            yield from turn((f"win{l}", 0, 1440 + 128 * j, 128))
            yield from MP.room(2)
            yield from TM.room()
            g, ps, t = gemm(win(1440 + 128 * j), uh(n), ul(n), 128, n)
            z = TM.get()
            zt = P.act(z.ap[:, 0:n], ps, ACT.Copy, t, z.free)
            g.done(zt)
            yield
            yield from MP.room(ns)
            half = []
            for s in range(ns):
                m, a = MP.get(), AR.get()
                for i in range(2):
                    c = 256 * s + 128 * i
                    e = P.mm(m.ap[:, 256 * i:256 * i + 256], z.ap[:, c:c + 128], CS, True, True, zt, k3, m.free)
                at = P.copy("dve", a.ap, m.ap.rearrange("p (i c) -> p i c", i=2), e, a.free, fold)
                m.done(at)
                half.append((a, at))
            z.done(e)
            yield
            yield from MP.room()
            fm = MP.get()
            for s, (a, at) in enumerate(half):
                o = fm.ap[:, 256 * s:256 * s + 256]
                for i in range(2):
                    P.mm(o, a.ap[:, i, 0:128], CT[:, i, :], i == 0, False, at, fm.free)
                    e2 = P.mm(o, a.ap[:, i, 128:256], ST[:, i, :], False, i == 1)
                a.done(e2)
            _, ft = cut(FOH[:, j, :], FOL[:, j, :], fm.ap[:, 0:n], e2, fold)
            fm.done(ft)

        with ExitStack() as s3:
            K2 = tile("K2", [128, 640], F32, s3)
            k2 = P.dma(K2[:], consts2[:, 0:640], "k2" + L, old, e="pool")
            ROT, COS, SIN = K2[0:96, 0:96], K2[0:96, 128:384], K2[0:96, 384:640]
            VC = tile("VC", [128, 3, ns, 286], F32, s3)
            AC = tile("AC", [128, 3, ns, 256], F32, s3)
            CQH, CQL = tile("CQH", [128, 3, n], F32R, s3), tile("CQL", [128, 3, n], F32R, s3)
            CKH, CKL = tile("CKH", [128, 2, 512], F32R, s3), tile("CKL", [128, 2, 512], F32R, s3)
            KR = tile("KR", [96, 512], F32, s3)
            V = tile("V", [128, 4, 512], F32, s3)
            QK = tile("QK", [96, 6, 512], F32, s3)
            QR, KRG = Ring([QK[:, i] for i in range(3)]), Ring([QK[:, i] for i in range(3, 6)])
            PTT = tile("PTT", [128, 2, 4, 256], F32, s3)
            PTR = Ring([PTT[:, 0], PTT[:, 1]])
            pads = [P.do("pool", lambda g: g.memset(VC[:, :, :, 0:15], 0.0), old),
                    P.do("pool", lambda g: g.memset(VC[:, :, :, 271:286], 0.0))]
            sv = lambda ap: ap.rearrange("p (s t) -> p s t", s=ns)
            fl = lambda ap: ap.rearrange("p s t -> p (s t)")
            acc = []

            first = pair(first, n, ready)
            for c in range(3):
                g, ps, t = gemm(win(384 + 128 * c), uh(n), ul(n), 128, n) if c else first[0]
                s = TM.get()
                a = P.act(s.ap[:, 0:n], ps, ACT.Sigmoid, t, s.free)
                g.done(a)
                g, ps, t = gemm(win(128 * c), uh(n), ul(n), 128, n) if c else first[1]
                b = P.tt("dve", VC[:, c, :, 15:271], sv(s.ap[:, 0:n]), sv(ps), ALU.mult, a, t, old)
                g.done(b)
                s.done(b)
                acc.append(P.ts("dve", AC[:, c], VC[:, c, :, 0:256], col(f"w_dw{l}", 31 * c), col(f"b_dw{l}", c),
                                ALU.mult, ALU.add, b, pads))

            def taps_():
                for i in range(1, 31):
                    for c in range(3):
                        acc[c] = P.stt(AC[:, c], VC[:, c, :, i:i + 256], col(f"w_dw{l}", 31 * c + i), AC[:, c],
                                       ALU.mult, ALU.add, acc[c])
                        if (3 * i + c) % TAPS[l] == 0:
                            yield
                yield from TM.room(2)
                yield from MP.room(2)
                s, m = TM.get(), MP.get()
                a = P.tt("dve", s.ap[:, 0:n], fl(AC[:, 0]), fl(AC[:, 1]), ALU.add, acc, s.free)
                a = P.tt("dve", s.ap[:, 0:n], s.ap[:, 0:n], fl(AC[:, 2]), ALU.add, a)
                yield
                e = P.mm(m.ap[:, 0:n], ones, s.ap[:, 0:n], True, True, a, m.free)
                s.done(e)
                yield from TM.room(2)
                stat = Stat(n)
                for c in range(3):
                    acc[c] = P.stt(fl(AC[:, c]), m.ap[:, 0:n], -1.0 / 384, fl(AC[:, c]), ALU.mult, ALU.add, e)
                    stat.add(fl(AC[:, c]), acc[c])
                m.done(acc[2])
                sq = every("act")
                yield
                r, rt = stat.rsqrt(384, TM)
                yield
                for c in range(3):
                    a = P.stt(fl(AC[:, c]), fl(AC[:, c]), col(f"ln_g{l}", c), r.ap[:, 0:n], ALU.mult, ALU.mult, rt,
                              sq, acc[c])
                    b = P.act(fl(AC[:, c]), fl(AC[:, c]), ACT.Silu, a, bias=col(f"ln_b{l}", c))
                    cut(CVH[:, c, :], CVL[:, c, :], fl(AC[:, c]), b, old)
                r.done(a)

            def latent(nt, base, gname, hi, lo, nn, got):
                stat, toks = Stat(nn), []
                for j in range(nt):
                    g, ps, t = gemm(win(base + 128 * j), uh(nn), ul(nn), 128, nn)
                    sq = stat.add(ps, t)
                    gc = col(f"{gname}{l}", j)
                    a = P.act(hi[:, j, :], ps, ACT.Copy, old, t, scale=gc)
                    b = P.stt(lo[:, j, :], ps, gc, hi[:, j, :].bitcast(F32), ALU.mult, ALU.subtract, a)
                    g.done(sq, b)
                    toks.append(b)
                    yield
                got.extend(stat.rsqrt(128 * nt) + (toks,))

            def rope(q, tok):
                m, s = MP.get(), TM.get()
                e = P.mm(m.ap[0:96, 0:256], ROT, q[:, 0:256], True, True, tok, m.free, k2)
                a = P.tt("dve", s.ap[0:96, 0:256], m.ap[0:96, 0:256], SIN, ALU.mult, e, s.free, k2)
                m.done(a)
                b = P.tt("dve", q[:, 0:256], q[:, 0:256], COS, ALU.mult, e)
                c = P.tt("dve", q[:, 0:256], q[:, 0:256], s.ap[0:96, 0:256], ALU.add, a, b)
                s.done(c)
                return c

            SC = 96 ** -0.5

            def attention():
                gq, gk = [], []
                yield from latent(3, 768, "g_q", CQH, CQL, n, gq)
                yield from latent(2, 1152, "g_kv", CKH, CKL, 512, gk)
                (rq, rqt, cqt), (rk, rkt, ckt) = gq, gk
                g, ps, t = gemm([(f"wkr{l}", k, 0, 96) for k in range(8)], uh(512), ul(512), 96, 512)
                a = P.copy("dve", KR[:], ps, t, old)
                g.done(a)
                m, sm = MP.get(), SM.get()
                for i in range(4):
                    e = P.tr(m.ap[:, 128 * i:128 * i + 128], rk.ap[:, 128 * i:128 * i + 128], ident, rkt, m.free)
                rc = P.copy("dve", sm.ap[:, 0:4], m.ap.rearrange("p (i c) -> p i c", i=4)[:, :, 0:1].rearrange(
                    "p i c -> p (i c)"), e, sm.free)
                m.done(rc)
                yield
                ada.fill()
                pc = [W.next((f"wv{l}", k, 0, 512)) for k in range(2)]
                vt = []
                for i in range(4):
                    g = GP.get()
                    x = slice(128 * i, 128 * i + 128)
                    for k in range(2):
                        wh, wl, rdy, _ = pc[k]
                        P.mm(g.ap, CKH[:, k, x], wh, k == 0, False, rdy, ckt, g.free, sig=False)
                        P.mm(g.ap, CKH[:, k, x], wl, False, False, sig=False)
                        t = P.mm(g.ap, CKL[:, k, x], wh, False, k == 1)
                    vt.append(P.act(V[:, i, :], g.ap, ACT.Copy, t, rc, old, scale=sm.ap[:, i:i + 1]))
                    g.done(vt[-1])
                W.release(t)
                sm.done(vt[-1])
                kr = rope(KR, a)
                yield
                out = {}

                prepared, todo = {}, {}

                def prep(h):
                    yield from QR.room()
                    yield from KRG.room()
                    q, kk = QR.get(), KRG.get()
                    yield from turn((f"wuq{l}", 0, 96 * h, 96))
                    yield from MP.room(3)
                    g, ps, t = gemm([(f"wuq{l}", k, 96 * h, 96) for k in range(3)], lambda k: CQH[:, k, :],
                                    lambda k: CQL[:, k, :], 96, n, cqt)
                    a = P.tt("dve", q.ap[:, 0:n], ps, rq.ap[0:96, 0:n], ALU.mult, t, rqt, q.free, old)
                    g.done(a)
                    g, ps, t = gemm([(f"wkn{l}", k, 96 * h, 96) for k in range(2)], lambda k: CKH[:, k, :],
                                    lambda k: CKL[:, k, :], 96, 512, ckt)
                    ka = P.tt("dve", kk.ap[0:64, :], ps[0:64, :], rk.ap[0:64, :], ALU.mult, t, rkt, kk.free, old)
                    g.done(ka)
                    kt = krt.setdefault(h % 3, None) or P.copy("dve", kk.ap[64:96, :], KR[64:96, :], kk.free, kr, old)
                    krt[h % 3] = kt
                    yield
                    yield from MP.room(2)
                    yield from TM.room()
                    qt = rope(q.ap, a)
                    todo[h] = ns
                    prepared[h] = (q, kk, [qt, ka, kt])

                def soft(h, s):
                    c, b0 = h // 2, 64 * (h % 2)
                    while h not in prepared:
                        yield
                    q, kk, made = prepared[h]
                    k0, nk = (0, 512) if s == 0 else (256, 256)
                    yield from MP.room(3)
                    yield from TM.room(3)
                    yield from SM.room(2)
                    work = []
                    for i in range(2):
                        m, sm, p = MP.get(), SM.get(), TM.get()
                        qs = 256 * s + 128 * i
                        e = P.mm(m.ap[:, 0:nk], q.ap[:, qs:qs + 128], kk.ap[:, k0:k0 + nk], True, True, made, m.free)
                        mx = P.rmax(sm.ap[:, 0:1], m.ap[:, 0:nk], e, sm.free)
                        mx = P.ts("dve", sm.ap[:, 1:2], sm.ap[:, 0:1], -SC, None, ALU.mult, None, mx)
                        ex = P.act(p.ap[:, 0:nk], m.ap[:, 0:nk], ACT.Exp, mx, p.free, scale=SC,
                                   bias=sm.ap[:, 1:2], accum_out=sm.ap[:, 2:3])
                        m.done(ex)
                        work.append((sm, p, ex))
                    todo[h] -= 1
                    if not todo[h]:
                        q.done(e)
                        kk.done(e)
                    yield
                    for i, (sm, p, ex) in enumerate(work):
                        rcp = P.recip(sm.ap[:, 3:4], sm.ap[:, 2:3], ex)
                        nm = P.ts("dve", p.ap[:, 0:nk], p.ap[:, 0:nk], sm.ap[:, 3:4], None, ALU.mult, None, rcp)
                        sm.done(nm)
                        work[i] = (p, nm)
                    yield
                    yield from PTR.room()
                    yield from MP.room(2)
                    pt = PTR.get()
                    for i, (p, nm) in enumerate(work):
                        m = MP.get()
                        for kc in range(nk // 128):
                            e = P.tr(m.ap[:, 128 * kc:128 * kc + 128], p.ap[:, 128 * kc:128 * kc + 128], ident, nm,
                                     m.free, sig=kc == nk // 128 - 1)
                        p.done(e)
                        ev = P.act(pt.ap[:, 0:nk // 128, 128 * i:128 * i + 128],
                                   m.ap[:, 0:nk].rearrange("p (a b) -> p a b", b=128), ACT.Copy, e, pt.free, old)
                        m.done(ev)
                    yield
                    if c not in out:
                        yield from MP.room()
                    if c not in out:
                        out[c] = MP.get()
                        left[c] = 2 * ns
                    o = out[c]
                    for kc in range(nk // 128):
                        e = P.mm(o.ap[b0:b0 + 64, 256 * s:256 * s + 256], V[:, k0 // 128 + kc, 64 * h:64 * h + 64],
                                 pt.ap[:, kc, :], kc == 0, kc == nk // 128 - 1, ev, vt, o.free)
                    pt.done(e)
                    left[c] -= 1
                    if not left[c]:
                        yield
                        _, u = cut(ATH[:, c, :], ATL[:, c, :], o.ap[:, 0:n], e, old)
                        o.done(u)

                left, krt = {}, {}
                tasks = []
                for h in range(8):
                    tasks.append(prep(h))
                    tasks += [soft(h, s) for s in range(ns)]
                yield from rounds(tasks, WIDTH)
                rq.done(*every("dve"))
                rk.done(*every("dve"))

            if l:
                fb = fourier_setup(s3)
                beside(attention(), taps_(), rounds([fourier(j, *fb) for j in range(4)], 1))
            else:
                beside(attention(), taps_())
        if not l:
            FOH, FOL = tile("FOH", [128, 4, n], F32R), tile("FOL", [128, 4, n], F32R)
            with ExitStack() as s4:
                fb = fourier_setup(s4)
                run(*[fourier(j, *fb) for j in range(4)], width=2)
        adone = every("pe", "act", "dve", "pool")
        YH, YL = tile("YH", [128, 8, n], F32R), tile("YL", [128, 8, n], F32R)
        yt = []
        for m in range(8):
            sig = []
            for b in range(3):
                g, ps, t = gemm([(f"wbg{l}", k, 1024 * b + 128 * m, 128) for k in range(8)], uh(n), ul(n), 128, n)
                s = TM.get()
                a = P.act(s.ap[:, 0:n], ps, ACT.Sigmoid, t, s.free, bias=col(f"b_bg{l}", 8 * b + m))
                g.done(a)
                sig.append((s, a))
            v = [s.ap[:, 0:n] for s, _ in sig]
            g, ps, t = gemm([(f"wpw{l}", k, 128 * m, 128) for k in range(3)], lambda k: CVH[:, k, :],
                            lambda k: CVL[:, k, :], 128, n, adone)
            a0 = P.stt(v[0], ps, col(f"b_pw{l}", m), v[0], ALU.add, ALU.mult, t, sig[0][1])
            g.done(a0)
            g, ps, t = gemm([(f"wo{l}", k, 128 * m, 128) for k in range(4)], lambda k: ATH[:, k, :],
                            lambda k: ATL[:, k, :], 128, n)
            a1 = P.tt("dve", v[1], ps, v[1], ALU.mult, t, sig[1][1])
            g.done(a1)
            g, ps, t = gemm([(f"wf{l}", k, 128 * m, 128) for k in range(4)], lambda k: FOH[:, k, :],
                            lambda k: FOL[:, k, :], 128, n)
            a2 = P.stt(v[2], ps, col(f"b_f{l}", m), v[2], ALU.add, ALU.mult, t, sig[2][1])
            g.done(a2)
            a0 = P.tt("dve", v[0], v[0], v[1], ALU.add, a0, a1)
            a0 = P.tt("dve", v[0], v[0], v[2], ALU.add, a0, a2)
            _, u = cut(YH[:, m, :], YL[:, m, :], v[0], a0, adone)
            for s, _ in sig:
                s.done(u)
            yt.append(u)
        stat = Stat(n)
        for m in range(8):
            g, ps, t = gemm([(f"wout{l}", k, 128 * m, 128) for k in range(8)], lambda k: YH[:, k, :],
                            lambda k: YL[:, k, :], 128, n, each=yt)
            a = add_to_x(m, ps, n, gate(l, 1), t)
            g.done(a)
            stat.add(X[:, m, 0:n], a)
        mix2.stat = stat


def host_arrays(inputs):
    a = {k: np.asarray(v, dtype=np.asarray(v).dtype) for k, v in inputs.items()}
    wt = {"f1g": a["ffn1_w_gate"][0], "f1u": a["ffn1_w_up"][0], "f1d": a["ffn1_w_down"][0],
          "f2g": a["ffn2_w_gate"][0], "f2u": a["ffn2_w_up"][0], "f2d": a["ffn2_w_down"][0],
          "win": a["w_in"][0], "wout": a["w_out"][0]}
    for l in range(2):
        for f in (1, 2):
            wt[f"f{f}{l}g"], wt[f"f{f}{l}u"], wt[f"f{f}{l}d"] = (
                a[f"w1_ffn{f}_2"][l], a[f"w3_ffn{f}_2"][l], a[f"w2_ffn{f}_2"][l])
        wt[f"ada{l}"] = wt[f"adr{l}"] = a["w_ada_2"][l]
        wt[f"win{l}"], wt[f"wpw{l}"] = a["w_in_2"][l], a["w_pw_conv_2"][l]
        wt[f"wuq{l}"], wt[f"wo{l}"], wt[f"wf{l}"] = a["w_uq_2"][l], a["w_o_mla_2"][l], a["w_fourier_2"][l]
        wt[f"wbg{l}"], wt[f"wout{l}"] = a["w_bgate_2"][l], a["w_out_2"][l]
        wt[f"wkr{l}"] = np.concatenate([np.zeros((1024, 64), np.float32), a["w_in_2"][l][:, 1408:1440]], axis=1)
        kv = a["w_ukv_2"][l].reshape(256, 8, 128)
        wt[f"wkn{l}"] = np.concatenate([kv[:, :, :64], np.zeros((256, 8, 32), np.float32)], axis=2).reshape(256, 768)
        wt[f"wv{l}"] = kv[:, :, 64:].reshape(256, 512)
    units, total = plan()
    stream = np.empty(total, np.float32)
    for at, n, ps in units:
        u = stream[at:at + 128 * n].reshape(128, n)
        for (name, k, m0, m), c in ps:
            u[:, c:c + m] = wt[name][128 * k:128 * k + 128, m0:m0 + m]

    def fm(v):
        v = np.asarray(v)
        return v.reshape(-1, 128).T

    c1 = {"ffn1_norm": fm(a["ffn1_norm"][0]), "mix_norm": fm(a["mix_norm"][0]), "ffn2_norm": fm(a["ffn2_norm"][0]),
          "final_norm": fm(a["final_norm"][0]),
          "conv_w": a["conv_w"][0].reshape(12, 128, 5).transpose(1, 0, 2).reshape(128, 60),
          "gdn_norm_w": fm(a["gdn_norm_w"][0]), "q_norm_w": np.tile(a["q_norm_w"][0], 2)[:, None],
          "k_norm_w": np.tile(a["k_norm_w"][0], 2)[:, None],
          "dt_bias": np.broadcast_to(a["dt_bias"][0].reshape(1, 8), (128, 8)),
          "a_log": np.broadcast_to(a["a_log"][0].reshape(1, 8), (128, 8)),
          "g_final": fm(a["g_final_2"]),
          "cc": np.stack([fm(a["c_2"][0]), fm(a["c_ctx_2"])], axis=2).reshape(128, 16)}
    for l in range(2):
        for name, src in (("b_ada", "b_ada_2"), ("g_ffn1", "g_ffn1_2"), ("g_mix", "g_mix_2"), ("g_ffn2", "g_ffn2_2"),
                          ("b_dw", "b_dw_2"), ("ln_g", "ln_g_conv_2"), ("ln_b", "ln_b_conv_2"), ("b_pw", "b_pw_conv_2"),
                          ("g_q", "g_qnorm_2"), ("g_kv", "g_kvnorm_2"), ("b_f", "b_fourier_2"), ("b_bg", "b_bgate_2")):
            c1[f"{name}{l}"] = fm(a[src][l])
        c1[f"w_dw{l}"] = a["w_dw_2"][l].T.reshape(3, 128, 31).transpose(1, 0, 2).reshape(128, 93)
    COL, ncol = columns()
    cols = np.empty((128, ncol), np.float32)
    for name, (at, n) in COL.items():
        cols[:, at:at + n] = c1[name]
    strip = a["rel_bias"][t5_buckets()]
    idx = np.clip(np.arange(384)[None, :] - 128 - np.arange(128)[:, None], -255, 255) + 255
    bias = np.ascontiguousarray(strip[idx].transpose(0, 2, 1))
    xt = a["x"][0].T.reshape(8, 128, 256).transpose(1, 0, 2)
    ct = a["ctx_2"][0].T.reshape(8, 128, 256).transpose(1, 0, 2)
    xin = np.ascontiguousarray(np.concatenate([xt, ct], axis=2).reshape(128, 4096))
    return {"in_w": stream, "in_cols": cols, "in_bias": bias, "in_x": xin,
            "in_consts": np.concatenate(list(const_blocks().values()), axis=1),
            "in_consts2": np.concatenate(list(const_blocks2().values()), axis=1)}


def kernel(**inputs):
    import concourse.bacc as bacc
    from concourse.bass_utils import run_bass_kernel_spmd

    arrays = host_arrays(inputs)
    nc = bacc.Bacc("TRN2", target_bir_lowering=False, num_devices=1)
    ap = {n: nc.dram_tensor(n, v.shape, F32, kind="ExternalInput").ap() for n, v in arrays.items()}
    out = nc.dram_tensor("out_x", (128, 2048), F32, kind="ExternalOutput").ap()
    build(nc, ap["in_w"], ap["in_cols"], ap["in_consts"], ap["in_consts2"], ap["in_bias"], ap["in_x"], out)
    r = run_bass_kernel_spmd(nc, [arrays], core_ids=[0])
    y = r.results[0]["out_x"].reshape(128, 8, 256).transpose(2, 1, 0).reshape(1, 256, 1024)
    return np.ascontiguousarray(y)
```
